# Optimizing a Trainium2 kernel written in Bass

```python
import jax, jax.numpy as jnp
from jax import lax
import numpy as np

D_MODEL = 1024
BATCH = 1
SEQ = 512
DEPTH = 1

GRID_W = 64
CTX_LEN = 256
D_MIX = D_MODEL
RET_DIM = 64
RET_WIDTH = D_MIX // 2
RET_HEADS = RET_WIDTH // RET_DIM
RWKV_DIM = 64
RWKV_WIDTH = D_MIX - RET_WIDTH
RWKV_HEADS = RWKV_WIDTH // RWKV_DIM
DECAY_LORA = 64
ICLR_LORA = 64
GATE_LORA = 128
CHUNK = 128
CONV_W = 3
N_EXPERTS = 16
EC_CAPACITY = 2
D_EXPERT = D_MODEL
ROPE_BASE = 10000.0
NORM_EPS = 1e-6
RWKV_GN_EPS = 64e-5
RET_COLS = 5 * RET_WIDTH
RWKV_SPLITS = (RWKV_WIDTH, RWKV_WIDTH, RWKV_WIDTH, DECAY_LORA, DECAY_LORA, ICLR_LORA, GATE_LORA, GATE_LORA)
RWKV_COLS = sum(RWKV_SPLITS)
D_IN = RET_COLS + RWKV_COLS


def split_cols(u, sizes):
    outs, start = [], 0
    for s in sizes:
        outs.append(u[..., start:start + s])
        start += s
    return outs

def flip(t):
    return jnp.flip(t, axis=1)

def rms_norm(x, g):
    xf = x.astype(jnp.float32)
    y = xf * lax.rsqrt(jnp.mean(xf * xf, axis=-1, keepdims=True) + NORM_EPS)
    return (y * g.astype(jnp.float32)).astype(x.dtype)

def head_rms(y):
    y = y * lax.rsqrt(jnp.mean(y * y, axis=-1, keepdims=True) + NORM_EPS)
    return y.reshape(y.shape[0], y.shape[1], -1)

def depthwise_conv(x, w):
    return lax.conv_general_dilated(x, w[:, None, :].astype(x.dtype), window_strides=(1,), padding='SAME',
                                    dimension_numbers=('NWC', 'WIO', 'NWC'), feature_group_count=x.shape[-1])

def axial_rope(x):
    n_tok, d = x.shape[1], x.shape[-1]
    rows = n_tok // GRID_W
    row = jnp.repeat(jnp.arange(rows, dtype=jnp.float32), GRID_W)
    col = jnp.tile(jnp.arange(GRID_W, dtype=jnp.float32), rows)
    n_freq = d // 4
    freq = ROPE_BASE ** (-jnp.arange(n_freq, dtype=jnp.float32) / n_freq)
    ang = jnp.concatenate([row[:, None] * freq, col[:, None] * freq], axis=-1)[None, :, None, :]
    cos, sin = jnp.cos(ang), jnp.sin(ang)
    x1, x2 = x[..., : d // 2], x[..., d // 2:]
    return jnp.concatenate([x1 * cos - x2 * sin, x2 * cos + x1 * sin], axis=-1)

def retention_scan(q, k, v, log_gamma, s0):
    B, T, H, d = q.shape
    n = T // CHUNK
    to_chunks = lambda t: t.reshape(B, n, CHUNK, H, d).transpose(1, 0, 3, 2, 4)
    idx = jnp.arange(CHUNK, dtype=jnp.float32)
    rel = idx[:, None] - idx[None, :]
    decay_in = jnp.where(rel >= 0, jnp.exp(jnp.maximum(rel, 0.0) * log_gamma[:, None, None]), 0.0)
    q_dec = jnp.exp((idx + 1.0) * log_gamma[:, None])[..., None]
    k_dec = jnp.exp((CHUNK - 1.0 - idx) * log_gamma[:, None])[..., None]
    chunk_dec = jnp.exp(CHUNK * log_gamma)[:, None, None]

    def step(S, inp):
        qc, kc, vc = inp
        scores = jnp.einsum('bhid,bhjd->bhij', qc, kc) * decay_in
        out = jnp.einsum('bhij,bhjd->bhid', scores, vc) + jnp.einsum('bhid,bhde->bhie', qc * q_dec, S)
        S = S * chunk_dec + jnp.einsum('bhjd,bhje->bhde', kc * k_dec, vc)
        return S, out

    S_fin, ys = lax.scan(step, s0, (to_chunks(q), to_chunks(k), to_chunks(v)))
    return ys.transpose(1, 0, 3, 2, 4).reshape(B, T, H, d), S_fin

def retention_group(u, uc, need_ctx):
    def split_heads(t):
        q, k, v, gf, gb = split_cols(t.astype(jnp.float32), (RET_WIDTH,) * 5)
        hd = lambda a: a.reshape(a.shape[0], a.shape[1], RET_HEADS, RET_DIM)
        return hd(q), hd(k) * RET_DIM ** -0.5, hd(v), gf, gb

    q, k, v, gf, gb = split_heads(u)
    qc, kc, vc, gfc, gbc = split_heads(uc)
    q, k = axial_rope(q), axial_rope(k)
    log_gamma = jnp.log1p(-jnp.exp2(-5.0 - jnp.arange(RET_HEADS, dtype=jnp.float32)))
    s0 = jnp.zeros((u.shape[0], RET_HEADS, RET_DIM, RET_DIM), jnp.float32)
    yc_f, sc_f = retention_scan(qc, kc, vc, log_gamma, s0)
    yc_b, sc_b = retention_scan(flip(qc), flip(kc), flip(vc), log_gamma, s0)
    y_f, _ = retention_scan(q, k, v, log_gamma, sc_f)
    y_b, _ = retention_scan(flip(q), flip(k), flip(v), log_gamma, sc_b)
    lat = jax.nn.silu(gf) * head_rms(y_f) + jax.nn.silu(gb) * head_rms(flip(y_b))
    if not need_ctx:
        return lat, None
    ctx_out = jax.nn.silu(gfc) * head_rms(yc_f) + jax.nn.silu(gbc) * head_rms(flip(yc_b))
    return lat, ctx_out

def rwkv_prepare(u, w0, w2, a0, a2, g2, k_k, k_a, r_k):
    u = u.astype(jnp.float32)
    B, T, _ = u.shape
    r, k, v, wl_f, wl_b, al, gl_f, gl_b = split_cols(u, RWKV_SPLITS)
    heads = lambda t: t.reshape(B, T, RWKV_HEADS, RWKV_DIM)

    def decay(wl, w0_d, w2_d):
        w_log = -jax.nn.softplus(-(w0_d + jnp.tanh(wl) @ w2_d)) - 0.5
        return heads(jnp.exp(-jnp.exp(w_log)))

    iclr = jax.nn.sigmoid(a0 + al @ a2)
    kk = heads(k * k_k)
    kk = kk / jnp.maximum(jnp.linalg.norm(kk, axis=-1, keepdims=True), 1e-12)
    k_mod = heads(k * (1.0 + (iclr - 1.0) * k_a))
    r, v = heads(r), heads(v)
    bonus = (jnp.sum(r * k_mod * r_k.reshape(RWKV_HEADS, RWKV_DIM), axis=-1, keepdims=True) * v).reshape(B, T, -1)
    g_f = jax.nn.sigmoid(gl_f) @ g2[0]
    g_b = jax.nn.sigmoid(gl_b) @ g2[1]
    return (r, decay(wl_f, w0[0], w2[0]), decay(wl_b, w0[1], w2[1]), k_mod, v, -kk, kk * heads(iclr), g_f, g_b, bonus)

def rwkv7_scan(r, w, k, v, a, b, s0):
    def step(S, inp):
        r_t, w_t, k_t, v_t, a_t, b_t = inp
        sa = jnp.einsum('bhvk,bhk->bhv', S, a_t)
        S = S * w_t[:, :, None, :] + sa[..., None] * b_t[:, :, None, :] + v_t[..., None] * k_t[:, :, None, :]
        return S, jnp.einsum('bhvk,bhk->bhv', S, r_t)

    xs = tuple(jnp.moveaxis(t, 1, 0) for t in (r, w, k, v, a, b))
    S_fin, ys = lax.scan(step, s0, xs)
    return jnp.moveaxis(ys, 0, 1), S_fin

def rwkv_group_norm(y, w, b):
    mu = jnp.mean(y, axis=-1, keepdims=True)
    var = jnp.mean((y - mu) ** 2, axis=-1, keepdims=True)
    yn = ((y - mu) * lax.rsqrt(var + RWKV_GN_EPS)).reshape(y.shape[0], y.shape[1], -1)
    return yn * w + b

def rwkv_group(rw, rwc, w0, w2, a0, a2, g2, k_k, k_a, r_k, lnx_w, lnx_b, need_ctx):
    r, w_f, w_b, k, v, a, b, g_f, g_b, bonus = rwkv_prepare(rw, w0, w2, a0, a2, g2, k_k, k_a, r_k)
    rc, wc_f, wc_b, kc, vc, ac, bc, gc_f, gc_b, bonus_c = rwkv_prepare(rwc, w0, w2, a0, a2, g2, k_k, k_a, r_k)
    s0 = jnp.zeros((rw.shape[0], RWKV_HEADS, RWKV_DIM, RWKV_DIM), jnp.float32)
    yc_f, sc_f = rwkv7_scan(rc, wc_f, kc, vc, ac, bc, s0)
    yc_b, sc_b = rwkv7_scan(*[flip(t) for t in (rc, wc_b, kc, vc, ac, bc)], s0)
    y_f, _ = rwkv7_scan(r, w_f, k, v, a, b, sc_f)
    y_b, _ = rwkv7_scan(*[flip(t) for t in (r, w_b, k, v, a, b)], sc_b)
    lat = g_f * (rwkv_group_norm(y_f, lnx_w, lnx_b) + bonus) + g_b * (rwkv_group_norm(flip(y_b), lnx_w, lnx_b) + bonus)
    if not need_ctx:
        return lat, None
    ctx_out = (gc_f * (rwkv_group_norm(yc_f, lnx_w, lnx_b) + bonus_c)
               + gc_b * (rwkv_group_norm(flip(yc_b), lnx_w, lnx_b) + bonus_c))
    return lat, ctx_out

def token_mix(h, hc, w_in, conv_w, w0, w2, a0, a2, g2, k_k, k_a, r_k, lnx_w, lnx_b, w_out, need_ctx):
    u, uc = h @ w_in, hc @ w_in
    ret_lat, ret_ctx = retention_group(u[..., :RET_COLS], uc[..., :RET_COLS], need_ctx)
    rw = depthwise_conv(u[..., RET_COLS:], conv_w)
    rwc = depthwise_conv(uc[..., RET_COLS:], conv_w)
    rwkv_lat, rwkv_ctx = rwkv_group(rw, rwc, w0, w2, a0, a2, g2, k_k, k_a, r_k, lnx_w, lnx_b, need_ctx)
    lat = jnp.concatenate([ret_lat, rwkv_lat], axis=-1).astype(h.dtype) @ w_out
    if not need_ctx:
        return lat, None
    ctx_out = jnp.concatenate([ret_ctx, rwkv_ctx], axis=-1).astype(hc.dtype) @ w_out
    return lat, ctx_out

def ec_moe(h, w_router, w_gate, w_up, w_down):
    B, T, D = h.shape
    cap = max(1, EC_CAPACITY * T // N_EXPERTS)
    affinity = jax.nn.softmax((h @ w_router).astype(jnp.float32), axis=-1)
    gate_vals, tok_idx = lax.top_k(jnp.swapaxes(affinity, 1, 2), cap)
    xs = jax.vmap(lambda hb, ib: hb[ib])(h, tok_idx)
    hid = jax.nn.silu(jnp.einsum('becd,edf->becf', xs, w_gate)) * jnp.einsum('becd,edf->becf', xs, w_up)
    ye = jnp.einsum('becf,efd->becd', hid, w_down) * gate_vals[..., None].astype(h.dtype)
    return jax.vmap(lambda yb, ib: jnp.zeros((T, D), yb.dtype).at[ib.reshape(-1)].add(yb.reshape(-1, D)))(ye, tok_idx)

def first_inputs(seed: int = 0) -> dict:
    key = jax.random.key(seed)
    ks = jax.random.split(key, 24)
    nrm = lambda k, shape, s: s * jax.random.normal(k, shape, jnp.float32)
    L, D, W, E, F = DEPTH, D_MODEL, RWKV_WIDTH, N_EXPERTS, D_EXPERT
    return {
        'x': nrm(ks[0], (BATCH, SEQ, D), 1.0),
        'c': nrm(ks[1], (BATCH, D), 1.0),
        'ctx': nrm(ks[2], (BATCH, CTX_LEN, D), 1.0),
        'c_ctx': nrm(ks[3], (D,), 1.0),
        'w_mod': nrm(ks[4], (L, D, 6 * D), 0.5 * D ** -0.5),
        'b_mod': nrm(ks[5], (L, 6 * D), 0.02),
        'norm_gains': 1.0 + nrm(ks[6], (L, 4, D), 0.1),
        'w_in': nrm(ks[7], (L, D, D_IN), D ** -0.5),
        'rwkv_conv': jnp.array([0.3, 1.0, 0.3], jnp.float32)[None, :, None] + nrm(ks[8], (L, CONV_W, RWKV_COLS), 0.05),
        'rwkv_w0': jnp.linspace(-6.0, -1.0, W, dtype=jnp.float32) + nrm(ks[9], (L, 2, W), 0.1),
        'rwkv_w2': nrm(ks[10], (L, 2, DECAY_LORA, W), 0.5 * DECAY_LORA ** -0.5),
        'rwkv_a0': nrm(ks[11], (L, W), 0.1),
        'rwkv_a2': nrm(ks[12], (L, ICLR_LORA, W), 0.5 * ICLR_LORA ** -0.5),
        'rwkv_g2': nrm(ks[13], (L, 2, GATE_LORA, W), GATE_LORA ** -0.5),
        'rwkv_k_k': 0.85 + nrm(ks[14], (L, W), 0.05),
        'rwkv_k_a': 1.0 + nrm(ks[15], (L, W), 0.05),
        'rwkv_r_k': nrm(ks[16], (L, W), 0.1),
        'rwkv_lnx_w': 1.0 + nrm(ks[17], (L, W), 0.1),
        'rwkv_lnx_b': nrm(ks[18], (L, W), 0.02),
        'w_out': nrm(ks[19], (L, D_MIX, D), D_MIX ** -0.5),
        'w_router': nrm(ks[20], (L, D, E), D ** -0.5),
        'w_gate': nrm(ks[21], (L, E, D, F), D ** -0.5),
        'w_up': nrm(ks[22], (L, E, D, F), D ** -0.5),
        'w_down': nrm(ks[23], (L, E, F, D), F ** -0.5),
    }

def first_block(x, c, ctx, c_ctx, w_mod, b_mod, norm_gains, w_in, rwkv_conv, rwkv_w0, rwkv_w2, rwkv_a0, rwkv_a2,
              rwkv_g2, rwkv_k_k, rwkv_k_a, rwkv_r_k, rwkv_lnx_w, rwkv_lnx_b, w_out, w_router, w_gate, w_up, w_down):
    for i in range(DEPTH):
        need_ctx = i < DEPTH - 1
        sh1, sc1, gt1, sh2, sc2, gt2 = jnp.split((jax.nn.silu(c) @ w_mod[i] + b_mod[i])[:, None, :], 6, axis=-1)
        csh1, csc1, cgt1, csh2, csc2, cgt2 = jnp.split(jax.nn.silu(c_ctx) @ w_mod[i] + b_mod[i], 6, axis=-1)
        g_pre_mix, g_post_mix, g_pre_ffn, g_post_ffn = norm_gains[i]
        h = rms_norm(x, g_pre_mix) * (1.0 + sc1) + sh1
        hc = rms_norm(ctx, g_pre_mix) * (1.0 + csc1) + csh1
        mix, mix_c = token_mix(h, hc, w_in[i], rwkv_conv[i], rwkv_w0[i], rwkv_w2[i], rwkv_a0[i], rwkv_a2[i],
                               rwkv_g2[i], rwkv_k_k[i], rwkv_k_a[i], rwkv_r_k[i], rwkv_lnx_w[i], rwkv_lnx_b[i],
                               w_out[i], need_ctx)
        x = x + gt1 * rms_norm(mix, g_post_mix)
        h2 = rms_norm(x, g_pre_ffn) * (1.0 + sc2) + sh2
        x = x + gt2 * rms_norm(ec_moe(h2, w_router[i], w_gate[i], w_up[i], w_down[i]), g_post_ffn)
        if need_ctx:
            ctx = ctx + cgt1 * rms_norm(mix_c, g_post_mix)
            hc2 = rms_norm(ctx, g_pre_ffn) * (1.0 + csc2) + csh2
            ctx = ctx + cgt2 * rms_norm(ec_moe(hc2, w_router[i], w_gate[i], w_up[i], w_down[i]), g_post_ffn)
    return x


DEPTH_2 = 2

N_MIXERS = 3
HEAD_DIM = 64
EPS = 1e-6
NEG_INF = -1e30

A_HEADS = D_MODEL // HEAD_DIM
A_WINDOWS = (128, 512, 2048)
A_DILATIONS = (1, 4, 16)
A_GROUPS = len(A_WINDOWS)
ROPE_THETA = 500000.0
ROPE_DIMS = HEAD_DIM // 4

B_CONV_WIDTH = 3

C_Q_HEADS = D_MODEL // HEAD_DIM
C_KV_HEADS = 4
C_THETA = 10000.0
Q_BLOCK = 128

D_FF = 4 * D_MODEL

N_A = len(range(0, DEPTH_2, N_MIXERS))
N_B = len(range(1, DEPTH_2, N_MIXERS))
N_C = len(range(2, DEPTH_2, N_MIXERS))


def rms_norm_2(x, g):
    xf = x.astype(jnp.float32)
    y = xf * lax.rsqrt(jnp.mean(xf * xf, axis=-1, keepdims=True) + EPS)
    return (y * g.astype(jnp.float32)).astype(x.dtype)

def rope_angles(pos, dim, theta):
    inv = theta ** (-jnp.arange(0, dim, 2, dtype=jnp.float32) / dim)
    ang = pos.astype(jnp.float32)[:, None] * inv[None, :]
    return jnp.cos(ang), jnp.sin(ang)

def apply_rope(x, cos, sin):
    half = x.shape[-1] // 2
    xf = x.astype(jnp.float32)
    x1, x2 = xf[..., :half], xf[..., half:]
    c, s = cos[:, None, :], sin[:, None, :]
    return jnp.concatenate([x1 * c - x2 * s, x2 * c + x1 * s], axis=-1).astype(x.dtype)

def partial_rope(x, cos, sin):
    return jnp.concatenate([apply_rope(x[..., :ROPE_DIMS], cos, sin), x[..., ROPE_DIMS:]], axis=-1)

def dilated_group(q, k, v, dilation, radius):
    B, S, H, Dh = q.shape
    L = S // dilation
    nb = -(-L // radius)
    Lp = nb * radius

    def split(t):
        t = jnp.moveaxis(t.reshape(B, L, dilation, H, Dh), 2, 1)
        return jnp.pad(t, ((0, 0), (0, 0), (0, Lp - L), (0, 0), (0, 0)))

    def band(t):
        tp = jnp.pad(t, ((0, 0), (0, 0), (radius, radius), (0, 0), (0, 0)))
        tb = tp.reshape(B, dilation, nb + 2, radius, H, Dh)
        return jnp.concatenate([tb[:, :, :-2], tb[:, :, 1:-1], tb[:, :, 2:]], axis=3)

    qb = split(q).reshape(B, dilation, nb, radius, H, Dh)
    kb = band(split(k))
    vb = band(split(v))

    q_idx = jnp.arange(Lp).reshape(nb, radius)
    k_idx = jnp.arange(nb)[:, None] * radius - radius + jnp.arange(3 * radius)[None, :]
    mask = ((jnp.abs(q_idx[:, :, None] - k_idx[:, None, :]) <= radius)
            & (k_idx[:, None, :] >= 0) & (k_idx[:, None, :] < L))

    s = jnp.einsum('bdnqhe,bdnkhe->bdnqhk', qb, kb).astype(jnp.float32) * (HEAD_DIM ** -0.5)
    s = jnp.where(mask[None, None, :, :, None, :], s, NEG_INF)
    mx = jnp.max(s, axis=-1)
    p = jnp.exp(s - mx[..., None])
    den = jnp.sum(p, axis=-1)
    num = jnp.einsum('bdnqhk,bdnkhe->bdnqhe', p, vb.astype(jnp.float32))

    def unsplit(t):
        rest = t.shape[4:]
        t = t.reshape((B, dilation, Lp) + rest)[:, :, :L]
        return jnp.moveaxis(t, 1, 2).reshape((B, S) + rest)

    return unsplit(num), unsplit(den), unsplit(mx)

def mixer_a(h, w_qkv, q_gain, k_gain, w_o, cos, sin):
    B, S, _ = h.shape
    qkv = (h @ w_qkv).reshape(B, S, A_GROUPS, 3, A_HEADS, HEAD_DIM)
    nums, dens, mxs = [], [], []
    for g in range(A_GROUPS):
        dil = A_DILATIONS[g]
        radius = A_WINDOWS[g] // (2 * dil)
        q = partial_rope(rms_norm_2(qkv[:, :, g, 0], q_gain[g]), cos, sin)
        k = partial_rope(rms_norm_2(qkv[:, :, g, 1], k_gain[g]), cos, sin)
        v = qkv[:, :, g, 2]
        num, den, mx = dilated_group(q, k, v, dil, radius)
        nums.append(num); dens.append(den); mxs.append(mx)
    mx = jnp.stack(mxs, 0)
    wts = jnp.exp(mx - jnp.max(mx, axis=0, keepdims=True))
    num = jnp.sum(wts[..., None] * jnp.stack(nums, 0), axis=0)
    den = jnp.sum(wts * jnp.stack(dens, 0), axis=0)
    o = (num / den[..., None]).astype(h.dtype).reshape(B, S, D_MODEL)
    return o @ w_o

def mixer_b(h, w_in, conv_w, w_out):
    b_gate, c_gate, xt = jnp.split(h @ w_in, 3, axis=-1)
    u = c_gate * xt
    y = lax.conv_general_dilated(u, conv_w[:, None, :].astype(u.dtype), window_strides=(1,),
                                 padding=((1, 1),), dimension_numbers=('NWC', 'WIO', 'NWC'),
                                 feature_group_count=D_MODEL)
    return (b_gate * y) @ w_out

def axial_rope_2(x, cos_r, sin_r, cos_c, sin_c):
    half = HEAD_DIM // 2
    return jnp.concatenate([apply_rope(x[..., :half], cos_r, sin_r),
                            apply_rope(x[..., half:], cos_c, sin_c)], axis=-1)

def mixer_c(h, w_qkv, q_gain, k_gain, w_o):
    B, S, _ = h.shape
    rows = S // GRID_W
    row_id = jnp.repeat(jnp.arange(rows), GRID_W)
    col_id = jnp.tile(jnp.arange(GRID_W), rows)
    cos_r, sin_r = rope_angles(row_id, HEAD_DIM // 2, C_THETA)
    cos_c, sin_c = rope_angles(col_id, HEAD_DIM // 2, C_THETA)

    qkv = h @ w_qkv
    nq, nk = C_Q_HEADS * HEAD_DIM, C_KV_HEADS * HEAD_DIM
    q = qkv[..., :nq].reshape(B, S, C_Q_HEADS, HEAD_DIM)
    k = qkv[..., nq:nq + nk].reshape(B, S, C_KV_HEADS, HEAD_DIM)
    v = qkv[..., nq + nk:].reshape(B, S, C_KV_HEADS, HEAD_DIM)
    q = axial_rope_2(rms_norm_2(q, q_gain), cos_r, sin_r, cos_c, sin_c)
    k = axial_rope_2(rms_norm_2(k, k_gain), cos_r, sin_r, cos_c, sin_c)

    grp = C_Q_HEADS // C_KV_HEADS
    nblk = S // Q_BLOCK
    qb = jnp.moveaxis(q.reshape(B, nblk, Q_BLOCK, C_KV_HEADS, grp, HEAD_DIM), 1, 0)

    def attend(qblk):
        s = jnp.einsum('bqhgd,bkhd->bhgqk', qblk, k).astype(jnp.float32) * (HEAD_DIM ** -0.5)
        p = jax.nn.softmax(s, axis=-1)
        return jnp.einsum('bhgqk,bkhd->bqhgd', p.astype(v.dtype), v)

    o = lax.map(attend, qb)
    o = jnp.moveaxis(o, 0, 1).reshape(B, S, D_MODEL)
    return o @ w_o

def mlp_sq_relu(h, w1, w2):
    return jnp.square(jax.nn.relu(h @ w1)) @ w2

def second_inputs(seed: int = 0) -> dict:
    key = jax.random.key(seed)
    ks = jax.random.split(key, 20)
    D, Dh = D_MODEL, HEAD_DIM
    nrm = lambda k, shape, fan_in: jax.random.normal(k, shape, jnp.float32) * (fan_in ** -0.5)
    gain = lambda k, shape: 1.0 + 0.02 * jax.random.normal(k, shape, jnp.float32)
    c_cols = (C_Q_HEADS + 2 * C_KV_HEADS) * Dh
    return {
        "x": jax.random.normal(ks[0], (BATCH, SEQ, D), jnp.float32),
        "norm1": gain(ks[1], (DEPTH_2, D)),
        "norm2": gain(ks[2], (DEPTH_2, D)),
        "a_wqkv": nrm(ks[3], (N_A, D, A_GROUPS * 3 * D), D),
        "a_q_gain": gain(ks[4], (N_A, A_GROUPS, Dh)),
        "a_k_gain": gain(ks[5], (N_A, A_GROUPS, Dh)),
        "a_wo": nrm(ks[6], (N_A, D, D), D),
        "b_win": nrm(ks[7], (N_B, D, 3 * D), D),
        "b_conv": nrm(ks[8], (N_B, B_CONV_WIDTH, D), B_CONV_WIDTH),
        "b_wout": nrm(ks[9], (N_B, D, D), D),
        "c_wqkv": nrm(ks[10], (N_C, D, c_cols), D),
        "c_q_gain": gain(ks[11], (N_C, Dh)),
        "c_k_gain": gain(ks[12], (N_C, Dh)),
        "c_wo": nrm(ks[13], (N_C, D, D), D),
        "mlp_w1": nrm(ks[14], (DEPTH_2, D, D_FF), D),
        "mlp_w2": nrm(ks[15], (DEPTH_2, D_FF, D), D_FF),
    }

def second_block(x, norm1, norm2, a_wqkv, a_q_gain, a_k_gain, a_wo, b_win, b_conv, b_wout,
              c_wqkv, c_q_gain, c_k_gain, c_wo, mlp_w1, mlp_w2):
    S = x.shape[1]
    cos, sin = rope_angles(jnp.arange(S), ROPE_DIMS, ROPE_THETA)
    h = x
    for i in range(DEPTH_2):
        kind, j = i % N_MIXERS, i // N_MIXERS
        y = rms_norm_2(h, norm1[i])
        if kind == 0:
            y = mixer_a(y, a_wqkv[j], a_q_gain[j], a_k_gain[j], a_wo[j], cos, sin)
        elif kind == 1:
            y = mixer_b(y, b_win[j], b_conv[j], b_wout[j])
        else:
            y = mixer_c(y, c_wqkv[j], c_q_gain[j], c_k_gain[j], c_wo[j])
        h = h + y
        h = h + mlp_sq_relu(rms_norm_2(h, norm2[i]), mlp_w1[i], mlp_w2[i])
    return h


def setup_inputs(seed=0):
    out = dict(first_inputs(seed))
    for name, value in second_inputs(seed + 1).items():
        if name != "x":
            out[name + "_2"] = value
    return out


def reference(
    x, c, ctx, c_ctx, w_mod, b_mod, norm_gains, w_in, rwkv_conv, rwkv_w0, rwkv_w2, rwkv_a0,
    rwkv_a2, rwkv_g2, rwkv_k_k, rwkv_k_a, rwkv_r_k, rwkv_lnx_w, rwkv_lnx_b, w_out, w_router,
    w_gate, w_up, w_down, norm1_2, norm2_2, a_wqkv_2, a_q_gain_2, a_k_gain_2, a_wo_2, b_win_2,
    b_conv_2, b_wout_2, c_wqkv_2, c_q_gain_2, c_k_gain_2, c_wo_2, mlp_w1_2, mlp_w2_2,
):
    x = first_block(
        x, c, ctx, c_ctx, w_mod, b_mod, norm_gains, w_in, rwkv_conv, rwkv_w0, rwkv_w2, rwkv_a0,
        rwkv_a2, rwkv_g2, rwkv_k_k, rwkv_k_a, rwkv_r_k, rwkv_lnx_w, rwkv_lnx_b, w_out, w_router,
        w_gate, w_up, w_down,
    )
    return second_block(
        x, norm1_2, norm2_2, a_wqkv_2, a_q_gain_2, a_k_gain_2, a_wo_2, b_win_2, b_conv_2,
        b_wout_2, c_wqkv_2, c_q_gain_2, c_k_gain_2, c_wo_2, mlp_w1_2, mlp_w2_2,
    )


_drawn_inputs = setup_inputs


def setup_inputs(seed=0):
    import zlib

    import numpy as np

    out = dict(_drawn_inputs(seed))
    spreads = {}
    factors = {'rwkv_lnx_b': 8.0,
     'norm1_2': 2.787,
     'a_q_gain_2': 8.0,
     'a_k_gain_2': 8.0,
     'norm2_2': 3.792}
    for name, (base, spread) in spreads.items():
        noise = np.random.default_rng([zlib.crc32(name.encode()), seed]).standard_normal(out[name].shape)
        drawn = base * np.exp(spread * noise) if base else spread * noise
        out[name] = __import__('jax').numpy.asarray(drawn.astype(out[name].dtype))
    for name, factor in factors.items():
        out[name] = (out[name] * factor).astype(out[name].dtype)
    return out
```

```python
from contextlib import ExitStack

import numpy as np

import concourse.bass as bass
from concourse import mybir

F32 = mybir.dt.float32
U32 = mybir.dt.uint32
ALU = mybir.AluOpType
ACT = mybir.ActivationFunctionType
AX = mybir.AxisListType.X

P = 128
D = 1024
KD = D // P
T = 512
TC = 256
TA = T + TC
NT = T // P
NTC = TC // P
HD = 64
EPS = 1e-6
GN_EPS = 64e-5
RET_W = 512
RET_H = RET_W // HD
RET_COLS = 5 * RET_W
RW_W = 512
RW_COLS = 3 * RW_W + 64 * 3 + 128 * 2
E_N = 16
CAP = 2 * T // E_N
FF = 4 * D
GRID_W = 64
SLOTS = 6
PW = 256
DECAY = float(np.exp(-0.5))


class Buffers:
    pass


class Tally:

    def __init__(self, sem):
        self.sem, self.n = sem, 0

    def link(self, eng, ins):
        self.n += 1
        ins.then_inc(self.sem, 1)
        eng.wait_ge(self.sem, self.n)

    def mark(self, ins):
        self.n += 1
        ins.then_inc(self.sem, 1)

    def settle(self, eng):
        eng.wait_ge(self.sem, self.n)


class Stream:

    def __init__(self, ring, full, used):
        self.ring, self.full, self.used = ring, full, used
        self.panels, self.landed = [], []
        self.loaded = self.taken = 0
        self.counts = [0] * SLOTS

    def add(self, *pieces):
        s = len(self.panels) % SLOTS
        self.counts[s] += 16 * len(pieces)
        self.panels.append(pieces)
        self.landed.append(self.counts[s])

    def add_matrix(self, w, rows, c0, c1):
        for c in range(c0, c1, PW):
            self.add((w[rows:rows + D, c:min(c + PW, c1)], 0))

    def load_until(self, sp, n):
        while self.loaded < min(n, len(self.panels)):
            p, s = self.loaded, self.loaded % SLOTS
            if p >= SLOTS:
                sp.wait_ge(self.used, p - SLOTS + 1)
            for src, c in self.panels[p]:
                w = src.shape[1]
                sp.dma_start(self.ring[:, s, :, c:c + w],
                             src.rearrange("(k p) n -> p k n", p=P)).then_inc(self.full[s], 16)
            self.loaded += 1

    def take(self, pe):
        p, s = self.taken, self.taken % SLOTS
        pe.wait_ge(self.full[s], self.landed[p])
        self.taken += 1
        return self.ring[:, s]


def consts():
    i = np.arange(P)
    f = np.float32
    out = {}
    out["ident"] = np.eye(P, dtype=f)
    out["headsum"] = (i[:, None] // HD == i[None, :] // HD).astype(f)
    before = (i[:, None] < i[None, :])
    low = [np.zeros((P, 2, P), f) for _ in range(9)]
    for d in range(2):
        b = before if d == 0 else before.T
        low[0][:, d] = b
        low[1][:, d] = b | np.eye(P, dtype=bool)
        for lv in range(7):
            h = 1 << lv
            low[2 + lv][:, d] = b & (i[:, None] // (2 * h) == i[None, :] // (2 * h)) & (i[:, None] // h != i[None, :] // h)
    out["tri"] = np.stack(low, 1)
    t = np.arange(T)
    freq = 10000.0 ** (-np.arange(16) / 16.0)
    freq = freq.astype(f).astype(np.float64)
    ang = np.concatenate([(t // GRID_W)[:, None] * freq, (t % GRID_W)[:, None] * freq], -1)
    ang = ang.astype(f).astype(np.float64).reshape(NT, P, 32).transpose(1, 0, 2)
    out["rope"] = np.stack([np.cos(ang), np.sin(ang)], 1).astype(f)
    inv = (500000.0 ** (-np.arange(0, 16, 2) / 16.0)).astype(f).astype(np.float64)
    ang = (t[:, None] * inv).astype(f).astype(np.float64).reshape(P, NT, 8)
    out["rope2"] = np.stack([np.cos(ang), np.sin(ang)], 1).astype(f)
    x = np.arange(TA)
    far = 1e9
    ef = (x[None] - i[:, None]).astype(f)
    ef[ef < 0] = far
    eb = (i[:, None] + 640 - x[None]).astype(f)
    eb[eb < 0] = far
    out["dist"] = np.stack([ef, eb], 1)
    rs = np.ones((P, TA), f)
    rs[:, ::P] = 0
    rb = np.ones((P, TA), f)
    rb[:, P - 1::P] = 0
    out["restart"] = np.stack([rs, rb], 1)
    tok = np.arange(P)[None] * 4 + np.arange(4)[:, None]
    far0 = np.abs(tok.T[:, :, None, None] - tok[None, None]) > 64
    out["band"] = np.where(far0, f(-1e30), f(0)).astype(f)
    m1 = np.abs(i[:, None] - i[None]) > 64
    m2 = (i[:, None] % 4) != (i[None] % 4)
    out["stride"] = np.stack([np.where(m1, f(-1e30), f(0)), np.where(m2, f(-1e30), f(0))], 1).astype(f)
    out["tokrow"] = np.broadcast_to(tok.reshape(T).astype(f), (P, T)).copy()
    out["tokcol"] = (np.arange(4)[None] + 4 * i[:, None]).astype(f)
    pick = np.zeros((E_N, E_N, P), f)
    for e in range(E_N):
        pick[e, e] = 1
    out["pick"] = pick
    return {"c_" + k: np.ascontiguousarray(v) for k, v in out.items()}


CONSTS = {k: v.shape for k, v in consts().items()}


def setup(nc, g, a):
    sem = g.sem
    loaded = sem("params_loaded")
    padded = sem("params_padded")
    turned = sem("params_turned")
    copied = sem("params_copied")
    rows = [[("c", 8, a["c"]), ("c_ctx", 8, a["c_ctx"]), ("b_mod", 48, a["b_mod"]), ("gains", 32, a["norm_gains"])],
            [], []]
    cv = a["rwkv_conv"]
    for tap in range(3):
        rows[1] += [(f"conv{tap}", 13, cv[tap, 0:1664]), (f"conv{tap}_al", 1, cv[tap, 1664:1728]),
                    (f"conv{tap}_gl", 2, cv[tap, 1728:1984])]
    rows[1] += [("w0", 8, a["rwkv_w0"]), ("a0", 4, a["rwkv_a0"]), ("k_k", 4, a["rwkv_k_k"]),
                ("k_a", 4, a["rwkv_k_a"]), ("r_k", 4, a["rwkv_r_k"]), ("lnx_w", 4, a["rwkv_lnx_w"]),
                ("lnx_b", 4, a["rwkv_lnx_b"])]
    rows[2] += [("norm1", 16, a["norm1_2"]), ("norm2", 16, a["norm2_2"]), ("b_conv", 24, a["b_conv_2"])]
    g.col = {}
    n_dma = sum(len(r) for r in rows) + 2
    with ExitStack() as tmp, nc.Block() as block:
        raw = tmp.enter_context(nc.sbuf_tensor("param_rows", [P, 3, P], F32))
        turn = tmp.enter_context(nc.psum_tensor("param_cols", [P, 3, P], F32))

        for n, group in enumerate(rows):
            at = 0
            for name, k, _ in group:
                g.col[name] = n * P + at
                at += k

        @block.sync
        def _(sp):
            g.stream.load_until(sp, SLOTS)

        @block.scalar
        def _(act):
            act.dma_start(g.ident[:], a["c_ident"]).then_inc(loaded, 16)
            act.dma_start(g.headsum[:], a["c_headsum"]).then_inc(loaded, 16)
            act.wait_ge(padded, 1)
            for n, group in enumerate(rows):
                at = 0
                for name, k, src in group:
                    if name.endswith("_al"):
                        act.dma_start(raw[at:at + 1, n, 0:64], src.rearrange("(k n) -> k n", k=1)).then_inc(loaded, 16)
                    else:
                        act.dma_start(raw[at:at + k, n, :], src.rearrange("(k n) -> k n", n=P)).then_inc(loaded, 16)
                    at += k

        @block.gpsimd
        def _(pool):
            nc.gpsimd.memset(raw[:], 0.0).then_inc(padded, 1)
            nc.gpsimd.memset(g.ones[:], 1.0)

        @block.tensor
        def _(pe):
            pe.wait_ge(loaded, 16 * n_dma)
            for n in range(3):
                last = nc.tensor.transpose(turn[:, n, :], raw[:, n, :], g.ident[:])
            last.then_inc(turned, 1)

        @block.vector
        def _(dve):
            dve.wait_ge(turned, 1)
            nc.vector.tensor_copy(g.cols[:], turn[:].rearrange("p a b -> p (a b)")).then_inc(copied, 1)


def modulation(nc, g):
    sem, st = g.sem, g.stream
    n_col = 6 * KD
    n_panel = 6 * D // PW
    p0 = st.taken
    sigmoid_ready = sem("c_sigmoid_ready")
    silu_ready = sem("c_silu_ready")
    step = Tally(sem("mod_steps"))
    cc = g.col["c"]
    c_cols = g.cols[:, cc:cc + 2 * KD].rearrange("p (c k) -> p k c", c=2)
    with ExitStack() as tmp, nc.Block() as block:
        silu = tmp.enter_context(nc.sbuf_tensor("c_silu", [P, KD, 2], F32))
        sig = tmp.enter_context(nc.sbuf_tensor("c_sig", [P, KD, 2], F32))
        acc = tmp.enter_context(nc.psum_tensor("mod_acc", [P, n_col, 2], F32))

        @block.sync
        def _(sp):
            st.load_until(sp, p0 + n_panel + SLOTS)

        @block.scalar
        def _(act):
            nc.scalar.activation(sig[:], c_cols, ACT.Sigmoid).then_inc(sigmoid_ready, 1)

        @block.vector
        def _(dve):
            dve.wait_ge(sigmoid_ready, 1)
            nc.vector.tensor_tensor(silu[:], sig[:], c_cols, ALU.mult).then_inc(silu_ready, 1)
            b = g.cols[:, g.col["b_mod"]:g.col["b_mod"] + n_col].unsqueeze(2).to_broadcast([P, n_col, 2])
            dve.wait_ge(st.used, p0 + n_panel)
            step.link(dve, nc.vector.tensor_tensor(g.mod[:], acc[:], b, ALU.add))
            gain = g.cols[:, g.col["gains"]:g.col["gains"] + KD].unsqueeze(2).to_broadcast([P, KD, 2])
            step.link(dve, nc.vector.tensor_scalar(g.mix_scale[:], g.mod[:, KD:2 * KD, :], 1.0, None, ALU.add))
            gains = lambda i: g.cols[:, g.col["gains"] + i * KD:g.col["gains"] + (i + 1) * KD]
            step.link(dve, nc.vector.tensor_tensor(g.mix_scale[:], g.mix_scale[:], gain, ALU.mult))
            step.link(dve, nc.vector.tensor_scalar(g.ffn_scale[:], g.mod[:, 4 * KD:5 * KD, :], 1.0, None, ALU.add))
            step.mark(nc.vector.tensor_tensor(g.ffn_scale[:], g.ffn_scale[:], gains(2).unsqueeze(2).to_broadcast([P, KD, 2]), ALU.mult))
            step.mark(nc.vector.tensor_tensor(g.post[:, 0], g.mod[:, 2 * KD:3 * KD, 0], gains(1), ALU.mult))
            step.mark(nc.vector.tensor_tensor(g.post[:, 1], g.mod[:, 5 * KD:6 * KD, 0], gains(3), ALU.mult))

        @block.tensor
        def _(pe):
            pe.wait_ge(silu_ready, 1)
            for n in range(n_panel):
                w = st.take(pe)
                for h in range(PW // P):
                    for k in range(KD):
                        last = nc.tensor.matmul(acc[:, 2 * n + h, :], w[:, k, h * P:(h + 1) * P], silu[:, k, :],
                                                start=(k == 0), stop=(k == KD - 1))
                last.then_inc(st.used, 1)


def norm_turn(nc, g, name, groups, permuted=False):
    sem = g.sem
    squares = sem(name + "_squares")
    meaned = sem(name + "_mean_ready")
    rooted = sem(name + "_root_ready")
    scaled = sem(name + "_tiles_scaled")
    turned = sem(name + "_turned")
    written = sem(name + "_written")
    step = Tally(sem(name + "_steps"))
    n_tile = sum(x[1] for x in groups)
    with ExitStack() as tmp, nc.Block() as block:
        junk = tmp.enter_context(nc.sbuf_tensor(name + "_sq", [P, 2, D], F32))
        xn = tmp.enter_context(nc.sbuf_tensor(name + "_xn", [P, n_tile, D], F32))
        ms = tmp.enter_context(nc.sbuf_tensor(name + "_ms", [P, n_tile], F32))
        rt = tmp.enter_context(nc.sbuf_tensor(name + "_rt", [P, n_tile], F32))
        rs = tmp.enter_context(nc.sbuf_tensor(name + "_rs", [P, n_tile], F32))
        acc = [tmp.enter_context(nc.psum_tensor(f"{name}_t{i}", [P, 4, P], F32)) for i in range(4)]
        tiles = [grp[0][:, j, :] for grp in groups for j in range(grp[1])]
        turns = [(grp, k) for grp in groups for k in range(KD)]
        base = [sum(x[1] for x in groups[:i]) for i in range(len(groups))]

        @block.scalar
        def _(act):
            for n, x in enumerate(tiles):
                if n >= 2:
                    act.wait_ge(squares, n - 1)
                nc.scalar.activation(junk[:, n % 2, :], x, ACT.Square, accum_out=ms[:, n:n + 1]).then_inc(squares, 1)
            act.wait_ge(meaned, 1)
            nc.scalar.activation(rt[:], ms[:], ACT.Sqrt).then_inc(rooted, 1)

        @block.vector
        def _(dve):
            dve.wait_ge(squares, n_tile)
            nc.vector.tensor_scalar(ms[:], ms[:], 1.0 / D, EPS, ALU.mult, ALU.add).then_inc(meaned, 1)
            dve.wait_ge(rooted, 1)
            step.link(dve, nc.vector.reciprocal(rs[:], rt[:]))
            for n, x in enumerate(tiles):
                nc.vector.tensor_scalar(xn[:, n, :], x, rs[:, n:n + 1], None, ALU.mult).then_inc(scaled, 1)
            for i, (grp, k) in enumerate(turns):
                _, nt, out, t0, scale, shift = grp
                dve.wait_ge(turned, i + 1)
                order = "c (j p) -> c j p" if permuted else "c (p j) -> c j p"
                dst = out[:, k, t0:t0 + nt * P].rearrange(order, j=nt)
                src = acc[i % 4][:, 0:nt, :]
                if shift is None:
                    nc.vector.tensor_scalar(dst, src, scale(k), None, ALU.mult).then_inc(written, 1)
                else:
                    nc.vector.tensor_scalar(dst, src, scale(k), shift(k), ALU.mult, ALU.add).then_inc(written, 1)

        @block.tensor
        def _(pe):
            for i, (grp, k) in enumerate(turns):
                b = base[groups.index(grp)]
                if k == 0:
                    pe.wait_ge(scaled, b + grp[1])
                if i >= 4:
                    pe.wait_ge(written, i - 3)
                for j in range(grp[1]):
                    last = nc.tensor.transpose(acc[i % 4][:, j, :], xn[:, b + j, k * P:(k + 1) * P], g.ident[:])
                last.then_inc(turned, 1)


def retention_inputs(nc, g, hT, q_tok, k_tok, v_tok, gates, rope):
    sem, st = g.sem, g.stream
    p0 = st.taken
    n_panel = RET_COLS // PW
    emptied = sem("ret_banks_emptied")
    gated = sem("ret_gates_emptied")
    step = Tally(sem("ret_rope_steps"))
    with ExitStack() as tmp, nc.Block() as block:
        acc = [tmp.enter_context(nc.psum_tensor(f"ret_in{i}", [P, 512], F32)) for i in range(6)]
        prod = [tmp.enter_context(nc.sbuf_tensor(f"ret_rope{i}", [P, NT, RET_H, 32], F32)) for i in range(4)]

        def tiles(n):
            return range(NTC, NTC + NT) if n < 2 else range(NTC + NT)

        @block.sync
        def _(sp):
            st.load_until(sp, p0 + n_panel + SLOTS)

        @block.tensor
        def _(pe):
            for n in range(6):
                w = st.take(pe)
                if n >= 2:
                    pe.wait_ge(emptied, n - 1)
                for i, t in enumerate(tiles(n)):
                    dst = acc[3 * (n % 2) + i // 2][:, (i % 2) * PW:(i % 2 + 1) * PW]
                    for k in range(KD):
                        last = nc.tensor.matmul(dst, hT[:, k, t * P:(t + 1) * P], w[:, k, :],
                                                start=(k == 0), stop=(k == KD - 1))
                last.then_inc(st.used, 1)
            for n in range(6, n_panel):
                w = st.take(pe)
                pe.wait_ge(emptied, min(n - 1, 6))
                if n >= 8:
                    pe.wait_ge(gated, n - 7)
                for h in range(2):
                    for k in range(KD):
                        last = nc.tensor.matmul(acc[3 * (n % 2) + h][:], w[:, k, h * P:(h + 1) * P], hT[:, k, TC:TA],
                                                start=(k == 0), stop=(k == KD - 1))
                last.then_inc(st.used, 1)

        def rotate(dve, x):
            v = x[:, :, :].rearrange("p t (h d) -> p t h d", d=HD)
            x1, x2 = v[:, :, :, 0:32], v[:, :, :, 32:64]
            cos, sin = (rope[:, i].unsqueeze(2).to_broadcast([P, NT, RET_H, 32]) for i in range(2))
            for dst, half, tab in ((prod[0], x1, cos), (prod[1], x2, sin), (prod[2], x2, cos), (prod[3], x1, sin)):
                step.mark(nc.vector.tensor_tensor(dst[:], half, tab, ALU.mult))
            step.settle(dve)
            step.mark(nc.vector.tensor_tensor(x1, prod[0][:], prod[1][:], ALU.subtract))
            step.mark(nc.vector.tensor_tensor(x2, prod[2][:], prod[3][:], ALU.add))
            step.settle(dve)

        @block.vector
        def _(dve):
            for n in range(6):
                dve.wait_ge(st.used, p0 + n + 1)
                ts = list(tiles(n))
                c = slice((n % 2) * PW, (n % 2 + 1) * PW)
                for i in range(0, len(ts), 2):
                    src = acc[3 * (n % 2) + i // 2][:].rearrange("p (t c) -> p t c", t=2)
                    dst = (q_tok[:, ts[i] - NTC:ts[i] - NTC + 2, c] if n < 2 else (k_tok if n < 4 else v_tok)[:, ts[i]:ts[i] + 2, c])
                    last = nc.vector.tensor_copy(dst, src)
                last.then_inc(emptied, 1)
                if n in (1, 3):
                    dve.wait_ge(emptied, n + 1)
                    rotate(dve, q_tok if n == 1 else k_tok[:, NTC:, :])

        @block.scalar
        def _(act):
            for n in range(6, n_panel):
                act.wait_ge(st.used, p0 + n + 1)
                for h in range(2):
                    last = nc.scalar.activation(gates[:, 2 * (n - 6) + h, :], acc[3 * (n % 2) + h][:], ACT.Silu)
                last.then_inc(gated, 1)


def retention_turn(nc, g, q_tok, k_tok, qT, kT):
    sem = g.sem
    turned = sem("ret_turned")
    written = sem("ret_turn_written")
    jobs = [(x, hp) for hp in range(4) for x in "qkc"]
    with ExitStack() as tmp, nc.Block() as block:
        acc = [tmp.enter_context(nc.psum_tensor(f"ret_t{i}", [P, 4, P], F32)) for i in range(4)]

        @block.tensor
        def _(pe):
            for n, (x, hp) in enumerate(jobs):
                if n >= 4:
                    pe.wait_ge(written, n - 3)
                for t in range(NTC if x == "c" else NT):
                    src = q_tok[:, t] if x == "q" else k_tok[:, t if x == "c" else NTC + t]
                    last = nc.tensor.transpose(acc[n % 4][:, t, :], src[:, hp * P:(hp + 1) * P], g.ident[:])
                last.then_inc(turned, 1)

        @block.vector
        def _(dve):
            for n, (x, hp) in enumerate(jobs):
                dve.wait_ge(turned, n + 1)
                if x == "q":
                    ins = nc.vector.tensor_copy(qT[:, hp, :], acc[n % 4][:].rearrange("p t c -> p (t c)"))
                else:
                    nt, t0 = (NTC, 0) if x == "c" else (NT, TC)
                    ins = nc.vector.tensor_scalar(kT[:, hp, t0:t0 + nt * P], acc[n % 4][:, 0:nt, :].rearrange("p t c -> p (t c)"),
                                                  HD ** -0.5, None, ALU.mult)
                ins.then_inc(written, 1)


def retention(nc, g, qT, kT, v_tok, gates, dist, latT):
    sem = g.sem
    strips_ready = sem("ret_strips_ready")
    scored = sem("ret_scored")
    decayed = sem("ret_decayed")
    applied = sem("ret_applied")
    squared = sem("ret_squared")
    summed = sem("ret_sums_ready")
    meaned = sem("ret_mean_ready")
    rooted = sem("ret_root_ready")
    normed = sem("ret_normed")
    step = Tally(sem("ret_norm_steps"))
    jobs = [(h, j) for h in range(RET_H) for j in range(NTC + NT)]
    per_pair = 2 * (NTC + NT)
    lg = [float(np.log1p(-np.exp2(-5.0 - h))) for h in range(RET_H)]
    with ExitStack() as tmp, nc.Block() as block:
        strip = tmp.enter_context(nc.sbuf_tensor("ret_strip", [P, 2, 2, TA], F32))
        dec = tmp.enter_context(nc.sbuf_tensor("ret_decayed_scores", [P, 2, 2, T], F32))
        sq = tmp.enter_context(nc.sbuf_tensor("ret_sq", [P, 2, T], F32))
        rt = tmp.enter_context(nc.sbuf_tensor("ret_rt", [P, 2, T], F32))
        part = tmp.enter_context(nc.sbuf_tensor("ret_part", [P, 2, T], F32))
        sc = [tmp.enter_context(nc.psum_tensor(f"ret_s{i}", [P, T], F32)) for i in range(3)]
        y = [[tmp.enter_context(nc.psum_tensor(f"ret_y{i}{d}", [P, T], F32)) for d in range(2)] for i in range(2)]
        ms = tmp.enter_context(nc.psum_tensor("ret_ms", [P, T], F32))

        def span(j, d):
            if j < NTC:
                return 0, T, (TC - P * j if d == 0 else P - P * j)
            t = j - NTC
            return (P * t, T, 0) if d == 0 else (0, P * (t + 1), 640 - P * t)

        @block.scalar
        def _(act):
            def strips(h):
                if h >= 2:
                    act.wait_ge(decayed, (NTC + NT) * (h - 1))
                for d in range(2):
                    last = nc.scalar.activation(strip[:, h % 2, d, :], dist[:, d, :], ACT.Exp, scale=lg[h])
                last.then_inc(strips_ready, 1)

            def squares(hp):
                act.wait_ge(applied, per_pair * (hp + 1))
                for d in range(2):
                    if hp >= 1:
                        act.wait_ge(summed, 2 * (hp - 1) + d + 1)
                    nc.scalar.activation(sq[:, d, :], y[hp % 2][d][:], ACT.Square).then_inc(squared, 1)

            def roots(hp):
                for d in range(2):
                    act.wait_ge(meaned, 2 * hp + d + 1)
                    nc.scalar.activation(rt[:, d, :], rt[:, d, :], ACT.Sqrt).then_inc(rooted, 1)

            for hp in range(4):
                strips(2 * hp)
                if hp:
                    squares(hp - 1)
                strips(2 * hp + 1)
                if hp:
                    roots(hp - 1)
            squares(3)
            roots(3)

        @block.tensor
        def _(pe):
            def score(n):
                h, j = jobs[n]
                e = slice(HD * (h % 2), HD * (h % 2 + 1))
                if n >= 3:
                    pe.wait_ge(decayed, n - 2)
                nc.tensor.matmul(sc[n % 3][:], kT[e, h // 2, j * P:(j + 1) * P], qT[e, h // 2, :],
                                 start=True, stop=True).then_inc(scored, 1)

            def apply(n):
                h, j = jobs[n]
                e = slice(HD * (h % 2), HD * (h % 2 + 1))
                hp = h // 2
                if n % per_pair == 0 and hp >= 2:
                    pe.wait_ge(normed, 2 * (hp - 1))
                pe.wait_ge(decayed, n + 1)
                for d in range(2):
                    i0, i1, _ = span(j, d)
                    last = nc.tensor.matmul(y[hp % 2][d][e, i0:i1], v_tok[:, j, h * HD:(h + 1) * HD], dec[:, n % 2, d, i0:i1],
                                            start=(j == 0), stop=(j == NTC + NT - 1))
                last.then_inc(applied, 1)

            def sums(hp, d):
                pe.wait_ge(squared, 2 * hp + d + 1)
                if 2 * hp + d >= 1:
                    pe.wait_ge(meaned, 2 * hp + d)
                nc.tensor.matmul(ms[:], g.headsum[:], sq[:, d, :], start=True, stop=True).then_inc(summed, 1)

            score(0)
            for n in range(len(jobs)):
                if n + 1 < len(jobs):
                    score(n + 1)
                apply(n)
                if n >= per_pair and n % per_pair in (3, 7):
                    sums(n // per_pair - 1, 0 if n % per_pair == 3 else 1)
            sums(3, 0)
            sums(3, 1)

        @block.vector
        def _(dve):
            def decay(n):
                h, j = jobs[n]
                if j == 0:
                    dve.wait_ge(strips_ready, h + 1)
                if n >= 2:
                    dve.wait_ge(applied, n - 1)
                dve.wait_ge(scored, n + 1)
                for d in range(2):
                    i0, i1, x0 = span(j, d)
                    last = nc.vector.tensor_tensor(dec[:, n % 2, d, i0:i1], sc[n % 3][:, i0:i1],
                                                   strip[:, h % 2, d, x0:x0 + i1 - i0], ALU.mult)
                last.then_inc(decayed, 1)

            def norm(hp, d):
                dve.wait_ge(summed, 2 * hp + d + 1)
                nc.vector.tensor_scalar(rt[:, d, :], ms[:], 1.0 / HD, EPS, ALU.mult, ALU.add).then_inc(meaned, 1)
                dve.wait_ge(rooted, 2 * hp + d + 1)
                step.link(dve, nc.vector.reciprocal(part[:, d, :], rt[:, d, :]))
                step.link(dve, nc.vector.tensor_tensor(part[:, d, :], part[:, d, :], gates[:, 4 * d + hp, :], ALU.mult))
                ins = nc.vector.tensor_tensor(part[:, d, :], part[:, d, :], y[hp % 2][d][:], ALU.mult)
                ins.then_inc(normed, 1)
                if d == 1:
                    dve.wait_ge(normed, 2 * hp + 2)
                    dst = latT[:, hp, :].rearrange("c (j p) -> c p j", j=NT)
                    f, b = (part[:, i, :].rearrange("c (p j) -> c p j", j=NT) for i in range(2))
                    step.link(dve, nc.vector.tensor_tensor(dst, f, b, ALU.add))

            for n in range(len(jobs)):
                decay(n)
                if n >= per_pair and n % per_pair in (5, 9):
                    norm(n // per_pair - 1, 0 if n % per_pair == 5 else 1)
            norm(3, 0)
            norm(3, 1)


def conv_taps(g, idx):
    return [g.cols[:, g.col[f"conv{t}"] + idx:g.col[f"conv{t}"] + idx + 1] for t in range(3)]


def conv(nc, dve, step, g, idx, out, parts, n=P):
    w = [x[0:n] for x in conv_taps(g, idx)]
    for src, t0, ln in parts:
        step.mark(nc.vector.tensor_scalar(out[0:n, t0:t0 + ln], src[0:n], w[1], None, ALU.mult))
    step.settle(dve)
    for src, t0, ln in parts:
        d = out[0:n, t0 + 1:t0 + ln]
        step.mark(nc.vector.scalar_tensor_tensor(d, src[0:n, 0:ln - 1], w[0], d, ALU.mult, ALU.add))
    step.settle(dve)
    for src, t0, ln in parts:
        d = out[0:n, t0:t0 + ln - 1]
        step.mark(nc.vector.scalar_tensor_tensor(d, src[0:n, 1:ln], w[2], d, ALU.mult, ALU.add))
    step.settle(dve)


def rwkv_low(nc, g, hT, wl, al, gl):
    sem, st = g.sem, g.stream
    p0 = st.taken
    step = Tally(sem("rw_low_steps"))
    with ExitStack() as tmp, nc.Block() as block:
        acc = [tmp.enter_context(nc.psum_tensor(f"rw_low{i}", [P, T], F32)) for i in range(5)]

        @block.sync
        def _(sp):
            st.load_until(sp, p0 + 2 + SLOTS)

        @block.tensor
        def _(pe):
            w = st.take(pe)
            for dst, c, n in ((0, slice(0, P), P), (2, slice(P, P + 64), 64)):
                for k in range(KD):
                    nc.tensor.matmul(acc[dst][0:n, :], w[:, k, c], hT[:, k, TC:], start=(k == 0), stop=(k == KD - 1))
                for k in range(KD):
                    last = nc.tensor.matmul(acc[1][0:n, dst * P:dst * P + TC], w[:, k, c], hT[:, k, 0:TC],
                                            start=(k == 0), stop=(k == KD - 1))
            last.then_inc(st.used, 1)
            w = st.take(pe)
            for d in range(2):
                for k in range(KD):
                    last = nc.tensor.matmul(acc[3 + d][:], w[:, k, d * P:(d + 1) * P], hT[:, k, TC:],
                                            start=(k == 0), stop=(k == KD - 1))
            last.then_inc(st.used, 1)

        @block.vector
        def _(dve):
            dve.wait_ge(st.used, p0 + 1)
            conv(nc, dve, step, g, 12, wl, [(acc[0][:], TC, T), (acc[1][:, 0:TC], 0, TC)])
            conv(nc, dve, step, g, 13, al, [(acc[2][:], TC, T), (acc[1][:, TC:T], 0, TC)], 64)
            dve.wait_ge(st.used, p0 + 2)
            for d in range(2):
                conv(nc, dve, step, g, 14 + d, gl[:, d], [(acc[3 + d][:], 0, T)])

        @block.scalar
        def _(act):
            act.wait_ge(step.sem, 12)
            nc.scalar.activation(wl[:], wl[:], ACT.Tanh)
            act.wait_ge(step.sem, 18)
            nc.scalar.activation(gl[:], gl[:], ACT.Sigmoid)


def rwkv_prepare(nc, g, hp, hT, f, low, par, restart):
    sem, st = g.sem, g.stream
    p0 = st.taken
    nm = f"rw{hp}_"
    NB = TA // P
    low_done = sem(nm + "decay_logits")
    sig_done = sem(nm + "sigmoids")
    sq_ready = sem(nm + "k_squared")
    sums_done = sem(nm + "head_sums")
    eps_done = sem(nm + "norm_sum_copied")
    root_done = sem(nm + "norm_rooted")
    exps_in = sem(nm + "exponents")
    exps_out = sem(nm + "exps")
    bonus_in = sem(nm + "bonus_terms")
    step = Tally(sem(nm + "prep_steps"))
    col = lambda name, i=hp: g.cols[:, g.col[name] + i:g.col[name] + i + 1]
    hc = slice(hp * P, (hp + 1) * P)
    blocks = lambda x: x.rearrange("c (b t) -> c b t", t=P)
    with ExitStack() as tmp, nc.Block() as block:
        t_ = lambda n, w=TA: tmp.enter_context(nc.sbuf_tensor(nm + n, [P, w], F32))
        r, k, kk, bn, km, ic = t_("r", T), t_("k"), t_("kk"), t_("b"), t_("km"), t_("ic")
        sg = [t_(f"sg{d}") for d in range(2)]
        cs = [t_(f"cs{d}") for d in range(2)]
        ex = [t_(f"ex{i}")[:] for i in range(3)] + [f.Y[:].rearrange("c d t -> c (d t)")[:, 0:TA]]
        acc = [tmp.enter_context(nc.psum_tensor(f"{nm}p{i}", [P, T], F32)) for i in range(8)]

        @block.sync
        def _(sp):
            st.load_until(sp, p0 + 2 + SLOTS)

        @block.tensor
        def _(pe):
            def project(dst, w, tokens):
                for i in range(KD):
                    last = nc.tensor.matmul(dst, w[:, i, :], hT[:, i, tokens], start=(i == 0), stop=(i == KD - 1))
                return last
            lat, ctx = slice(TC, TA), slice(0, TC)
            w = st.take(pe)
            project(acc[0][:], w[:, :, 0:P], lat)
            project(acc[1][:], w[:, :, P:2 * P], lat)
            project(acc[2][:, 0:TC], w[:, :, P:2 * P], ctx).then_inc(st.used, 1)
            w = st.take(pe)
            project(acc[3][:], w[:, :, 0:P], lat)
            project(acc[2][:, TC:T], w[:, :, 0:P], ctx).then_inc(st.used, 1)
            for d in range(2):
                e = slice(64 * d, 64 * (d + 1))
                nc.tensor.matmul(acc[4 + 2 * d][:], par.w2[e, hc], low.wl[e, lat], start=True, stop=True)
                last = nc.tensor.matmul(acc[5 + 2 * d][:, 0:TC], par.w2[e, hc], low.wl[e, ctx], start=True, stop=True)
            last.then_inc(low_done, 1)
            pe.wait_ge(sig_done, 2)
            nc.tensor.matmul(acc[4][:], par.a2[0:64, hc], low.al[0:64, lat], start=True, stop=True)
            nc.tensor.matmul(acc[5][:, 0:TC], par.a2[0:64, hc], low.al[0:64, ctx], start=True, stop=True).then_inc(low_done, 1)
            pe.wait_ge(sq_ready, 1)
            nc.tensor.matmul(acc[6][:], g.headsum[:], ex[0][:, lat], start=True, stop=True)
            nc.tensor.matmul(acc[7][:, 0:TC], g.headsum[:], ex[0][:, ctx], start=True, stop=True).then_inc(sums_done, 1)
            pe.wait_ge(bonus_in, 1)
            nc.tensor.matmul(acc[0][:], g.headsum[:], ex[1][:, 0:T], start=True, stop=True).then_inc(sums_done, 1)

        @block.scalar
        def _(act):
            lat, ctx = slice(TC, TA), slice(0, TC)
            act.wait_ge(low_done, 1)
            for d in range(2):
                nc.scalar.activation(sg[d][:, lat], acc[4 + 2 * d][:], ACT.Sigmoid, bias=col("w0", 4 * d + hp))
                nc.scalar.activation(sg[d][:, ctx], acc[5 + 2 * d][:, 0:TC], ACT.Sigmoid,
                                     bias=col("w0", 4 * d + hp)).then_inc(sig_done, 1)
            act.wait_ge(low_done, 2)
            nc.scalar.activation(ic[:, lat], acc[4][:], ACT.Sigmoid, bias=col("a0"))
            nc.scalar.activation(ic[:, ctx], acc[5][:, 0:TC], ACT.Sigmoid, bias=col("a0")).then_inc(sig_done, 1)
            act.wait_ge(eps_done, 1)
            nc.scalar.activation(ex[0], ex[0], ACT.Sqrt).then_inc(root_done, 1)
            for d in range(2):
                act.wait_ge(exps_in, d + 1)
                for i, s in enumerate((-DECAY, DECAY, -DECAY, -DECAY)):
                    nc.scalar.activation(ex[i], ex[i], ACT.Exp, scale=s)
                end, mid = (P - 1, P // 2 - 1) if d == 0 else (0, P // 2)
                nc.scalar.activation(f.pc[:, d, :].unsqueeze(2), blocks(cs[d][:])[:, :, end:end + 1], ACT.Exp, scale=-DECAY)
                nc.scalar.activation(f.pm[:, d, :].unsqueeze(2), blocks(cs[d][:])[:, :, mid:mid + 1], ACT.Exp, scale=-DECAY).then_inc(exps_out, 1)

        @block.vector
        def _(dve):
            lat, ctx = slice(TC, TA), slice(0, TC)
            V = nc.vector
            dve.wait_ge(st.used, p0 + 2)
            conv(nc, dve, step, g, 4 + hp, k, [(acc[1][:], TC, T), (acc[2][:, 0:TC], 0, TC)])
            conv(nc, dve, step, g, hp, r, [(acc[0][:], 0, T)])
            step.link(dve, V.tensor_scalar(kk[:], k[:], col("k_k"), None, ALU.mult))
            V.tensor_tensor(ex[0], kk[:], kk[:], ALU.mult).then_inc(sq_ready, 1)
            conv(nc, dve, step, g, 8 + hp, f.v, [(acc[3][:], TC, T), (acc[2][:, TC:T], 0, TC)])
            dve.wait_ge(sig_done, 3)
            step.link(dve, V.tensor_scalar(km[:], ic[:], 1.0, col("k_a"), ALU.subtract, ALU.mult))
            step.link(dve, V.scalar_tensor_tensor(km[:], km[:], 1.0, k[:], ALU.add, ALU.mult))
            step.link(dve, V.scalar_tensor_tensor(ex[1][:, 0:T], r[:], col("r_k"), km[:, lat], ALU.mult, ALU.mult))
            V.memset(ex[2][:, 0:1], 0.0).then_inc(bonus_in, 1)
            dve.wait_ge(sums_done, 1)
            V.tensor_copy(ex[0][:, lat], acc[6][:])
            V.tensor_copy(ex[0][:, ctx], acc[7][:, 0:TC]).then_inc(eps_done, 1)
            dve.wait_ge(root_done, 1)
            step.link(dve, V.tensor_scalar(ex[0], ex[0], 1e-12, None, ALU.max))
            step.link(dve, V.reciprocal(ex[0], ex[0]))
            step.link(dve, V.tensor_tensor(kk[:], kk[:], ex[0], ALU.mult))
            step.link(dve, V.scalar_tensor_tensor(bn[:], kk[:], -1.0, ic[:], ALU.mult, ALU.mult))
            dve.wait_ge(sums_done, 2)
            step.link(dve, V.tensor_tensor(f.bonus[:], acc[0][:], f.v[:, lat], ALU.mult))
            for d in range(2):
                o = slice(None, None, 1 if d == 0 else -1)
                end, mid = (P - 1, P // 2 - 1) if d == 0 else (0, P // 2)
                step.link(dve, V.tensor_tensor_scan(cs[d][:, o], restart[:, d, o], sg[d][:, o], 0.0, ALU.mult, ALU.add))
                b3 = blocks(cs[d][:])
                at = lambda c: b3[:, :, c:c + 1].to_broadcast([P, NB, P])
                step.mark(V.tensor_tensor(blocks(ex[0]), b3, at(mid), ALU.subtract))
                step.mark(V.tensor_tensor(blocks(ex[3]), at(end), b3, ALU.subtract))
                step.settle(dve)
                step.mark(V.tensor_copy(ex[1], ex[0]))
                V.tensor_tensor(ex[2], ex[0], sg[d][:], ALU.subtract).then_inc(exps_in, 1)
                dve.wait_ge(exps_out, d + 1)
                step.mark(V.tensor_tensor(f.R[:, d], r[:], ex[0][:, lat], ALU.mult))
                step.mark(V.tensor_tensor(f.A[:, d], kk[:], ex[2], ALU.mult))
                step.mark(V.tensor_tensor(f.Bh[:, d], bn[:], ex[1], ALU.mult))
                step.mark(V.tensor_tensor(f.Kh[:, d], km[:], ex[1], ALU.mult))
                step.mark(V.tensor_tensor(f.Bb[:, d], bn[:], ex[3], ALU.mult))
                step.mark(V.tensor_tensor(f.Kb[:, d], km[:], ex[3], ALU.mult))
                step.settle(dve)


def rwkv_scan(nc, g, hp, f, tri):
    sem = g.sem
    nm = f"rws{hp}_"
    LV = 6
    pe_done = [sem(nm + f"pe_jobs{x}") for x in range(2)]
    dve_done = [sem(nm + f"dve_jobs{x}") for x in range(2)]
    act_done = [sem(nm + f"act_jobs{x}") for x in range(2)]
    pool_done = [sem(nm + f"masks{x}") for x in range(2)]
    step = Tally(sem(nm + "steps"))
    back = [1, 0, 5, 4, 3, 2]
    levels = [j for lv in range(1, LV + 1) for j in ([f"T{lv}", f"M{lv}", f"N{lv}"] if lv < LV else [f"T{lv}", f"N{lv}"])]
    pe_jobs = {lat: ["SA", "TA", "TK"] + ["SR"] * lat + ["M0", "AKV"] + levels + ["X", "GR"] + ["Y"] * lat + ["S"]
               for lat in (False, True)}
    dve_jobs = {lat: ["SA", "MT", "TA", "TK"] + ["SR"] * lat + ["M0", "AKV"]
                + [j for j in levels if j[0] != "T"] + ["GR", "S"] for lat in (False, True)}
    act_jobs = {lat: [f"T{lv}" for lv in range(1, LV + 1)] + ["X"] + ["Y"] * lat for lat in (False, True)}

    def upto(jobs, n, name):
        return sum(len(jobs[m >= NTC]) for m in range(n % 2, n, 2)) + jobs[n >= NTC].index(name) + 1

    with ExitStack() as tmp, nc.Block() as block:
        two = lambda n, shape: [tmp.enter_context(nc.sbuf_tensor(f"{nm}{n}{x}", [P] + shape, F32)) for x in range(2)]
        AT, AK, RB, RK, M, MT, T1 = (two(n, [4, P]) for n in ("AT", "AK", "RB", "RK", "M", "MT", "T1"))
        ET = [two(f"ET{i}", [4, P]) for i in range(2)]
        W = two("W", [4, P])
        X = AT
        Bt, Kt, Vt = (two(n, [4, HD]) for n in ("Bt", "Kt", "Vt"))
        GT = [m[:, 0].rearrange("p (d k) -> p d k", d=2) for m in M]
        Rp = [m[:, 1:3] for m in M]
        S = tmp.enter_context(nc.sbuf_tensor(nm + "S", [P, 2, HD], F32))
        Sc = tmp.enter_context(nc.sbuf_tensor(nm + "Sc", [P, 2, HD], F32))
        bank = [[tmp.enter_context(nc.psum_tensor(f"{nm}q{x}{i}", [P, 512], F32)) for i in range(4)] for x in range(2)]
        four = lambda b: b[:].rearrange("p (c t) -> p c t", c=4)
        as4 = lambda b: b[:].rearrange("p (d h) t -> p d h t", d=2)
        mask = lambda i: tri[:, i].unsqueeze(2).to_broadcast([P, 2, 2, P])
        tok = lambda n, d: slice(P * (n if d == 0 else back[n]), P * (n if d == 0 else back[n]) + P)
        ltok = lambda n, d: slice(tok(n, d).start - TC, tok(n, d).stop - TC)
        head = lambda h: slice(HD * h, HD * (h + 1))
        chains = [(2 * d + h, d, h) for d in range(2) for h in range(2)]

        @block.tensor
        def _(pe):
            mm = nc.tensor.matmul

            def run(name, n):
                x, lat = n % 2, n >= NTC
                q = bank[x]
                need_dve = lambda job, m=n: pe.wait_ge(dve_done[x], upto(dve_jobs, m, job))
                need_act = lambda job, m=n: pe.wait_ge(act_done[x], upto(act_jobs, m, job))
                if name in ("SA", "SR"):
                    if name == "SR":
                        need_dve("SA")
                    elif n >= 2:
                        need_dve("S", n - 2)
                    for c, d, h in chains:
                        rhs = f.A[head(h), d, tok(n, d)] if name == "SA" else f.R[head(h), d, ltok(n, d)]
                        for i, lhs in enumerate((f.Bh, f.Kh)):
                            last = mm(four(q[h])[:, 2 * i + d], lhs[head(h), d, tok(n, d)], rhs, start=True, stop=True)
                elif name == "TA":
                    if n >= 2:
                        need_dve("N6", n - 2)
                        if n - 2 >= NTC:
                            need_act("Y", n - 2)
                    for i, src in enumerate((f.A, f.Bb)):
                        for d in range(2):
                            last = nc.tensor.transpose(four(q[2])[:, 2 * i + d], src[:, d, tok(n, d)], g.ident[:])
                elif name == "TK":
                    if n >= 2:
                        need_act("X", n - 2)
                    for d in range(2):
                        nc.tensor.transpose(four(q[3])[:, d], f.Kb[:, d, tok(n, d)], g.ident[:])
                        last = nc.tensor.transpose(four(q[3])[:, 2 + d], f.v[:, tok(n, d)], g.ident[:])
                elif name == "M0":
                    need_dve("TA")
                    for c, d, h in chains:
                        last = nc.tensor.transpose(four(q[2])[:, c], MT[x][:, c], g.ident[:])
                elif name == "AKV":
                    need_dve("TK")
                    for c, d, h in chains:
                        last = mm(q[3][:, c * HD:(c + 1) * HD], AK[x][:, c], Vt[x][:, c], start=True, stop=True)
                elif name[0] == "T":
                    lv = int(name[1])
                    pe.wait_ge(pool_done[x], LV * (n // 2) + lv)
                    need_dve(f"M{lv - 1}")
                    if lv == 1:
                        need_dve("SR" if lat else "SA")
                    else:
                        need_act(f"T{lv - 1}")
                    for c, d, h in chains:
                        last = mm(four(q[0])[:, c], ET[lv % 2][x][:, c], M[x][:, c], start=True, stop=True)
                elif name[0] == "M":
                    lv = int(name[1])
                    need_act(f"T{lv}")
                    if lv == 1:
                        need_dve("SR" if lat else "SA")
                    else:
                        need_dve(f"N{lv - 1}")
                    for c, d, h in chains:
                        last = mm(four(q[1])[:, c], MT[x][:, c], T1[x][:, c], start=True, stop=True)
                elif name[0] == "N":
                    lv = int(name[1])
                    need_act(f"T{lv}")
                    need_dve("M0" if lv == 1 else f"N{lv - 1}")
                    for c, d, h in chains:
                        last = mm(four(q[2])[:, c], T1[x][:, c], MT[x][:, c], start=True, stop=True)
                elif name == "X":
                    need_dve("N6")
                    for c, d, h in chains:
                        last = mm(four(q[3])[:, c], MT[x][:, c], W[x][:, c], start=True, stop=True)
                elif name == "GR":
                    need_act("X")
                    for c, d, h in chains:
                        last = mm(q[0][head(h), d * HD:(d + 1) * HD], X[x][:, c, 0:HD], Bt[x][:, c], start=True, stop=True)
                        if lat:
                            last = mm(q[0][head(h), P + d * P:P + (d + 1) * P], X[x][:, c, 0:HD], RB[x][:, c], start=True, stop=True)
                elif name == "Y":
                    need_dve("GR")
                    pe.wait_ge(dve_done[1 - x], upto(dve_jobs, n - 1, "S"))
                    for c, d, h in chains:
                        dst = q[2][head(h), d * P:(d + 1) * P]
                        mm(dst, Sc[head(h), d], Rp[x][head(h), d], start=True, stop=False)
                        mm(dst, X[x][:, c, HD:P], RB[x][:, c], start=False, stop=False)
                        last = mm(dst, Vt[x][:, c], RK[x][:, c], start=False, stop=True)
                elif name == "S":
                    need_dve("GR")
                    if n:
                        pe.wait_ge(dve_done[1 - x], upto(dve_jobs, n - 1, "S"))
                    else:
                        pe.wait_ge(step.sem, 2)
                    for c, d, h in chains:
                        dst = q[1][head(h), d * HD:(d + 1) * HD]
                        mm(dst, Bt[x][:, c], X[x][:, c, HD:P], start=True, stop=False)
                        mm(dst, Kt[x][:, c], Vt[x][:, c], start=False, stop=False)
                        last = mm(dst, GT[x][head(h), d], Sc[head(h), d], start=False, stop=True)
                last.then_inc(pe_done[x], 1)

            for n in range(0, TA // P, 2):
                jobs = pe_jobs[n >= NTC]
                tail = jobs.index("GR") + 1
                for job in jobs[:tail]:
                    run(job, n)
                    run(job, n + 1)
                for m in (n, n + 1):
                    for job in jobs[tail:]:
                        run(job, m)

        @block.vector
        def _(dve):
            V = nc.vector
            step.mark(V.memset(S[:], 0.0))
            step.mark(V.memset(Sc[:], 0.0))

            def run(name, n):
                x, lat = n % 2, n >= NTC
                q = bank[x]
                own = lambda job: dve.wait_ge(dve_done[x], upto(dve_jobs, n, job))
                if name == "MT":
                    own("SA")
                    step.link(dve, V.tensor_tensor(as4(MT[x]), as4(AT[x]), mask(2), ALU.mult))
                    last = V.tensor_tensor(MT[x][:], MT[x][:], g.ident[:].unsqueeze(1).to_broadcast([P, 4, P]), ALU.add)
                    last.then_inc(dve_done[x], 1)
                    return
                dve.wait_ge(pe_done[x], upto(pe_jobs, n, name))
                if name in ("SA", "SR"):
                    for i, dst in enumerate((AT, AK) if name == "SA" else (RB, RK)):
                        for h in range(2):
                            last = V.tensor_tensor(as4(dst[x])[:, :, h], four(q[h])[:, 2 * i:2 * i + 2], tri[:, 0 if name == "SA" else 1], ALU.mult)
                elif name == "TA":
                    V.tensor_copy(W[x][:, :, 0:HD], q[2][:, 0:2 * P].rearrange("p (c k) -> p c k", k=HD))
                    last = V.tensor_copy(Bt[x][:], q[2][:, 2 * P:].rearrange("p (c k) -> p c k", k=HD))
                elif name == "TK":
                    V.tensor_copy(Kt[x][:], q[3][:, 0:2 * P].rearrange("p (c k) -> p c k", k=HD))
                    last = V.tensor_copy(Vt[x][:], q[3][:, 2 * P:].rearrange("p (c k) -> p c k", k=HD))
                elif name == "M0":
                    last = V.tensor_copy(M[x][:], four(q[2]))
                elif name == "AKV":
                    last = V.tensor_copy(W[x][:, :, HD:P], q[3][:, 0:2 * P].rearrange("p (c k) -> p c k", k=HD))
                elif name[0] in "MN":
                    lv = int(name[1])
                    buf = M if name[0] == "M" else MT
                    own(f"M{lv - 1}" if name[0] == "M" else ("MT" if lv == 1 else f"N{lv - 1}"))
                    last = V.tensor_tensor(buf[x][:], buf[x][:], four(q[1 if name[0] == "M" else 2]), ALU.add)
                elif name == "GR":
                    last = V.tensor_copy(GT[x], q[0][:, 0:2 * HD].rearrange("p (d k) -> p d k", d=2))
                    if lat:
                        for d in range(2):
                            last = V.tensor_tensor(Rp[x][:, d], q[0][:, P + d * P:P + (d + 1) * P], f.R[:, d, ltok(n, d)], ALU.add)
                elif name == "S":
                    if n:
                        dve.wait_ge(dve_done[1 - x], upto(dve_jobs, n - 1, "S"))
                    else:
                        step.settle(dve)
                    for d in range(2):
                        b = tok(n, d).start // P
                        step.mark(V.scalar_tensor_tensor(S[:, d], S[:, d], f.pc[:, d, b:b + 1], q[1][:, d * HD:(d + 1) * HD],
                                                         ALU.mult, ALU.add))
                    step.settle(dve)
                    for d in range(2):
                        m = min(n + 1, TA // P - 1)
                        b = tok(m, d).start // P
                        last = V.tensor_scalar(Sc[:, d], S[:, d], f.pm[:, d, b:b + 1], None, ALU.mult)
                last.then_inc(dve_done[x], 1)

            for n in range(0, TA // P, 2):
                for job in dve_jobs[n >= NTC]:
                    run(job, n)
                    run(job, n + 1)

        @block.scalar
        def _(act):
            def run(name, n):
                x = n % 2
                act.wait_ge(pe_done[x], upto(pe_jobs, n, name))
                if name == "X":
                    last = nc.scalar.copy(X[x][:], four(bank[x][3]))
                elif name == "Y":
                    for d in range(2):
                        last = nc.scalar.copy(f.Y[:, d, ltok(n, d)], bank[x][2][:, d * P:(d + 1) * P])
                else:
                    last = nc.scalar.copy(T1[x][:], four(bank[x][0]))
                last.then_inc(act_done[x], 1)

            for n in range(0, TA // P, 2):
                for job in act_jobs[n >= NTC]:
                    run(job, n)
                    run(job, n + 1)

        @block.gpsimd
        def _(pool):
            for n in range(0, TA // P, 2):
                for lv in range(1, LV + 1):
                    for m in (n, n + 1):
                        x = m % 2
                        if lv == 1:
                            pool.wait_ge(dve_done[x], upto(dve_jobs, m, "SA"))
                        if lv >= 3:
                            pool.wait_ge(pe_done[x], upto(pe_jobs, m, f"T{lv - 2}"))
                        nc.gpsimd.tensor_tensor(as4(ET[lv % 2][x]), as4(AT[x]), mask(2 + lv), ALU.mult).then_inc(pool_done[x], 1)


def rwkv_out(nc, g, hp, f, low, par, latT):
    sem = g.sem
    nm = f"rwo{hp}_"
    sums = sem(nm + "sums")
    centred = sem(nm + "centred")
    squared = sem(nm + "squared")
    vared = sem(nm + "var_ready")
    rooted = sem(nm + "rooted")
    step = Tally(sem(nm + "steps"))
    col = lambda name: g.cols[:, g.col[name] + hp:g.col[name] + hp + 1]
    with ExitStack() as tmp, nc.Block() as block:
        yc = tmp.enter_context(nc.sbuf_tensor(nm + "yc", [P, 2, T], F32))
        sq = tmp.enter_context(nc.sbuf_tensor(nm + "sq", [P, 2, T], F32))
        rt = tmp.enter_context(nc.sbuf_tensor(nm + "rt", [P, 2, T], F32))
        g2 = tmp.enter_context(nc.sbuf_tensor(nm + "g2", [P, 2, P], F32))
        g2_loaded = sem(nm + "g2_loaded")
        acc = [tmp.enter_context(nc.psum_tensor(f"{nm}p{i}", [P, T], F32)) for i in range(6)]

        @block.sync
        def _(sp):
            sp.dma_start(g2[:], par.g2_rows[:, :, hp * P:(hp + 1) * P]).then_inc(g2_loaded, 16)

        @block.tensor
        def _(pe):
            for d in range(2):
                nc.tensor.matmul(acc[d][:], g.headsum[:], f.Y[:, d], start=True, stop=True).then_inc(sums, 1)
            pe.wait_ge(g2_loaded, 16)
            for d in range(2):
                last = nc.tensor.matmul(acc[4 + d][:], g2[:, d], low.gl[:, d], start=True, stop=True)
                last.then_inc(sums, 1)
            for d in range(2):
                pe.wait_ge(squared, d + 1)
                nc.tensor.matmul(acc[2 + d][:], g.headsum[:], sq[:, d], start=True, stop=True).then_inc(sums, 1)

        @block.scalar
        def _(act):
            for d in range(2):
                act.wait_ge(centred, d + 1)
                nc.scalar.activation(sq[:, d], yc[:, d], ACT.Square).then_inc(squared, 1)
            for d in range(2):
                act.wait_ge(vared, d + 1)
                nc.scalar.activation(rt[:, d], rt[:, d], ACT.Sqrt).then_inc(rooted, 1)

        @block.vector
        def _(dve):
            V = nc.vector
            for d in range(2):
                dve.wait_ge(sums, d + 1)
                V.scalar_tensor_tensor(yc[:, d], acc[d][:], -1.0 / HD, f.Y[:, d], ALU.mult, ALU.add).then_inc(centred, 1)
            for d in range(2):
                dve.wait_ge(sums, 5 + d)
                V.tensor_scalar(rt[:, d], acc[2 + d][:], 1.0 / HD, GN_EPS, ALU.mult, ALU.add).then_inc(vared, 1)
            for d in range(2):
                dve.wait_ge(rooted, d + 1)
                step.link(dve, V.reciprocal(rt[:, d], rt[:, d]))
                step.link(dve, V.tensor_tensor(yc[:, d], yc[:, d], rt[:, d], ALU.mult))
                step.link(dve, V.tensor_scalar(yc[:, d], yc[:, d], col("lnx_w"), col("lnx_b"), ALU.mult, ALU.add))
                step.link(dve, V.tensor_tensor(yc[:, d], yc[:, d], f.bonus[:], ALU.add))
                step.link(dve, V.tensor_tensor(yc[:, d], yc[:, d], acc[4 + d][:], ALU.mult))
            dst = latT[:, 4 + hp, :].rearrange("c (j p) -> c p j", j=NT)
            a, b = (yc[:, d].rearrange("c (p j) -> c p j", j=NT) for d in range(2))
            step.link(dve, V.tensor_tensor(dst, a, b, ALU.add))


def row_vector(nc, g, name, out, col):
    diag_ready = g.sem(name + "_diag_ready")
    spread = g.sem(name + "_spread")
    with ExitStack() as tmp, nc.Block() as block:
        diag = tmp.enter_context(nc.sbuf_tensor(name + "_diag", [P, KD, P], F32))
        acc = tmp.enter_context(nc.psum_tensor(name + "_rows", [P, 2, 512], F32))

        @block.vector
        def _(dve):
            nc.vector.tensor_tensor(diag[:], g.ident[:].unsqueeze(1).to_broadcast([P, KD, P]),
                                    col.unsqueeze(2).to_broadcast([P, KD, P]), ALU.mult).then_inc(diag_ready, 1)
            dve.wait_ge(spread, 1)
            nc.vector.tensor_copy(out[:], acc[:].rearrange("p a b -> p (a b)"))

        @block.tensor
        def _(pe):
            pe.wait_ge(diag_ready, 1)
            for h in range(2):
                last = nc.tensor.matmul(acc[:, h], g.ones[:], diag[:, 4 * h:4 * h + 4].rearrange("p k c -> p (k c)"),
                                        start=True, stop=True)
            last.then_inc(spread, 1)


def project_rows(nc, g, name, xT, write):
    st = g.stream
    p0 = st.taken
    n_panel = D // PW
    emptied = g.sem(name + "_emptied")
    with ExitStack() as tmp, nc.Block() as block:
        acc = [[tmp.enter_context(nc.psum_tensor(f"{name}_o{s}{i}", [P, 2, PW], F32)) for i in range(2)] for s in range(2)]

        @block.sync
        def _(sp):
            st.load_until(sp, p0 + n_panel + SLOTS)

        @block.tensor
        def _(pe):
            for n in range(n_panel):
                w = st.take(pe)
                if n >= 2:
                    pe.wait_ge(emptied, n - 1)
                for j in range(NT):
                    for k in range(KD):
                        last = nc.tensor.matmul(acc[n % 2][j // 2][:, j % 2], xT[:, k, j * P:(j + 1) * P], w[:, k, :],
                                                start=(k == 0), stop=(k == KD - 1))
                last.then_inc(st.used, 1)

        @block.vector
        def _(dve):
            for n in range(n_panel):
                dve.wait_ge(st.used, p0 + n + 1)
                for i in range(2):
                    last = write(slice(2 * i, 2 * i + 2), slice(n * PW, (n + 1) * PW), acc[n % 2][i][:])
                last.then_inc(emptied, 1)


def post_norm(nc, g, name, y, row, x):
    squares = g.sem(name + "_squares")
    meaned = g.sem(name + "_mean_ready")
    rooted = g.sem(name + "_root_ready")
    step = Tally(g.sem(name + "_steps"))
    with ExitStack() as tmp, nc.Block() as block:
        junk = tmp.enter_context(nc.sbuf_tensor(name + "_sq", [P, NT, D], F32))
        ms = tmp.enter_context(nc.sbuf_tensor(name + "_ms", [P, NT], F32))
        rt = tmp.enter_context(nc.sbuf_tensor(name + "_rt", [P, NT], F32))
        rs = tmp.enter_context(nc.sbuf_tensor(name + "_rs", [P, NT], F32))

        @block.scalar
        def _(act):
            for j in range(NT):
                nc.scalar.activation(junk[:, j], y[:, j], ACT.Square, accum_out=ms[:, j:j + 1]).then_inc(squares, 1)
            act.wait_ge(meaned, 1)
            nc.scalar.activation(rt[:], ms[:], ACT.Sqrt).then_inc(rooted, 1)

        @block.vector
        def _(dve):
            dve.wait_ge(squares, NT)
            nc.vector.tensor_scalar(ms[:], ms[:], 1.0 / D, EPS, ALU.mult, ALU.add).then_inc(meaned, 1)
            dve.wait_ge(rooted, 1)
            step.link(dve, nc.vector.reciprocal(rs[:], rt[:]))
            for j in range(NT):
                step.mark(nc.vector.scalar_tensor_tensor(y[:, j], y[:, j], rs[:, j:j + 1], row[:], ALU.mult, ALU.mult))
            step.settle(dve)
            for j in range(NT):
                nc.vector.tensor_tensor(x[:, j], x[:, j], y[:, j], ALU.add)


def router(nc, g, h2T, w_r, pick, tokrow, tokcol, xsT, selT):
    sem = g.sem
    logits_ready = sem("router_logits_ready")
    maxed = sem("router_max_ready")
    exps_ready = sem("router_exps_ready")
    aff_ready = sem("router_affinities_ready")
    aff_turned = sem("router_affinities_turned")
    picked = sem("router_picked")
    spread = sem("router_spread")
    cols_turned = sem("router_columns_turned")
    sel_ready = sem("router_sel_ready")
    tok_turned = sem("router_tokens_turned")
    tok_ready = sem("router_tokens_ready")
    gathered = sem("router_gathered")
    stored = sem("router_gather_stored")
    step = Tally(sem("router_steps"))
    rounds = CAP // 8
    with ExitStack() as tmp, nc.Block() as block:
        sb = lambda n, s, dt=F32: tmp.enter_context(nc.sbuf_tensor("router_" + n, s, dt))
        h2 = sb("h2", [P, NT, D])
        sel = sb("sel", [P, NT, E_N * CAP])
        aff = sb("aff", [P, NT, E_N])
        red = sb("red", [P, 2, NT])
        affT = sb("affT", [E_N, 2, T])
        val = sb("val", [E_N, 2, CAP])
        idx = sb("idx", [E_N, CAP], U32)
        idxf = sb("idxf", [E_N, 2, CAP])
        cols = sb("cols", [P, 2, E_N // 2])
        bank = [tmp.enter_context(nc.psum_tensor(f"router_b{i}", [P, 512], F32)) for i in range(8)]
        logit, turn, both = bank[0], bank[1], bank[2:4]
        half = lambda b: b[:, 0:NT * E_N].rearrange("p (j e) -> p j e", j=NT)

        @block.tensor
        def _(pe):
            for j in range(NT):
                for k in range(KD):
                    last = nc.tensor.matmul(half(logit)[:, j], h2T[:, k, j * P:(j + 1) * P], w_r[:, k, :],
                                            start=(k == 0), stop=(k == KD - 1))
            last.then_inc(logits_ready, 1)
            for i in range(2 * NT):
                j, c = i // 2, i % 2
                if i >= 4:
                    pe.wait_ge(tok_ready, i - 3)
                for k in range(4):
                    src = h2T[:, 4 * c + k, :].rearrange("c (p j) -> c j p", j=NT)[:, j]
                    last = nc.tensor.transpose(bank[4 + i % 4][:, k * P:(k + 1) * P], src, g.ident[:])
                last.then_inc(tok_turned, 1)
            pe.wait_ge(aff_ready, 1)
            for j in range(NT):
                last = nc.tensor.transpose(turn[0:E_N, j * P:(j + 1) * P], aff[:, j, :], g.ident[:])
            last.then_inc(aff_turned, 1)
            pe.wait_ge(picked, 1)
            for e in range(E_N):
                last = nc.tensor.matmul(both[e // 8][:, (e % 8) * CAP:(e % 8 + 1) * CAP], pick[:, e, :], idxf[:, 0, :],
                                        start=True, stop=True)
            last.then_inc(spread, 1)
            nc.tensor.transpose(logit[:, 0:E_N], idxf[:].rearrange("e a c -> e (a c)"), g.ident[0:E_N, 0:E_N])
            nc.tensor.transpose(logit[:, E_N:2 * E_N], val[:].rearrange("e a c -> e (a c)"), g.ident[0:E_N, 0:E_N]).then_inc(cols_turned, 1)
            pe.wait_ge(sel_ready, NT)
            pe.wait_ge(tok_ready, 2 * NT)
            for k in range(KD):
                for h in range(2):
                    n = 2 * k + h
                    if n >= 4:
                        pe.wait_ge(stored, n - 3)
                    for j in range(NT):
                        last = nc.tensor.matmul(bank[4 + n % 4][:], h2[:, j, k * P:(k + 1) * P], sel[:, j, h * 512:(h + 1) * 512],
                                                start=(j == 0), stop=(j == NT - 1))
                    last.then_inc(gathered, 1)

        @block.scalar
        def _(act):
            act.wait_ge(maxed, 1)
            nc.scalar.activation(aff[:], aff[:], ACT.Exp).then_inc(exps_ready, 1)
            for i in range(2 * NT):
                act.wait_ge(tok_turned, i + 1)
                nc.scalar.copy(h2[:, i // 2, (i % 2) * 512:(i % 2 + 1) * 512], bank[4 + i % 4][:]).then_inc(tok_ready, 1)
            for n in range(2 * KD):
                act.wait_ge(gathered, n + 1)
                nc.scalar.copy(xsT[:, n // 2, (n % 2) * 512:(n % 2 + 1) * 512], bank[4 + n % 4][:]).then_inc(stored, 1)

        @block.vector
        def _(dve):
            V = nc.vector
            spread_out = lambda x: x.unsqueeze(2).to_broadcast([P, NT, E_N])
            dve.wait_ge(logits_ready, 1)
            step.link(dve, V.tensor_reduce(red[:, 0], half(logit), AX, ALU.max))
            V.tensor_tensor(aff[:], half(logit), spread_out(red[:, 0]), ALU.subtract).then_inc(maxed, 1)
            dve.wait_ge(exps_ready, 1)
            step.link(dve, V.tensor_reduce(red[:, 1], aff[:], AX, ALU.add))
            step.link(dve, V.reciprocal(red[:, 1], red[:, 1]))
            V.tensor_tensor(aff[:], aff[:], spread_out(red[:, 1]), ALU.mult).then_inc(aff_ready, 1)
            dve.wait_ge(aff_turned, 1)
            step.link(dve, V.tensor_copy(affT[:, 0], turn[0:E_N, :]))
            for r in range(rounds):
                now, then = affT[:, r % 2], affT[:, (r + 1) % 2]
                c = slice(8 * r, 8 * r + 8)
                step.link(dve, V.max(val[:, 0, c], now))
                step.mark(V.max_index(idx[:, c], val[:, 0, c], now))
                if r + 1 < rounds:
                    step.mark(V.match_replace(then, val[:, 0, c], now, -1.0))
                step.settle(dve)
            step.mark(V.tensor_copy(idxf[:, 0], idx[:]))
            step.mark(V.tensor_copy(idxf[:, 1], idx[:]))
            step.settle(dve)
            V.tensor_copy(val[:, 1], val[:, 0]).then_inc(picked, 1)
            dve.wait_ge(spread, 1)
            for j in range(NT):
                for h in range(2):
                    last = V.tensor_scalar(sel[:, j, h * 512:(h + 1) * 512], both[h][:], tokcol[:, j:j + 1], None, ALU.is_equal)
                last.then_inc(sel_ready, 1)
            dve.wait_ge(cols_turned, 1)
            for i in range(2):
                src = logit[:, i * E_N:(i + 1) * E_N].rearrange("p (a b) -> p a b", b=2)
                for h in range(2):
                    step.mark(V.tensor_copy(cols[h * CAP:(h + 1) * CAP, i], src[h * CAP:(h + 1) * CAP, :, h]))
            step.settle(dve)
            for m in range(E_N // 2):
                V.tensor_scalar(selT[:, m], tokrow[:], cols[:, 0, m:m + 1], cols[:, 1, m:m + 1], ALU.is_equal, ALU.mult)


def experts(nc, g, xsT, ye):
    sem, st = g.sem, g.stream
    p0 = st.taken
    NP = D // PW
    per = 3 * NP
    copied = sem("moe_gate_up_copied")
    turned = sem("moe_gate_up_turned")
    silued = sem("moe_silu_ready")
    hidden = sem("moe_hidden_ready")
    stored = sem("moe_down_stored")
    with ExitStack() as tmp, nc.Block() as block:
        gu = tmp.enter_context(nc.sbuf_tensor("moe_gu", [P, 2, PW], F32))
        silu = tmp.enter_context(nc.sbuf_tensor("moe_silu", [P, 2, 2, CAP], F32))
        hid = tmp.enter_context(nc.sbuf_tensor("moe_hid", [P, 2, KD, CAP], F32))
        acc = [tmp.enter_context(nc.psum_tensor(f"moe_gu{i}", [P, 512], F32)) for i in range(2)]
        turn = [tmp.enter_context(nc.psum_tensor(f"moe_t{i}", [P, 512], F32)) for i in range(2)]
        down = [tmp.enter_context(nc.psum_tensor(f"moe_d{i}", [P, 512], F32)) for i in range(2)]
        chunk = lambda b: b[:, 0:2 * P].rearrange("p (f t) -> p f t", f=2)
        done = lambda e, n: p0 + per * e + n

        @block.sync
        def _(sp):
            st.load_until(sp, p0 + E_N * per + SLOTS)

        @block.tensor
        def _(pe):
            def turn_chunk(e, n):
                i = NP * e + n
                pe.wait_ge(copied, i + 1)
                if i >= 2:
                    pe.wait_ge(hidden, i - 1)
                for f in range(2):
                    last = nc.tensor.transpose(chunk(turn[i % 2])[:, f], gu[:, i % 2, f * P:(f + 1) * P], g.ident[:])
                last.then_inc(turned, 1)

            for e in range(E_N):
                tokens = slice(e * CAP, (e + 1) * CAP)
                for n in range(NP):
                    i = NP * e + n
                    wg = st.take(pe)
                    wu = st.take(pe)
                    if i >= 2:
                        pe.wait_ge(copied, i - 1)
                    for k in range(KD):
                        a = nc.tensor.matmul(acc[i % 2][0:CAP, 0:PW], xsT[:, k, tokens], wg[:, k, :], start=(k == 0), stop=(k == KD - 1))
                        b = nc.tensor.matmul(acc[i % 2][CAP:P, 0:PW], xsT[:, k, tokens], wu[:, k, :], start=(k == 0), stop=(k == KD - 1))
                    a.then_inc(st.used, 1)
                    b.then_inc(st.used, 1)
                    if n >= 1:
                        turn_chunk(e, n - 1)
                turn_chunk(e, NP - 1)
                pe.wait_ge(hidden, NP * (e + 1))
                rows = slice((e % 2) * CAP, (e % 2 + 1) * CAP)
                for n in range(NP):
                    i = NP * e + n
                    w = st.take(pe)
                    if i >= 2:
                        pe.wait_ge(stored, i - 1)
                    for k in range(KD):
                        last = nc.tensor.matmul(down[i % 2][rows, 0:PW], hid[:, e % 2, k, :], w[:, k, :], start=(k == 0), stop=(k == KD - 1))
                    last.then_inc(st.used, 1)

        @block.scalar
        def _(act):
            def silu_chunk(i):
                act.wait_ge(turned, i + 1)
                if i >= 2:
                    act.wait_ge(hidden, i - 1)
                nc.scalar.activation(silu[:, i % 2], chunk(turn[i % 2])[:, :, 0:CAP], ACT.Silu).then_inc(silued, 1)

            for e in range(E_N):
                for n in range(NP):
                    i = NP * e + n
                    act.wait_ge(st.used, done(e, 2 * n + 2))
                    if i >= 2:
                        act.wait_ge(turned, i - 1)
                    nc.scalar.copy(gu[:, i % 2, :], acc[i % 2][:, 0:PW]).then_inc(copied, 1)
                    if n >= 1:
                        silu_chunk(i - 1)
                silu_chunk(NP * (e + 1) - 1)

        @block.vector
        def _(dve):
            for e in range(E_N):
                for n in range(NP):
                    i = NP * e + n
                    dve.wait_ge(silued, i + 1)
                    if e >= 2 and n == 0:
                        dve.wait_ge(st.used, done(e - 2, per))
                    nc.vector.tensor_tensor(hid[:, e % 2, 2 * n:2 * n + 2, :], silu[:, i % 2], chunk(turn[i % 2])[:, :, CAP:P], ALU.mult).then_inc(hidden, 1)
                rows = slice((e % 2) * CAP, (e % 2 + 1) * CAP)
                for n in range(NP):
                    dve.wait_ge(st.used, done(e, 2 * NP + n + 1))
                    nc.vector.tensor_copy(ye[rows, e // 2, n * PW:(n + 1) * PW], down[(NP * e + n) % 2][rows, 0:PW]).then_inc(stored, 1)


def scatter(nc, g, ye, selT, moe):
    summed = g.sem("moe_summed")
    stored = g.sem("moe_sum_stored")
    with ExitStack() as tmp, nc.Block() as block:
        acc = [tmp.enter_context(nc.psum_tensor(f"moe_s{i}", [P, 512], F32)) for i in range(4)]

        @block.tensor
        def _(pe):
            for n in range(2 * NT):
                j, h = n // 2, n % 2
                if n >= 4:
                    pe.wait_ge(stored, n - 3)
                for m in range(E_N // 2):
                    last = nc.tensor.matmul(acc[n % 4][:], selT[:, m, j * P:(j + 1) * P], ye[:, m, h * 512:(h + 1) * 512],
                                            start=(m == 0), stop=(m == E_N // 2 - 1))
                last.then_inc(summed, 1)

        @block.vector
        def _(dve):
            for n in range(2 * NT):
                dve.wait_ge(summed, n + 1)
                nc.vector.tensor_copy(moe[:, n // 2, (n % 2) * 512:(n % 2 + 1) * 512], acc[n % 4][:]).then_inc(stored, 1)


GH = 8
HALF = GH * HD


def gain_rows(nc, g, a, out):
    loaded = g.sem("a_gains_loaded")
    cleared = g.sem("a_gains_cleared")
    spread = g.sem("a_gains_spread")
    with ExitStack() as tmp, nc.Block() as block:
        row = tmp.enter_context(nc.sbuf_tensor("a_gain_row", [P, 6 * HD], F32))
        acc = tmp.enter_context(nc.psum_tensor("a_gain_acc", [P, 6 * HD], F32))

        @block.gpsimd
        def _(pool):
            nc.gpsimd.memset(row[:], 0.0).then_inc(cleared, 1)

        @block.sync
        def _(sp):
            sp.wait_ge(cleared, 1)
            for i, name in enumerate(("a_q_gain_2", "a_k_gain_2")):
                sp.dma_start(row[0:1, i * 3 * HD:(i + 1) * 3 * HD], a[name].rearrange("(o n) -> o n", o=1)).then_inc(loaded, 16)

        @block.tensor
        def _(pe):
            pe.wait_ge(loaded, 32)
            nc.tensor.matmul(acc[:], g.ones[:], row[:], start=True, stop=True).then_inc(spread, 1)

        @block.vector
        def _(dve):
            dve.wait_ge(spread, 1)
            nc.vector.tensor_scalar(out[:, 0:3].rearrange("p g d -> p (g d)"), acc[:, 0:3 * HD], HD ** -0.5, None, ALU.mult)
            nc.vector.tensor_copy(out[:, 3:6].rearrange("p g d -> p (g d)"), acc[:, 3 * HD:])


def dilated_inputs(nc, g, nm, grp, yT, v, qT, kT, gains, rope):
    sem, st = g.sem, g.stream
    p0 = st.taken
    emptied = sem(nm + "_emptied")
    meaned = sem(nm + "_mean_ready")
    rooted = sem(nm + "_root_ready")
    normed = sem(nm + "_normed")
    turned = sem(nm + "_turned")
    written = sem(nm + "_written")
    step = Tally(sem(nm + "_steps"))
    with ExitStack() as tmp, nc.Block() as block:
        q = tmp.enter_context(nc.sbuf_tensor(nm + "_q", [P, NT, HALF], F32))
        k = tmp.enter_context(nc.sbuf_tensor(nm + "_k", [P, NT, HALF], F32))
        sq = tmp.enter_context(nc.sbuf_tensor(nm + "_sq", [P, NT, HALF], F32))
        ms = tmp.enter_context(nc.sbuf_tensor(nm + "_ms", [P, 2, NT, GH], F32))
        rt = tmp.enter_context(nc.sbuf_tensor(nm + "_rt", [P, 2, NT, GH], F32))
        prod = [tmp.enter_context(nc.sbuf_tensor(f"{nm}_rope{i}", [P, NT, GH, 8], F32)) for i in range(4)]
        acc = [[tmp.enter_context(nc.psum_tensor(f"{nm}_o{s}{i}", [P, 2, PW], F32)) for i in range(2)] for s in range(3)]
        turn = [tmp.enter_context(nc.psum_tensor(f"{nm}_t{i}", [P, NT, P], F32)) for i in range(2)]

        @block.sync
        def _(sp):
            st.load_until(sp, p0 + 6 + SLOTS)

        @block.tensor
        def _(pe):
            for n in range(6):
                w = st.take(pe)
                if n >= 3:
                    pe.wait_ge(emptied, n - 2)
                for j in range(NT):
                    for i in range(KD):
                        last = nc.tensor.matmul(acc[n % 3][j // 2][:, j % 2], yT[:, i, j * P:(j + 1) * P], w[:, i, :],
                                                start=(i == 0), stop=(i == KD - 1))
                last.then_inc(st.used, 1)
            for n in range(8):
                if n % 4 == 0:
                    pe.wait_ge(normed, n // 4 + 1)
                if n >= 2:
                    pe.wait_ge(written, n - 1)
                for j in range(NT):
                    last = nc.tensor.transpose(turn[n % 2][:, j], (q if n < 4 else k)[:, j, (n % 4) * P:(n % 4 + 1) * P], g.ident[:])
                last.then_inc(turned, 1)

        @block.scalar
        def _(act):
            def root(i):
                act.wait_ge(meaned, i + 1)
                nc.scalar.activation(rt[:, i], ms[:, i], ACT.Sqrt).then_inc(rooted, 1)

            for n in range(6):
                act.wait_ge(st.used, p0 + n + 1)
                for i in range(2):
                    last = nc.scalar.copy((q, k, v)[n // 2][:, 2 * i:2 * i + 2, (n % 2) * PW:(n % 2 + 1) * PW], acc[n % 3][i][:])
                last.then_inc(emptied, 1)
                if n in (2, 4):
                    root(n // 2 - 1)
            for n in range(8):
                act.wait_ge(turned, n + 1)
                nc.scalar.copy((qT if n < 4 else kT)[:, n % 4, :], turn[n % 2][:].rearrange("p j t -> p (j t)")).then_inc(written, 1)

        @block.vector
        def _(dve):
            V = nc.vector
            for i, x in enumerate((q, k)):
                heads = x[:].rearrange("p j (h d) -> p j h d", d=HD)
                dve.wait_ge(emptied, 2 * i + 2)
                step.link(dve, V.tensor_tensor(sq[:], x[:], x[:], ALU.mult))
                step.link(dve, V.tensor_reduce(ms[:, i], sq[:].rearrange("p j (h d) -> p j h d", d=HD), AX, ALU.add))
                V.tensor_scalar(ms[:, i], ms[:, i], 1.0 / HD, EPS, ALU.mult, ALU.add).then_inc(meaned, 1)
                dve.wait_ge(rooted, i + 1)
                step.link(dve, V.reciprocal(rt[:, i], rt[:, i]))
                step.link(dve, V.tensor_tensor(heads, heads, rt[:, i].unsqueeze(3).to_broadcast([P, NT, GH, HD]), ALU.mult))
                gain = gains[:, 3 * i + grp].unsqueeze(1).to_broadcast([P, NT * GH, HD])
                flat = x[:].rearrange("p j (h d) -> p (j h) d", d=HD)
                step.link(dve, V.tensor_tensor(flat, flat, gain, ALU.mult))
                x1, x2 = heads[:, :, :, 0:8], heads[:, :, :, 8:16]
                cos, sin = (rope[:, c].unsqueeze(2).to_broadcast([P, NT, GH, 8]) for c in range(2))
                for dst, part, tab in ((prod[0], x1, cos), (prod[1], x2, sin), (prod[2], x2, cos), (prod[3], x1, sin)):
                    step.mark(V.tensor_tensor(dst[:], part, tab, ALU.mult))
                step.settle(dve)
                step.mark(V.tensor_tensor(x1, prod[0][:], prod[1][:], ALU.subtract))
                step.mark(V.tensor_tensor(x2, prod[2][:], prod[3][:], ALU.add))
                step.settle(dve)
                V.tensor_copy(ms[:, i], rt[:, i]).then_inc(normed, 1)


def dilated_attention(nc, g, nm, grp, qT, kT, v, mask, num, mx, den):
    sem = g.sem
    scored = sem(nm + "_scored")
    masked = sem(nm + "_masked")
    maxed = sem(nm + "_max_ready")
    exped = sem(nm + "_exps_ready")
    turned = sem(nm + "_turned")
    copied = sem(nm + "_turned_copied")
    applied = sem(nm + "_applied")
    kept = sem(nm + "_kept")
    step = Tally(sem(nm + "_steps"))
    steps = [(h, (j,)) for h in range(GH) for j in range(NT)] if grp == 0 else [(h, tuple(range(NT))) for h in range(GH)]
    per_head = len(steps) // GH
    with ExitStack() as tmp, nc.Block() as block:
        s = [tmp.enter_context(nc.sbuf_tensor(f"{nm}_s{i}", [P, NT, P], F32)) for i in range(3)]
        neg = tmp.enter_context(nc.sbuf_tensor(nm + "_neg", [P, 3, NT], F32))
        pT = [tmp.enter_context(nc.sbuf_tensor(f"{nm}_pT{i}", [P, NT, P], F32)) for i in range(2)]
        sc = [tmp.enter_context(nc.psum_tensor(f"{nm}_sc{i}", [P, NT, P], F32)) for i in range(3)]
        tp = [tmp.enter_context(nc.psum_tensor(f"{nm}_tp{i}", [P, NT, P], F32)) for i in range(2)]
        pv = [tmp.enter_context(nc.psum_tensor(f"{nm}_pv{i}", [P, NT, HD], F32)) for i in range(2)]

        @block.tensor
        def _(pe):
            def score(u):
                h, js = steps[u]
                e = slice(HD * (h % 2), HD * (h % 2 + 1))
                if u >= 3:
                    pe.wait_ge(masked, u - 2)
                for j in js:
                    tile = slice(j * P, (j + 1) * P)
                    if grp == 0:
                        last = nc.tensor.matmul(sc[u % 3][:].rearrange("p j t -> p (j t)"), qT[e, h // 2, tile], kT[e, h // 2, :], start=True, stop=True)
                    else:
                        last = nc.tensor.matmul(sc[u % 3][:, j], qT[e, h // 2, tile], kT[e, h // 2, tile], start=True, stop=True)
                last.then_inc(scored, 1)

            def turn(u):
                if u >= 2:
                    pe.wait_ge(copied, u - 1)
                pe.wait_ge(exped, u + 1)
                for j in range(NT):
                    last = nc.tensor.transpose(tp[u % 2][:, j], s[u % 3][:, j], g.ident[:])
                last.then_inc(turned, 1)

            def apply(u):
                h, js = steps[u]
                pe.wait_ge(copied, u + 1)
                if u % per_head == 0 and h >= 2:
                    pe.wait_ge(kept, h - 1)
                for i in range(NT):
                    first, final = (i == 0, i == NT - 1) if grp == 0 else (True, True)
                    last = nc.tensor.matmul(pv[h % 2][:, js[0] if grp == 0 else i], pT[u % 2][:, i], v[:, i, h * HD:(h + 1) * HD],
                                            start=first, stop=final)
                last.then_inc(applied, 1)

            score(0)
            score(1)
            for u in range(len(steps)):
                if u + 2 < len(steps):
                    score(u + 2)
                turn(u)
                if u:
                    apply(u - 1)
            apply(len(steps) - 1)

        @block.vector
        def _(dve):
            V = nc.vector

            def keep(h):
                dve.wait_ge(applied, per_head * (h + 1))
                V.tensor_copy(num[:, grp, :, h, :], pv[h % 2][:]).then_inc(kept, 1)

            for u, (h, js) in enumerate(steps):
                dve.wait_ge(scored, u + 1)
                if u >= 3:
                    dve.wait_ge(turned, u - 2)
                m = mask[:, js[0]] if grp == 0 else mask.unsqueeze(1).to_broadcast([P, NT, P])
                V.tensor_tensor(s[u % 3][:], sc[u % 3][:], m, ALU.add).then_inc(masked, 1)
                dve.wait_ge(masked, u + 1)
                dst = mx[:, grp, js[0]:js[-1] + 1, h]
                src = s[u % 3][:].rearrange("p j t -> p (j t)").unsqueeze(1) if grp == 0 else s[u % 3][:]
                step.link(dve, V.tensor_reduce(dst, src, AX, ALU.max))
                V.tensor_scalar(neg[:, u % 3, 0:len(js)], dst, -1.0, None, ALU.mult).then_inc(maxed, 1)
                if u % per_head == per_head - 1 and h >= 1:
                    keep(h - 1)
            keep(GH - 1)

        @block.scalar
        def _(act):
            def copy(u):
                act.wait_ge(turned, u + 1)
                if u >= 2:
                    act.wait_ge(applied, u - 1)
                nc.scalar.copy(pT[u % 2][:], tp[u % 2][:]).then_inc(copied, 1)

            for u, (h, js) in enumerate(steps):
                act.wait_ge(maxed, u + 1)
                if grp == 0:
                    flat = s[u % 3][:].rearrange("p j t -> p (j t)")
                    last = nc.scalar.activation(flat, flat, ACT.Exp, bias=neg[:, u % 3, 0:1], accum_out=den[:, grp, js[0], h:h + 1])
                else:
                    for j in js:
                        last = nc.scalar.activation(s[u % 3][:, j], s[u % 3][:, j], ACT.Exp, bias=neg[:, u % 3, j:j + 1],
                                                    accum_out=den[:, grp, j, h:h + 1])
                last.then_inc(exped, 1)
                if u:
                    copy(u - 1)
            copy(len(steps) - 1)


def dilated_combine(nc, g, nm, half, num, mx, den, oT):
    sem = g.sem
    shifted = sem(nm + "_shifted")
    weighed = sem(nm + "_weights_ready")
    ready = sem(nm + "_out_ready")
    turned = sem(nm + "_turned")
    step = Tally(sem(nm + "_steps"))
    with ExitStack() as tmp, nc.Block() as block:
        top = tmp.enter_context(nc.sbuf_tensor(nm + "_top", [P, NT, GH], F32))
        wt = tmp.enter_context(nc.sbuf_tensor(nm + "_wt", [P, 3, NT, GH], F32))
        wd = tmp.enter_context(nc.sbuf_tensor(nm + "_wd", [P, 3, NT, GH], F32))
        acc = [tmp.enter_context(nc.psum_tensor(f"{nm}_t{i}", [P, NT, P], F32)) for i in range(4)]
        every = lambda x: x.unsqueeze(1).to_broadcast([P, 3, NT, GH])

        @block.vector
        def _(dve):
            V = nc.vector
            step.link(dve, V.tensor_tensor(top[:], mx[:, 0], mx[:, 1], ALU.max))
            step.link(dve, V.tensor_tensor(top[:], top[:], mx[:, 2], ALU.max))
            V.tensor_tensor(wt[:], mx[:], every(top[:]), ALU.subtract).then_inc(shifted, 1)
            dve.wait_ge(weighed, 1)
            step.link(dve, V.tensor_tensor(wd[:], wt[:], den[:], ALU.mult))
            step.link(dve, V.tensor_tensor(top[:], wd[:, 0], wd[:, 1], ALU.add))
            step.link(dve, V.tensor_tensor(top[:], top[:], wd[:, 2], ALU.add))
            step.link(dve, V.reciprocal(top[:], top[:]))
            step.link(dve, V.tensor_tensor(wt[:], wt[:], every(top[:]), ALU.mult))
            for i in range(3):
                step.mark(V.tensor_tensor(num[:, i], num[:, i], wt[:, i].unsqueeze(3).to_broadcast([P, NT, GH, HD]), ALU.mult))
            step.settle(dve)
            step.link(dve, V.tensor_tensor(num[:, 0], num[:, 0], num[:, 1], ALU.add))
            V.tensor_tensor(num[:, 0], num[:, 0], num[:, 2], ALU.add).then_inc(ready, 1)
            for c in range(4):
                dve.wait_ge(turned, c + 1)
                V.tensor_copy(oT[:, 4 * half + c, :], acc[c][:].rearrange("p j t -> p (j t)"))

        @block.scalar
        def _(act):
            act.wait_ge(shifted, 1)
            nc.scalar.activation(wt[:], wt[:], ACT.Exp).then_inc(weighed, 1)

        @block.tensor
        def _(pe):
            pe.wait_ge(ready, 1)
            o = num[:, 0].rearrange("p j h d -> p j (h d)")
            for c in range(4):
                for j in range(NT):
                    last = nc.tensor.transpose(acc[c][:, j], o[:, j, c * P:(c + 1) * P], g.ident[:])
                last.then_inc(turned, 1)


def mlp(nc, g, nm, yT, x):
    sem, st = g.sem, g.stream
    p0 = st.taken
    NP = D // PW
    quarters = FF // D
    positive = sem(nm + "_relu_ready")
    hidden = sem(nm + "_hidden_ready")
    emptied = sem(nm + "_emptied")
    with ExitStack() as tmp, nc.Block() as block:
        hid = tmp.enter_context(nc.sbuf_tensor(nm + "_hid", [P, 2, KD, T], F32))
        up = [[tmp.enter_context(nc.psum_tensor(f"{nm}_h{s}{i}", [P, T], F32)) for i in range(2)] for s in range(2)]
        acc = [[tmp.enter_context(nc.psum_tensor(f"{nm}_o{s}{i}", [P, 2, PW], F32)) for i in range(2)] for s in range(2)]

        @block.sync
        def _(sp):
            st.load_until(sp, p0 + 2 * NP * quarters + SLOTS)

        @block.tensor
        def _(pe):
            for q in range(quarters):
                for n in range(NP):
                    i = NP * q + n
                    w = st.take(pe)
                    if i >= 2:
                        pe.wait_ge(hidden, i - 1)
                    for h in range(2):
                        for k in range(KD):
                            last = nc.tensor.matmul(up[i % 2][h][:], w[:, k, h * P:(h + 1) * P], yT[:, k, :], start=(k == 0), stop=(k == KD - 1))
                    last.then_inc(st.used, 1)
                for n in range(NP):
                    i = NP * q + n
                    w = st.take(pe)
                    if n == 0:
                        pe.wait_ge(hidden, NP * (q + 1))
                    if i >= 2:
                        pe.wait_ge(emptied, i - 1)
                    for j in range(NT):
                        for k in range(KD):
                            last = nc.tensor.matmul(acc[i % 2][j // 2][:, j % 2], hid[:, q % 2, k, j * P:(j + 1) * P], w[:, k, :],
                                                    start=(k == 0), stop=(k == KD - 1))
                    last.then_inc(st.used, 1)

        @block.scalar
        def _(act):
            for q in range(quarters):
                for n in range(NP):
                    i = NP * q + n
                    act.wait_ge(st.used, p0 + 2 * NP * q + n + 1)
                    for h in range(2):
                        last = nc.scalar.activation(hid[:, q % 2, 2 * n + h, :], up[i % 2][h][:], ACT.Relu)
                    last.then_inc(positive, 1)

        @block.vector
        def _(dve):
            V = nc.vector
            for q in range(quarters):
                for n in range(NP):
                    i = NP * q + n
                    dve.wait_ge(positive, i + 1)
                    for h in range(2):
                        d = hid[:, q % 2, 2 * n + h, :]
                        last = V.tensor_tensor(d, d, up[i % 2][h][:], ALU.mult)
                    last.then_inc(hidden, 1)
                for n in range(NP):
                    i = NP * q + n
                    dve.wait_ge(st.used, p0 + 2 * NP * q + NP + n + 1)
                    if q:
                        dve.wait_ge(emptied, i - NP + 1)
                    for h in range(2):
                        d = x[:, 2 * h:2 * h + 2, n * PW:(n + 1) * PW]
                        last = V.tensor_tensor(d, d, acc[i % 2][h][:], ALU.add)
                    last.then_inc(emptied, 1)


def gated_conv(nc, g, yT, zT):
    sem, st = g.sem, g.stream
    p0 = st.taken
    emptied = sem("gc_emptied")
    copied = sem("gc_b_c_copied")
    step = Tally(sem("gc_steps"))
    n_chunk = D // PW
    with ExitStack() as tmp, nc.Block() as block:
        bc = tmp.enter_context(nc.sbuf_tensor("gc_bc", [P, 2, 2, 2, T], F32))
        u = tmp.enter_context(nc.sbuf_tensor("gc_u", [P, 2, T], F32))
        y = tmp.enter_context(nc.sbuf_tensor("gc_y", [P, 2, T], F32))
        acc = [[tmp.enter_context(nc.psum_tensor(f"gc_o{s}{i}", [P, T], F32)) for i in range(2)] for s in range(3)]

        @block.sync
        def _(sp):
            st.load_until(sp, p0 + 3 * n_chunk + SLOTS)

        @block.tensor
        def _(pe):
            for n in range(3 * n_chunk):
                c, part = n // 3, n % 3
                w = st.take(pe)
                if c:
                    if part < 2:
                        pe.wait_ge(copied, 2 * (c - 1) + part + 1)
                    else:
                        pe.wait_ge(emptied, c)
                for h in range(2):
                    for k in range(KD):
                        last = nc.tensor.matmul(acc[part][h][:], w[:, k, h * P:(h + 1) * P], yT[:, k, :], start=(k == 0), stop=(k == KD - 1))
                last.then_inc(st.used, 1)

        @block.scalar
        def _(act):
            for c in range(n_chunk):
                for part in range(2):
                    act.wait_ge(st.used, p0 + 3 * c + part + 1)
                    if c >= 2 and part == 0:
                        act.wait_ge(emptied, c)
                    for h in range(2):
                        last = nc.scalar.copy(bc[:, c % 2, part, h], acc[part][h][:])
                    last.then_inc(copied, 1)

        @block.vector
        def _(dve):
            V = nc.vector
            tap = lambda t, k: g.cols[:, g.col["b_conv"] + KD * t + k:g.col["b_conv"] + KD * t + k + 1]
            for c in range(n_chunk):
                dve.wait_ge(st.used, p0 + 3 * c + 3)
                dve.wait_ge(copied, 2 * c + 2)
                for h in range(2):
                    last = V.tensor_tensor(u[:, h], bc[:, c % 2, 1, h], acc[2][h][:], ALU.mult)
                    step.mark(last)
                step.settle(dve)
                for h in range(2):
                    step.mark(V.tensor_scalar(y[:, h], u[:, h], tap(1, 2 * c + h), None, ALU.mult))
                step.settle(dve)
                for h in range(2):
                    step.mark(V.scalar_tensor_tensor(y[:, h, 1:], u[:, h, 0:T - 1], tap(0, 2 * c + h), y[:, h, 1:], ALU.mult, ALU.add))
                step.settle(dve)
                for h in range(2):
                    step.mark(V.scalar_tensor_tensor(y[:, h, 0:T - 1], u[:, h, 1:], tap(2, 2 * c + h), y[:, h, 0:T - 1], ALU.mult, ALU.add))
                step.settle(dve)
                for h in range(2):
                    dst = zT[:, 2 * c + h, :].rearrange("c (j p) -> c p j", j=NT)
                    last = V.tensor_tensor(dst, y[:, h].rearrange("c (p j) -> c p j", j=NT), bc[:, c % 2, 0, h].rearrange("c (p j) -> c p j", j=NT), ALU.mult)
                last.then_inc(emptied, 1)
                dve.wait_ge(emptied, c + 1)


def store(nc, x, out, stored):
    with nc.Block() as block:
        @block.sync
        def _(sp):
            sp.dma_start(out.rearrange("(p j) d -> p j d", j=NT), x[:]).then_inc(stored, 16)
            sp.wait_ge(stored, 16)


def program(nc, a, out):
    with ExitStack() as ctx:
        g = Buffers()
        g.sb = lambda n, s, dt=F32: ctx.enter_context(nc.sbuf_tensor(n, s, dt))
        g.sb_in = lambda stack, n, s, dt=F32: stack.enter_context(nc.sbuf_tensor(n, s, dt))
        g.passing = []

        def sem(name):
            g.passing.append(nc.alloc_semaphore(name=name))
            return g.passing[-1]

        def retire():
            nc.clear_and_free_semaphores(g.passing)
            nc.all_engine_barrier()
            g.passing = []

        g.sem = sem
        lasting = lambda n: ctx.enter_context(nc.semaphore(n))
        g.ring = g.sb("weight_ring", [P, SLOTS, KD, PW])
        g.ident = g.sb("ident", [P, P])
        g.headsum = g.sb("headsum", [P, P])
        g.ones = g.sb("ones", [P, P])
        g.cols = g.sb("cols", [P, 3 * P])
        g.mod = g.sb("mod", [P, 6 * KD, 2])
        g.mix_scale = g.sb("mix_scale", [P, KD, 2])
        g.ffn_scale = g.sb("ffn_scale", [P, KD, 2])
        g.post = g.sb("post_gains", [P, 2, KD])
        output_stored = lasting("output_stored")
        g.stream = st = Stream(g.ring, [lasting(f"slot{s}_full") for s in range(SLOTS)], lasting("panels_used"))
        st.add_matrix(a["w_mod"], 0, 0, 6 * D)
        w = a["w_in"]
        st.add_matrix(w, 0, 0, RET_COLS)
        r0 = RET_COLS
        st.add((w[:, r0 + 1536:r0 + 1728], 0))
        st.add((w[:, r0 + 1728:r0 + 1984], 0))
        for hp in range(4):
            st.add((w[:, r0 + hp * P:r0 + (hp + 1) * P], 0), (w[:, r0 + 512 + hp * P:r0 + 512 + (hp + 1) * P], P))
            st.add((w[:, r0 + 1024 + hp * P:r0 + 1024 + (hp + 1) * P], 0))
        st.add_matrix(a["w_out"], 0, 0, D)
        for e in range(E_N):
            for c in range(0, D, PW):
                st.add((a["w_gate"][e, :, c:c + PW], 0))
                st.add((a["w_up"][e, :, c:c + PW], 0))
            for c in range(0, D, PW):
                st.add((a["w_down"][e, :, c:c + PW], 0))
        for half in range(2):
            for grp in range(3):
                for part in range(3):
                    c0 = (grp * 3 + part) * D + half * 512
                    st.add_matrix(a["a_wqkv"], 0, c0, c0 + 512)
        st.add_matrix(a["a_wo"], 0, 0, D)

        def add_mlp(layer):
            for q in range(FF // D):
                st.add_matrix(a["mlp_w1"][layer], 0, q * D, (q + 1) * D)
                st.add_matrix(a["mlp_w2"][layer][q * D:(q + 1) * D, :], 0, 0, D)
        add_mlp(0)
        for c in range(0, D, PW):
            for part in range(3):
                st.add((a["b_win"][:, part * D + c:part * D + c + PW], 0))
        st.add_matrix(a["b_wout"], 0, 0, D)
        add_mlp(1)

        def fetch(dst, src, name):
            there = g.sem(name + "_loaded")
            with nc.Block() as block:
                @block.sync
                def _(sp):
                    sp.dma_start(dst, src).then_inc(there, 16)
                    sp.wait_ge(there, 16)

        setup(nc, g, a)
        modulation(nc, g)
        with ExitStack() as first:
            latT = first.enter_context(nc.sbuf_tensor("latT", [P, KD, T], F32))
            with ExitStack() as mix:
                hT = mix.enter_context(nc.sbuf_tensor("hT", [P, KD, TA], F32))
                with ExitStack() as tmp:
                    x_tiles = tmp.enter_context(nc.sbuf_tensor("x_tiles", [P, NT, D], F32))
                    ctx_tiles = tmp.enter_context(nc.sbuf_tensor("ctx_tiles", [P, NTC, D], F32))
                    loaded = g.sem("tokens_loaded")
                    with nc.Block() as block:
                        @block.sync
                        def _(sp):
                            sp.dma_start(x_tiles[:], a["x"].rearrange("(p j) d -> p j d", j=NT)).then_inc(loaded, 16)
                            sp.dma_start(ctx_tiles[:], a["ctx"].rearrange("(p j) d -> p j d", j=NTC)).then_inc(loaded, 16)
                            sp.wait_ge(loaded, 32)
                    norm_turn(nc, g, "pre_mix", [
                        (x_tiles, NT, hT, TC, lambda k: g.mix_scale[:, k, 0:1], lambda k: g.mod[:, k, 0:1]),
                        (ctx_tiles, NTC, hT, 0, lambda k: g.mix_scale[:, k, 1:2], lambda k: g.mod[:, k, 1:2])])
                with ExitStack() as ret:
                    gates = ret.enter_context(nc.sbuf_tensor("ret_gates", [P, KD, T], F32))
                    v_tok = ret.enter_context(nc.sbuf_tensor("ret_v", [P, NTC + NT, RET_W], F32))
                    qT = ret.enter_context(nc.sbuf_tensor("ret_qT", [P, 4, T], F32))
                    kT = ret.enter_context(nc.sbuf_tensor("ret_kT", [P, 4, TA], F32))
                    with ExitStack() as tmp:
                        q_tok = tmp.enter_context(nc.sbuf_tensor("ret_q", [P, NT, RET_W], F32))
                        k_tok = tmp.enter_context(nc.sbuf_tensor("ret_k", [P, NTC + NT, RET_W], F32))
                        rope = tmp.enter_context(nc.sbuf_tensor("ret_rope_tab", [P, 2, NT, 32], F32))
                        fetch(rope[:], a["c_rope"], "rope")
                        retention_inputs(nc, g, hT, q_tok, k_tok, v_tok, gates, rope)
                        retention_turn(nc, g, q_tok, k_tok, qT, kT)
                    dist = ret.enter_context(nc.sbuf_tensor("ret_dist", [P, 2, TA], F32))
                    fetch(dist[:], a["c_dist"], "dist")
                    retention(nc, g, qT, kT, v_tok, gates, dist, latT)
                retire()
                with ExitStack() as rw:
                    buf = lambda stack, n, shape: stack.enter_context(nc.sbuf_tensor("rw_" + n, [P] + shape, F32))
                    low, par, f = Buffers(), Buffers(), Buffers()
                    low.wl, low.al, low.gl = buf(rw, "wl", [TA]), buf(rw, "al", [TA]), buf(rw, "gl", [2, T])
                    par.w2, par.a2 = buf(rw, "w2", [RW_W]), buf(rw, "a2", [RW_W])
                    tri = buf(rw, "tri", [9, 2, P])
                    fetch(tri[:], a["c_tri"], "tri")
                    fetch(par.w2[:], a["rwkv_w2"], "rwkv_w2")
                    fetch(par.a2[0:64, :], a["rwkv_a2"], "rwkv_a2")
                    par.g2_rows = a["rwkv_g2"].rearrange("d p n -> p d n")
                    rwkv_low(nc, g, hT, low.wl, low.al, low.gl)
                    f.A, f.Bh, f.Kh, f.Bb, f.Kb = (buf(rw, n, [2, TA]) for n in ("A", "Bh", "Kh", "Bb", "Kb"))
                    f.R, f.Y = buf(rw, "R", [2, T]), buf(rw, "Y", [2, T])
                    f.v, f.bonus = buf(rw, "v", [TA]), buf(rw, "bonus", [T])
                    f.pc, f.pm = (buf(rw, n, [2, TA // P]) for n in ("pc", "pm"))
                    for hp in range(4):
                        with ExitStack() as tmp:
                            restart = buf(tmp, f"restart{hp}", [2, TA])
                            fetch(restart[:], a["c_restart"], f"restart{hp}")
                            rwkv_prepare(nc, g, hp, hT, f, low, par, restart)
                        rwkv_scan(nc, g, hp, f, tri)
                        rwkv_out(nc, g, hp, f, low, par, latT)
                        retire()
            x = g.sb_in(first, "x", [P, NT, D])
            fetch(x[:], a["x"].rearrange("(p j) d -> p j d", j=NT), "x")
            with ExitStack() as tmp:
                mix = g.sb_in(tmp, "mix", [P, NT, D])
                row = g.sb_in(tmp, "post_mix_row", [P, D])
                row_vector(nc, g, "post_mix", row, g.post[:, 0])
                project_rows(nc, g, "w_out", latT, lambda js, c, acc: nc.vector.tensor_copy(mix[:, js, c], acc))
                post_norm(nc, g, "post_mix_norm", mix, row, x)
            retire()
            with ExitStack() as moe:
                xsT = g.sb_in(moe, "moe_xsT", [P, KD, E_N * CAP])
                selT = g.sb_in(moe, "moe_selT", [P, E_N // 2, T])
                with ExitStack() as tmp:
                    h2T = g.sb_in(tmp, "h2T", [P, KD, T])
                    norm_turn(nc, g, "pre_ffn", [(x, NT, h2T, 0, lambda k: g.ffn_scale[:, k, 0:1], lambda k: g.mod[:, 3 * KD + k, 0:1])])
                    w_r = g.sb_in(tmp, "w_router", [P, KD, E_N])
                    pick = g.sb_in(tmp, "pick", [E_N, E_N, P])
                    tokrow = g.sb_in(tmp, "tokrow", [P, T])
                    tokcol = g.sb_in(tmp, "tokcol", [P, NT])
                    fetch(w_r[:], a["w_router"].rearrange("(k p) e -> p k e", p=P), "w_router")
                    fetch(pick[:], a["c_pick"], "pick")
                    fetch(tokrow[:], a["c_tokrow"], "tokrow")
                    fetch(tokcol[:], a["c_tokcol"], "tokcol")
                    router(nc, g, h2T, w_r, pick, tokrow, tokcol, xsT, selT)
                ye = g.sb_in(moe, "moe_ye", [P, E_N // 2, D])
                experts(nc, g, xsT, ye)
                out_sum = g.sb_in(moe, "moe_sum", [P, NT, D])
                row = g.sb_in(moe, "post_ffn_row", [P, D])
                row_vector(nc, g, "post_ffn", row, g.post[:, 1])
                scatter(nc, g, ye, selT, out_sum)
                post_norm(nc, g, "post_ffn_norm", out_sum, row, x)
            retire()

            def add_to_x(js, c, acc):
                return nc.vector.tensor_tensor(x[:, js, c], x[:, js, c], acc, ALU.add)

            norm_gain = lambda name, layer: lambda k: g.cols[:, g.col[name] + KD * layer + k:g.col[name] + KD * layer + k + 1]

            with ExitStack() as att:
                norm_turn(nc, g, "norm1_0", [(x, NT, latT, 0, norm_gain("norm1", 0), None)], permuted=True)
                oT = g.sb_in(att, "a_oT", [P, KD, T])
                num = g.sb_in(att, "a_num", [P, 3, NT, GH, HD])
                mx = g.sb_in(att, "a_max", [P, 3, NT, GH])
                den = g.sb_in(att, "a_den", [P, 3, NT, GH])
                qT = g.sb_in(att, "a_qT", [P, 4, T])
                kT = g.sb_in(att, "a_kT", [P, 4, T])
                v = g.sb_in(att, "a_v", [P, NT, HALF])
                gains = g.sb_in(att, "a_gains", [P, 6, HD])
                rope = g.sb_in(att, "a_rope", [P, 2, NT, 8])
                band = g.sb_in(att, "a_band", [P, NT, NT, P])
                stride = g.sb_in(att, "a_stride", [P, 2, P])
                gain_rows(nc, g, a, gains)
                fetch(rope[:], a["c_rope2"], "a_rope")
                fetch(band[:], a["c_band"], "a_band")
                fetch(stride[:], a["c_stride"], "a_stride")
                for half in range(2):
                    for grp in range(3):
                        nm = f"a{half}{grp}"
                        dilated_inputs(nc, g, nm + "i", grp, latT, v, qT, kT, gains, rope)
                        dilated_attention(nc, g, nm + "s", grp, qT, kT, v, band[:] if grp == 0 else stride[:, grp - 1], num, mx, den)
                        retire()
                    dilated_combine(nc, g, f"a{half}c", half, num, mx, den, oT)
                project_rows(nc, g, "a_wo", oT, add_to_x)
            retire()
            norm_turn(nc, g, "norm2_0", [(x, NT, latT, 0, norm_gain("norm2", 0), None)], permuted=True)
            mlp(nc, g, "mlp0", latT, x)
            retire()
            norm_turn(nc, g, "norm1_1", [(x, NT, latT, 0, norm_gain("norm1", 1), None)])
            with ExitStack() as tmp:
                zT = g.sb_in(tmp, "gc_zT", [P, KD, T])
                gated_conv(nc, g, latT, zT)
                project_rows(nc, g, "b_wout", zT, add_to_x)
            retire()
            norm_turn(nc, g, "norm2_1", [(x, NT, latT, 0, norm_gain("norm2", 1), None)], permuted=True)
            mlp(nc, g, "mlp1", latT, x)
            store(nc, x, out, output_stored)


_FLAT = {"x": (T, D), "c": (D,), "ctx": (TC, D), "w_mod": (D, 6 * D), "b_mod": (6 * D,), "norm_gains": (4 * D,),
         "w_in": (D, RET_COLS + RW_COLS), "rwkv_conv": (3, RW_COLS), "rwkv_w0": (2 * RW_W,), "rwkv_w2": (P, RW_W),
         "rwkv_a0": (RW_W,), "rwkv_a2": (64, RW_W), "rwkv_g2": (2, P, RW_W), "rwkv_k_k": (RW_W,),
         "rwkv_k_a": (RW_W,), "rwkv_r_k": (RW_W,), "rwkv_lnx_w": (RW_W,), "rwkv_lnx_b": (RW_W,),
         "w_out": (D, D), "w_router": (D, E_N), "w_gate": (E_N, D, D), "w_up": (E_N, D, D), "w_down": (E_N, D, D),
         "norm1_2": (2 * D,), "norm2_2": (2 * D,), "a_wqkv_2": (D, 9 * D), "a_q_gain_2": (3 * HD,),
         "a_k_gain_2": (3 * HD,), "a_wo_2": (D, D), "b_win_2": (D, 3 * D), "b_conv_2": (3 * D,),
         "b_wout_2": (D, D), "mlp_w1_2": (2, D, FF), "mlp_w2_2": (2, FF, D), "c_ctx": (D,)}


def kernel(**inputs):
    import concourse.bacc as _bacc
    from concourse.bass_utils import run_bass_kernel_spmd as _run

    nc = _bacc.Bacc("TRN2", target_bir_lowering=False, num_devices=1)
    arrays, a = {}, {}
    for name, shape in _FLAT.items():
        arrays["in_" + name] = np.ascontiguousarray(inputs[name]).reshape(shape)
    for name, table in consts().items():
        arrays["in_" + name] = table
    for name, x in arrays.items():
        a[name[3:]] = nc.dram_tensor(name, x.shape, F32, kind="ExternalInput").ap()
    aliases(a)
    out = nc.dram_tensor("out_0", (T, D), F32, kind="ExternalOutput").ap()
    program(nc, a, out)
    r = _run(nc, [arrays], core_ids=[0])
    return np.asarray(r.results[0]["out_0"]).reshape(1, T, D)


def aliases(a):
    for name in ("a_wqkv", "a_wo", "b_win", "b_wout", "mlp_w1", "mlp_w2"):
        a[name] = a[name + "_2"]
```

```python
from contextlib import ExitStack

import numpy as np

import concourse.bass as bass
from concourse import mybir

F32 = mybir.dt.float32
F32R = mybir.dt.float32r
U32 = mybir.dt.uint32
ALU = mybir.AluOpType
ACT = mybir.ActivationFunctionType
AX = mybir.AxisListType.X

P = 128
D = 1024
KD = D // P
T = 512
TC = 256
TA = T + TC
NT = T // P
NTC = TC // P
HD = 64
EPS = 1e-6
GN_EPS = 64e-5
RET_W = 512
RET_H = RET_W // HD
RET_COLS = 5 * RET_W
RW_W = 512
RW_COLS = 3 * RW_W + 64 * 3 + 128 * 2
E_N = 16
CAP = 2 * T // E_N
FF = 4 * D
GRID_W = 64
SLOTS = 5
PW = 256
DECAY = float(np.exp(-0.5))


class Buffers:
    pass


class Tally:

    def __init__(self, sem):
        self.sem, self.n = sem, 0

    def link(self, eng, ins):
        self.n += 1
        ins.then_inc(self.sem, 1)
        eng.wait_ge(self.sem, self.n)

    def mark(self, ins):
        self.n += 1
        ins.then_inc(self.sem, 1)

    def settle(self, eng):
        eng.wait_ge(self.sem, self.n)


class Stream:

    def __init__(self, nc, ring, lo, hi, full, used, hi_ready, lo_ready):
        self.nc, self.ring, self.lo, self.hi = nc, ring, lo, hi
        self.full, self.used, self.hi_ready, self.lo_ready = full, used, hi_ready, lo_ready
        self.panels, self.landed, self.width, self.order, self.split = [], [], [], [], []
        self.loaded = self.taken = self.rounded = self.reduced = 0
        self.counts = [0] * SLOTS

    def add(self, *pieces, split=True):
        p = len(self.panels)
        self.counts[p % SLOTS] += 16 * len(pieces)
        self.panels.append(pieces)
        self.landed.append(self.counts[p % SLOTS])
        self.width.append(sum(src.shape[1] for src, _ in pieces))
        self.order.append(len(self.split))
        if split:
            self.split.append(p)

    def add_matrix(self, w, rows, c0, c1, split=True):
        for c in range(c0, c1, PW):
            self.add((w[rows:rows + D, c:min(c + PW, c1)], 0), split=split)

    def load_until(self, sp, n):
        while self.loaded < min(n, len(self.panels)):
            p, s = self.loaded, self.loaded % SLOTS
            if p >= SLOTS:
                sp.wait_ge(self.used, p - SLOTS + 1)
            for src, c in self.panels[p]:
                w = src.shape[1]
                sp.dma_start(self.ring[:, s, :, c:c + w],
                             src.rearrange("(k p) n -> p k n", p=P)).then_inc(self.full[s], 16)
            self.loaded += 1

    def round_until(self, act, n):
        while self.rounded < len(self.split) and self.split[self.rounded] < n:
            q = self.rounded
            p, w = self.split[q], self.width[self.split[q]]
            act.wait_ge(self.full[p % SLOTS], self.landed[p])
            if q >= 2:
                act.wait_ge(self.used, self.split[q - 2] + 1)
            self.nc.scalar.copy(self.hi[:, q % 2, :, 0:w], self.ring[:, p % SLOTS, :, 0:w]).then_inc(self.hi_ready, 1)
            self.rounded += 1

    def reduce_until(self, pool, n):
        while self.reduced < len(self.split) and self.split[self.reduced] < n:
            q = self.reduced
            p, w = self.split[q], self.width[self.split[q]]
            pool.wait_ge(self.hi_ready, q + 1)
            slot = self.ring[:, p % SLOTS, :, 0:w]
            self.nc.gpsimd.tensor_tensor(self.lo[:, p % SLOTS, :, 0:w], slot, self.hi[:, q % 2, :, 0:w].bitcast(F32),
                                         ALU.subtract).then_inc(self.lo_ready, 1)
            self.reduced += 1

    def take(self, pe):
        p, s = self.taken, self.taken % SLOTS
        pe.wait_ge(self.full[s], self.landed[p])
        self.taken += 1
        return self.ring[:, s]

    def take_split(self, pe):
        p = self.taken
        q = self.order[p]
        pe.wait_ge(self.lo_ready, q + 1)
        self.taken += 1
        return self.hi[:, q % 2], self.lo[:, p % SLOTS]


def dense(nc, dst, left, right):
    for a, b in ((0, 0), (0, 1), (1, 0)):
        for k in range(KD):
            last = nc.tensor.matmul(dst, left(a, k), right(b, k), start=(a + b + k == 0), stop=(a == 1 and k == KD - 1))
    return last


def consts():
    i = np.arange(P)
    f = np.float32
    out = {}
    out["ident"] = np.eye(P, dtype=f)
    out["headsum"] = (i[:, None] // HD == i[None, :] // HD).astype(f)
    before = (i[:, None] < i[None, :])
    low = [np.zeros((P, 2, P), f) for _ in range(9)]
    for d in range(2):
        b = before if d == 0 else before.T
        low[0][:, d] = b
        low[1][:, d] = b | np.eye(P, dtype=bool)
        for lv in range(7):
            h = 1 << lv
            low[2 + lv][:, d] = b & (i[:, None] // (2 * h) == i[None, :] // (2 * h)) & (i[:, None] // h != i[None, :] // h)
    out["tri"] = np.stack(low, 1)
    t = np.arange(T)
    freq = 10000.0 ** (-np.arange(16) / 16.0)
    freq = freq.astype(f).astype(np.float64)
    ang = np.concatenate([(t // GRID_W)[:, None] * freq, (t % GRID_W)[:, None] * freq], -1)
    ang = ang.astype(f).astype(np.float64).reshape(NT, P, 32).transpose(1, 0, 2)
    out["rope"] = np.stack([np.cos(ang), np.sin(ang)], 1).astype(f)
    inv = (500000.0 ** (-np.arange(0, 16, 2) / 16.0)).astype(f).astype(np.float64)
    ang = (t[:, None] * inv).astype(f).astype(np.float64).reshape(P, NT, 8)
    out["rope2"] = np.stack([np.cos(ang), np.sin(ang)], 1).astype(f)
    x = np.arange(TA)
    far = 1e9
    ef = (x[None] - i[:, None]).astype(f)
    ef[ef < 0] = far
    eb = (i[:, None] + 640 - x[None]).astype(f)
    eb[eb < 0] = far
    out["dist"] = np.stack([ef, eb], 1)
    rs = np.ones((P, TA), f)
    rs[:, ::P] = 0
    out["restart"] = rs
    tok = np.arange(P)[None] * 4 + np.arange(4)[:, None]
    far0 = np.abs(tok.T[:, :, None, None] - tok[None, None]) > 64
    out["band"] = np.where(far0, f(-1e30), f(0)).astype(f)
    m1 = np.abs(i[:, None] - i[None]) > 64
    m2 = (i[:, None] % 4) != (i[None] % 4)
    out["stride"] = np.stack([np.where(m1, f(-1e30), f(0)), np.where(m2, f(-1e30), f(0))], 1).astype(f)
    out["tokrow"] = np.broadcast_to(tok.reshape(T).astype(f), (P, T)).copy()
    out["tokcol"] = (np.arange(4)[None] + 4 * i[:, None]).astype(f)
    pick = np.zeros((E_N, E_N, P), f)
    for e in range(E_N):
        pick[e, e] = 1
    out["pick"] = pick
    return {"c_" + k: np.ascontiguousarray(v) for k, v in out.items()}


CONSTS = {k: v.shape for k, v in consts().items()}


def setup(nc, g, a):
    sem = g.sem
    loaded = sem("params_loaded")
    padded = sem("params_padded")
    turned = sem("params_turned")
    copied = sem("params_copied")
    rows = [[("c", 8, a["c"]), ("c_ctx", 8, a["c_ctx"]), ("b_mod", 48, a["b_mod"]), ("gains", 32, a["norm_gains"])],
            [], []]
    cv = a["rwkv_conv"]
    for tap in range(3):
        rows[1] += [(f"conv{tap}", 13, cv[tap, 0:1664]), (f"conv{tap}_al", 1, cv[tap, 1664:1728]),
                    (f"conv{tap}_gl", 2, cv[tap, 1728:1984])]
    rows[1] += [("w0", 8, a["rwkv_w0"]), ("a0", 4, a["rwkv_a0"]), ("k_k", 4, a["rwkv_k_k"]),
                ("k_a", 4, a["rwkv_k_a"]), ("r_k", 4, a["rwkv_r_k"]), ("lnx_w", 4, a["rwkv_lnx_w"]),
                ("lnx_b", 4, a["rwkv_lnx_b"])]
    rows[2] += [("norm1", 16, a["norm1_2"]), ("norm2", 16, a["norm2_2"]), ("b_conv", 24, a["b_conv_2"])]
    g.col = {}
    n_dma = sum(len(r) for r in rows) + 2
    with ExitStack() as tmp, nc.Block() as block:
        raw = tmp.enter_context(nc.sbuf_tensor("param_rows", [P, 3, P], F32))
        turn = tmp.enter_context(nc.psum_tensor("param_cols", [P, 3, P], F32))

        for n, group in enumerate(rows):
            at = 0
            for name, k, _ in group:
                g.col[name] = n * P + at
                at += k

        @block.sync
        def _(sp):
            g.stream.load_until(sp, SLOTS)

        @block.scalar
        def _(act):
            act.dma_start(g.ident[:], a["c_ident"]).then_inc(loaded, 16)
            act.dma_start(g.headsum[:], a["c_headsum"]).then_inc(loaded, 16)
            act.wait_ge(padded, 1)
            for n, group in enumerate(rows):
                at = 0
                for name, k, src in group:
                    if name.endswith("_al"):
                        act.dma_start(raw[at:at + 1, n, 0:64], src.rearrange("(k n) -> k n", k=1)).then_inc(loaded, 16)
                    else:
                        act.dma_start(raw[at:at + k, n, :], src.rearrange("(k n) -> k n", n=P)).then_inc(loaded, 16)
                    at += k

        @block.gpsimd
        def _(pool):
            nc.gpsimd.memset(raw[:], 0.0).then_inc(padded, 1)
            nc.gpsimd.memset(g.ones[:], 1.0)

        @block.tensor
        def _(pe):
            pe.wait_ge(loaded, 16 * n_dma)
            for n in range(3):
                last = nc.tensor.transpose(turn[:, n, :], raw[:, n, :], g.ident[:])
            last.then_inc(turned, 1)

        @block.vector
        def _(dve):
            dve.wait_ge(turned, 1)
            nc.vector.tensor_copy(g.cols[:], turn[:].rearrange("p a b -> p (a b)")).then_inc(copied, 1)


def modulation(nc, g):
    sem, st = g.sem, g.stream
    n_col = 6 * KD
    n_panel = 6 * D // PW
    p0 = st.taken
    sigmoid_ready = sem("c_sigmoid_ready")
    silu_ready = sem("c_silu_ready")
    kept = sem("mod_rows_kept")
    turned = sem("mod_turned")
    step = Tally(sem("mod_steps"))
    cc = g.col["c"]
    c_cols = g.cols[:, cc:cc + 2 * KD].rearrange("p (c k) -> p k c", c=2)
    with ExitStack() as tmp, nc.Block() as block:
        silu = tmp.enter_context(nc.sbuf_tensor("c_silu", [P, KD, 2], F32))
        sig = tmp.enter_context(nc.sbuf_tensor("c_sig", [P, KD, 2], F32))
        rows = tmp.enter_context(nc.sbuf_tensor("mod_rows", [2, 6 * D], F32))
        part = [tmp.enter_context(nc.psum_tensor(f"mod_part{i}", [2, PW], F32)) for i in range(4)]
        acc = tmp.enter_context(nc.psum_tensor("mod_acc", [P, n_col, 2], F32))

        @block.sync
        def _(sp):
            st.load_until(sp, p0 + n_panel + SLOTS)

        @block.scalar
        def _(act):
            nc.scalar.activation(sig[:], c_cols, ACT.Sigmoid).then_inc(sigmoid_ready, 1)

        @block.vector
        def _(dve):
            dve.wait_ge(sigmoid_ready, 1)
            nc.vector.tensor_tensor(silu[:], sig[:], c_cols, ALU.mult).then_inc(silu_ready, 1)
            b = g.cols[:, g.col["b_mod"]:g.col["b_mod"] + n_col].unsqueeze(2).to_broadcast([P, n_col, 2])
            for n in range(n_panel):
                dve.wait_ge(st.used, p0 + n + 1)
                nc.vector.tensor_copy(rows[:, n * PW:(n + 1) * PW], part[n % 4][:]).then_inc(kept, 1)
            dve.wait_ge(turned, 1)
            step.link(dve, nc.vector.tensor_tensor(g.mod[:], acc[:], b, ALU.add))
            gain = g.cols[:, g.col["gains"]:g.col["gains"] + KD].unsqueeze(2).to_broadcast([P, KD, 2])
            step.link(dve, nc.vector.tensor_scalar(g.mix_scale[:], g.mod[:, KD:2 * KD, :], 1.0, None, ALU.add))
            gains = lambda i: g.cols[:, g.col["gains"] + i * KD:g.col["gains"] + (i + 1) * KD]
            step.link(dve, nc.vector.tensor_tensor(g.mix_scale[:], g.mix_scale[:], gain, ALU.mult))
            step.link(dve, nc.vector.tensor_scalar(g.ffn_scale[:], g.mod[:, 4 * KD:5 * KD, :], 1.0, None, ALU.add))
            step.mark(nc.vector.tensor_tensor(g.ffn_scale[:], g.ffn_scale[:], gains(2).unsqueeze(2).to_broadcast([P, KD, 2]), ALU.mult))
            step.mark(nc.vector.tensor_tensor(g.post[:, 0], g.mod[:, 2 * KD:3 * KD, 0], gains(1), ALU.mult))
            step.mark(nc.vector.tensor_tensor(g.post[:, 1], g.mod[:, 5 * KD:6 * KD, 0], gains(3), ALU.mult))

        @block.tensor
        def _(pe):
            pe.wait_ge(silu_ready, 1)
            for n in range(n_panel):
                w = st.take(pe)
                if n >= 4:
                    pe.wait_ge(kept, n - 3)
                for k in range(KD):
                    last = nc.tensor.matmul(part[n % 4][:], silu[:, k, :], w[:, k, :], start=(k == 0), stop=(k == KD - 1))
                last.then_inc(st.used, 1)
            pe.wait_ge(kept, n_panel)
            for i in range(n_col):
                last = nc.tensor.transpose(acc[:, i, :], rows[:, i * P:(i + 1) * P], g.ident[0:2, 0:2])
            last.then_inc(turned, 1)


def norm_turn(nc, g, name, groups, permuted=False, hi=None, lo=None):
    sem = g.sem
    squares = sem(name + "_squares")
    meaned = sem(name + "_mean_ready")
    rooted = sem(name + "_root_ready")
    scaled = sem(name + "_tiles_scaled")
    turned = sem(name + "_turned")
    written = sem(name + "_written")
    rounded = sem(name + "_rounded")
    step = Tally(sem(name + "_steps"))
    n_tile = sum(x[1] for x in groups)
    with ExitStack() as tmp, nc.Block() as block:
        junk = tmp.enter_context(nc.sbuf_tensor(name + "_sq", [P, 2, D], F32))
        xn = tmp.enter_context(nc.sbuf_tensor(name + "_xn", [P, n_tile, D], F32))
        ms = tmp.enter_context(nc.sbuf_tensor(name + "_ms", [P, n_tile], F32))
        rt = tmp.enter_context(nc.sbuf_tensor(name + "_rt", [P, n_tile], F32))
        rs = tmp.enter_context(nc.sbuf_tensor(name + "_rs", [P, n_tile], F32))
        acc = [tmp.enter_context(nc.psum_tensor(f"{name}_t{i}", [P, 4, P], F32)) for i in range(4)]
        tiles = [grp[0][:, j, :] for grp in groups for j in range(grp[1])]
        turns = [(grp, k) for grp in groups for k in range(KD)]
        base = [sum(x[1] for x in groups[:i]) for i in range(len(groups))]

        @block.scalar
        def _(act):
            for n, x in enumerate(tiles):
                if n >= 2:
                    act.wait_ge(squares, n - 1)
                nc.scalar.activation(junk[:, n % 2, :], x, ACT.Square, accum_out=ms[:, n:n + 1]).then_inc(squares, 1)
            act.wait_ge(meaned, 1)
            nc.scalar.activation(rt[:], ms[:], ACT.Sqrt).then_inc(rooted, 1)
            if hi is not None:
                g.stream.round_until(act, g.stream.taken + 2)
                for i, (grp, k) in enumerate(turns):
                    c = slice(grp[3], grp[3] + grp[1] * P)
                    act.wait_ge(written, i + 1)
                    nc.scalar.copy(hi[:, k, c], grp[2][:, k, c]).then_inc(rounded, 1)

        if hi is not None:
            @block.gpsimd
            def _(pool):
                g.stream.reduce_until(pool, g.stream.taken + 2)

        @block.vector
        def _(dve):
            dve.wait_ge(squares, n_tile)
            nc.vector.tensor_scalar(ms[:], ms[:], 1.0 / D, EPS, ALU.mult, ALU.add).then_inc(meaned, 1)
            dve.wait_ge(rooted, 1)
            step.link(dve, nc.vector.reciprocal(rs[:], rt[:]))
            for n, x in enumerate(tiles):
                nc.vector.tensor_scalar(xn[:, n, :], x, rs[:, n:n + 1], None, ALU.mult).then_inc(scaled, 1)
            def reduce(i):
                grp, k = turns[i]
                c = slice(grp[3], grp[3] + grp[1] * P)
                x = grp[2][:, k, c]
                dve.wait_ge(rounded, i + 1)
                nc.vector.tensor_tensor(lo[:, k, c], x, hi[:, k, c].bitcast(F32), ALU.subtract)

            for i, (grp, k) in enumerate(turns):
                _, nt, out, t0, scale, shift = grp
                if hi is not None and i >= 2:
                    reduce(i - 2)
                dve.wait_ge(turned, i + 1)
                order = "c (j p) -> c j p" if permuted else "c (p j) -> c j p"
                dst = out[:, k, t0:t0 + nt * P].rearrange(order, j=nt)
                src = acc[i % 4][:, 0:nt, :]
                if shift is None:
                    nc.vector.tensor_scalar(dst, src, scale(k), None, ALU.mult).then_inc(written, 1)
                else:
                    nc.vector.tensor_scalar(dst, src, scale(k), shift(k), ALU.mult, ALU.add).then_inc(written, 1)
            if hi is not None:
                reduce(len(turns) - 2)
                reduce(len(turns) - 1)

        @block.tensor
        def _(pe):
            for i, (grp, k) in enumerate(turns):
                b = base[groups.index(grp)]
                if k == 0:
                    pe.wait_ge(scaled, b + grp[1])
                if i >= 4:
                    pe.wait_ge(written, i - 3)
                for j in range(grp[1]):
                    last = nc.tensor.transpose(acc[i % 4][:, j, :], xn[:, b + j, k * P:(k + 1) * P], g.ident[:])
                last.then_inc(turned, 1)


def retention_inputs(nc, g, hT, q_tok, k_tok, v_tok, gates, rope):
    sem, st = g.sem, g.stream
    p0 = st.taken
    n_panel = RET_COLS // PW
    emptied = sem("ret_banks_emptied")
    gated = sem("ret_gates_emptied")
    step = Tally(sem("ret_rope_steps"))
    with ExitStack() as tmp, nc.Block() as block:
        acc = [tmp.enter_context(nc.psum_tensor(f"ret_in{i}", [P, 512], F32)) for i in range(6)]
        prod = [tmp.enter_context(nc.sbuf_tensor(f"ret_rope{i}", [P, NT, RET_H, 32], F32)) for i in range(2)]

        def tiles(n):
            return range(NTC, NTC + NT) if n < 2 else range(NTC + NT)

        @block.sync
        def _(sp):
            st.load_until(sp, p0 + n_panel + SLOTS)

        @block.tensor
        def _(pe):
            for n in range(6):
                w = st.take_split(pe)
                if n >= 2:
                    pe.wait_ge(emptied, n - 1)
                for i, t in enumerate(tiles(n)):
                    dst = acc[3 * (n % 2) + i // 2][:, (i % 2) * PW:(i % 2 + 1) * PW]
                    last = dense(nc, dst, lambda a, k: hT[a][:, k, t * P:(t + 1) * P], lambda b, k: w[b][:, k, :])
                last.then_inc(st.used, 1)
            for n in range(6, n_panel):
                w = st.take_split(pe)
                pe.wait_ge(emptied, min(n - 1, 6))
                if n >= 8:
                    pe.wait_ge(gated, n - 7)
                for h in range(2):
                    last = dense(nc, acc[3 * (n % 2) + h][:], lambda a, k: w[a][:, k, h * P:(h + 1) * P],
                                 lambda b, k: hT[b][:, k, TC:TA])
                last.then_inc(st.used, 1)

        def rotate(dve, x):
            v = x[:, :, :].rearrange("p t (h d) -> p t h d", d=HD)
            x1, x2 = v[:, :, :, 0:32], v[:, :, :, 32:64]
            cos, sin = (rope[:, i].unsqueeze(2).to_broadcast([P, NT, RET_H, 32]) for i in range(2))
            step.mark(nc.vector.tensor_tensor(prod[0][:], x1, sin, ALU.mult))
            step.mark(nc.vector.tensor_tensor(prod[1][:], x2, sin, ALU.mult))
            step.settle(dve)
            step.mark(nc.vector.tensor_tensor(x1, x1, cos, ALU.mult))
            step.mark(nc.vector.tensor_tensor(x2, x2, cos, ALU.mult))
            step.settle(dve)
            step.mark(nc.vector.tensor_tensor(x1, x1, prod[1][:], ALU.subtract))
            step.mark(nc.vector.tensor_tensor(x2, x2, prod[0][:], ALU.add))
            step.settle(dve)

        @block.vector
        def _(dve):
            for n in range(6):
                dve.wait_ge(st.used, p0 + n + 1)
                ts = list(tiles(n))
                c = slice((n % 2) * PW, (n % 2 + 1) * PW)
                for i in range(0, len(ts), 2):
                    src = acc[3 * (n % 2) + i // 2][:].rearrange("p (t c) -> p t c", t=2)
                    dst = (q_tok[:, ts[i] - NTC:ts[i] - NTC + 2, c] if n < 2 else (k_tok if n < 4 else v_tok)[:, ts[i]:ts[i] + 2, c])
                    last = nc.vector.tensor_copy(dst, src)
                last.then_inc(emptied, 1)
                if n in (1, 3):
                    dve.wait_ge(emptied, n + 1)
                    rotate(dve, q_tok if n == 1 else k_tok[:, NTC:, :])

        @block.gpsimd
        def _(pool):
            st.reduce_until(pool, p0 + n_panel)

        @block.scalar
        def _(act):
            st.round_until(act, p0 + 8)
            for n in range(6, n_panel):
                act.wait_ge(st.used, p0 + n + 1)
                st.round_until(act, min(p0 + n + 3, p0 + n_panel))
                for h in range(2):
                    last = nc.scalar.activation(gates[:, 2 * (n - 6) + h, :], acc[3 * (n % 2) + h][:], ACT.Silu)
                last.then_inc(gated, 1)


def retention_turn(nc, g, q_tok, k_tok, qT, kT):
    sem = g.sem
    turned = sem("ret_turned")
    written = sem("ret_turn_written")
    jobs = [(x, hp) for hp in range(4) for x in "qkc"]
    with ExitStack() as tmp, nc.Block() as block:
        acc = [tmp.enter_context(nc.psum_tensor(f"ret_t{i}", [P, 4, P], F32)) for i in range(4)]

        @block.tensor
        def _(pe):
            for n, (x, hp) in enumerate(jobs):
                if n >= 4:
                    pe.wait_ge(written, n - 3)
                for t in range(NTC if x == "c" else NT):
                    src = q_tok[:, t] if x == "q" else k_tok[:, t if x == "c" else NTC + t]
                    last = nc.tensor.transpose(acc[n % 4][:, t, :], src[:, hp * P:(hp + 1) * P], g.ident[:])
                last.then_inc(turned, 1)

        @block.vector
        def _(dve):
            for n, (x, hp) in enumerate(jobs):
                dve.wait_ge(turned, n + 1)
                if x == "q":
                    ins = nc.vector.tensor_copy(qT[:, hp, :], acc[n % 4][:].rearrange("p t c -> p (t c)"))
                else:
                    nt, t0 = (NTC, 0) if x == "c" else (NT, TC)
                    ins = nc.vector.tensor_scalar(kT[:, hp, t0:t0 + nt * P], acc[n % 4][:, 0:nt, :].rearrange("p t c -> p (t c)"),
                                                  HD ** -0.5, None, ALU.mult)
                ins.then_inc(written, 1)


def retention(nc, g, qT, kT, v_tok, gates, dist, latT):
    sem = g.sem
    strips_ready = sem("ret_strips_ready")
    scored = sem("ret_scored")
    decayed = sem("ret_decayed")
    applied = sem("ret_applied")
    squared = sem("ret_squared")
    summed = sem("ret_sums_ready")
    meaned = sem("ret_mean_ready")
    rooted = sem("ret_root_ready")
    normed = sem("ret_normed")
    step = Tally(sem("ret_norm_steps"))
    jobs = [(h, j) for h in range(RET_H) for j in range(NTC + NT)]
    per_pair = 2 * (NTC + NT)
    lg = [float(np.log1p(-np.exp2(-5.0 - h))) for h in range(RET_H)]
    with ExitStack() as tmp, nc.Block() as block:
        strip = tmp.enter_context(nc.sbuf_tensor("ret_strip", [P, 2, 2, TA], F32))
        dec = tmp.enter_context(nc.sbuf_tensor("ret_decayed_scores", [P, 2, 2, T], F32))
        sq = tmp.enter_context(nc.sbuf_tensor("ret_sq", [P, 2, T], F32))
        rt = tmp.enter_context(nc.sbuf_tensor("ret_rt", [P, 2, T], F32))
        sc = [tmp.enter_context(nc.psum_tensor(f"ret_s{i}", [P, T], F32)) for i in range(3)]
        y = [[tmp.enter_context(nc.psum_tensor(f"ret_y{i}{d}", [P, T], F32)) for d in range(2)] for i in range(2)]
        ms = tmp.enter_context(nc.psum_tensor("ret_ms", [P, T], F32))

        def span(j, d):
            if j < NTC:
                return 0, T, (TC - P * j if d == 0 else P - P * j)
            t = j - NTC
            return (P * t, T, 0) if d == 0 else (0, P * (t + 1), 640 - P * t)

        @block.gpsimd
        def _(pool):
            g.stream.reduce_until(pool, g.stream.taken + 2)

        @block.scalar
        def _(act):
            g.stream.round_until(act, g.stream.taken + 2)

            def strips(h):
                if h >= 2:
                    act.wait_ge(decayed, (NTC + NT) * (h - 1))
                for d in range(2):
                    last = nc.scalar.activation(strip[:, h % 2, d, :], dist[:, d, :], ACT.Exp, scale=lg[h])
                last.then_inc(strips_ready, 1)

            def squares(hp):
                act.wait_ge(applied, per_pair * (hp + 1))
                for d in range(2):
                    if hp >= 1:
                        act.wait_ge(summed, 2 * (hp - 1) + d + 1)
                    nc.scalar.activation(sq[:, d, :], y[hp % 2][d][:], ACT.Square).then_inc(squared, 1)

            def roots(hp):
                for d in range(2):
                    act.wait_ge(meaned, 2 * hp + d + 1)
                    nc.scalar.activation(rt[:, d, :], rt[:, d, :], ACT.Sqrt).then_inc(rooted, 1)

            for hp in range(4):
                strips(2 * hp)
                if hp:
                    squares(hp - 1)
                strips(2 * hp + 1)
                if hp:
                    roots(hp - 1)
            squares(3)
            roots(3)

        @block.tensor
        def _(pe):
            def score(n):
                h, j = jobs[n]
                e = slice(HD * (h % 2), HD * (h % 2 + 1))
                if n >= 3:
                    pe.wait_ge(decayed, n - 2)
                nc.tensor.matmul(sc[n % 3][:], kT[e, h // 2, j * P:(j + 1) * P], qT[e, h // 2, :],
                                 start=True, stop=True).then_inc(scored, 1)

            def apply(n):
                h, j = jobs[n]
                e = slice(HD * (h % 2), HD * (h % 2 + 1))
                hp = h // 2
                if n % per_pair == 0 and hp >= 2:
                    pe.wait_ge(normed, 2 * (hp - 1))
                pe.wait_ge(decayed, n + 1)
                for d in range(2):
                    i0, i1, _ = span(j, d)
                    last = nc.tensor.matmul(y[hp % 2][d][e, i0:i1], v_tok[:, j, h * HD:(h + 1) * HD], dec[:, n % 2, d, i0:i1],
                                            start=(j == 0), stop=(j == NTC + NT - 1))
                last.then_inc(applied, 1)

            def sums(hp, d):
                pe.wait_ge(squared, 2 * hp + d + 1)
                if 2 * hp + d >= 1:
                    pe.wait_ge(meaned, 2 * hp + d)
                nc.tensor.matmul(ms[:], g.headsum[:], sq[:, d, :], start=True, stop=True).then_inc(summed, 1)

            score(0)
            for n in range(len(jobs)):
                if n + 1 < len(jobs):
                    score(n + 1)
                apply(n)
                if n >= per_pair and n % per_pair in (3, 7):
                    sums(n // per_pair - 1, 0 if n % per_pair == 3 else 1)
            sums(3, 0)
            sums(3, 1)

        @block.vector
        def _(dve):
            def decay(n):
                h, j = jobs[n]
                if j == 0:
                    dve.wait_ge(strips_ready, h + 1)
                if n >= 2:
                    dve.wait_ge(applied, n - 1)
                dve.wait_ge(scored, n + 1)
                for d in range(2):
                    i0, i1, x0 = span(j, d)
                    last = nc.vector.tensor_tensor(dec[:, n % 2, d, i0:i1], sc[n % 3][:, i0:i1],
                                                   strip[:, h % 2, d, x0:x0 + i1 - i0], ALU.mult)
                last.then_inc(decayed, 1)

            def norm(hp, d):
                dve.wait_ge(summed, 2 * hp + d + 1)
                nc.vector.tensor_scalar(rt[:, d, :], ms[:], 1.0 / HD, EPS, ALU.mult, ALU.add).then_inc(meaned, 1)
                dve.wait_ge(rooted, 2 * hp + d + 1)
                part = gates[:, 4 * d + hp, :]
                step.link(dve, nc.vector.reciprocal(rt[:, d, :], rt[:, d, :]))
                step.link(dve, nc.vector.tensor_tensor(part, part, rt[:, d, :], ALU.mult))
                nc.vector.tensor_tensor(part, part, y[hp % 2][d][:], ALU.mult).then_inc(normed, 1)
                if d == 1:
                    dve.wait_ge(normed, 2 * hp + 2)
                    dst = latT[:, hp, :].rearrange("c (j p) -> c p j", j=NT)
                    f, b = (gates[:, 4 * i + hp, :].rearrange("c (p j) -> c p j", j=NT) for i in range(2))
                    step.link(dve, nc.vector.tensor_tensor(dst, f, b, ALU.add))

            for n in range(len(jobs)):
                decay(n)
                if n >= per_pair and n % per_pair in (5, 9):
                    norm(n // per_pair - 1, 0 if n % per_pair == 5 else 1)
            norm(3, 0)
            norm(3, 1)


def conv_taps(g, idx):
    return [g.cols[:, g.col[f"conv{t}"] + idx:g.col[f"conv{t}"] + idx + 1] for t in range(3)]


def conv(nc, dve, step, g, idx, out, parts, n=P):
    w = [x[0:n] for x in conv_taps(g, idx)]
    for src, t0, ln in parts:
        step.mark(nc.vector.tensor_scalar(out[0:n, t0:t0 + ln], src[0:n], w[1], None, ALU.mult))
    step.settle(dve)
    for src, t0, ln in parts:
        d = out[0:n, t0 + 1:t0 + ln]
        step.mark(nc.vector.scalar_tensor_tensor(d, src[0:n, 0:ln - 1], w[0], d, ALU.mult, ALU.add))
    step.settle(dve)
    for src, t0, ln in parts:
        d = out[0:n, t0:t0 + ln - 1]
        step.mark(nc.vector.scalar_tensor_tensor(d, src[0:n, 1:ln], w[2], d, ALU.mult, ALU.add))
    step.settle(dve)


def rwkv_low(nc, g, hT, wl, al, gl):
    sem, st = g.sem, g.stream
    p0 = st.taken
    step = Tally(sem("rw_low_steps"))
    with ExitStack() as tmp, nc.Block() as block:
        acc = [tmp.enter_context(nc.psum_tensor(f"rw_low{i}", [P, T], F32)) for i in range(5)]

        @block.sync
        def _(sp):
            st.load_until(sp, p0 + 2 + SLOTS)

        @block.tensor
        def _(pe):
            w = st.take_split(pe)
            for dst, c, n in ((0, slice(0, P), P), (2, slice(P, P + 64), 64)):
                dense(nc, acc[dst][0:n, :], lambda a, k: w[a][:, k, c], lambda b, k: hT[b][:, k, TC:])
                last = dense(nc, acc[1][0:n, dst * P:dst * P + TC], lambda a, k: w[a][:, k, c], lambda b, k: hT[b][:, k, 0:TC])
            last.then_inc(st.used, 1)
            w = st.take_split(pe)
            for d in range(2):
                last = dense(nc, acc[3 + d][:], lambda a, k: w[a][:, k, d * P:(d + 1) * P], lambda b, k: hT[b][:, k, TC:])
            last.then_inc(st.used, 1)

        @block.vector
        def _(dve):
            dve.wait_ge(st.used, p0 + 1)
            conv(nc, dve, step, g, 12, wl, [(acc[0][:], TC, T), (acc[1][:, 0:TC], 0, TC)])
            conv(nc, dve, step, g, 13, al, [(acc[2][:], TC, T), (acc[1][:, TC:T], 0, TC)], 64)
            dve.wait_ge(st.used, p0 + 2)
            for d in range(2):
                conv(nc, dve, step, g, 14 + d, gl[:, d], [(acc[3 + d][:], 0, T)])

        @block.gpsimd
        def _(pool):
            st.reduce_until(pool, p0 + 4)

        @block.scalar
        def _(act):
            st.round_until(act, p0 + 2)
            act.wait_ge(step.sem, 12)
            nc.scalar.activation(wl[:], wl[:], ACT.Tanh)
            act.wait_ge(step.sem, 18)
            nc.scalar.activation(gl[:], gl[:], ACT.Sigmoid)
            st.round_until(act, p0 + 4)


def rwkv_prepare(nc, g, hp, hT, f, low, par, restart):
    sem, st = g.sem, g.stream
    p0 = st.taken
    nm = f"rw{hp}_"
    NB = TA // P
    low_done = sem(nm + "decay_logits")
    sig_done = sem(nm + "sigmoids")
    sq_ready = sem(nm + "k_squared")
    sums_done = sem(nm + "head_sums")
    eps_done = sem(nm + "norm_sum_copied")
    root_done = sem(nm + "norm_rooted")
    exps_in = sem(nm + "exponents")
    exps_out = sem(nm + "exps")
    bonus_in = sem(nm + "bonus_terms")
    keys_ready = sem(nm + "keys_ready")
    half_scaled = sem(nm + "pool_scaled")
    step = Tally(sem(nm + "prep_steps"))
    col = lambda name, i=hp: g.cols[:, g.col[name] + i:g.col[name] + i + 1]
    hc = slice(hp * P, (hp + 1) * P)
    blocks = lambda x: x.rearrange("c (b t) -> c b t", t=P)
    with ExitStack() as tmp, nc.Block() as block:
        t_ = lambda n, w=TA: tmp.enter_context(nc.sbuf_tensor(nm + n, [P, w], F32))
        r, k, kk, ic, cs = t_("r", T), t_("k"), t_("kk"), t_("ic"), t_("cs")
        sg = [t_(f"sg{d}") for d in range(2)]
        ex = [t_("ex0")[:], t_("ex1")[:], f.Y[:].rearrange("c d t -> c (d t)")[:, 0:TA]]
        km, bn = k, ic
        sq = sg[0]
        less, terms = f.Kh[:, 0], f.Bh[:, 0, 0:T]
        acc = [tmp.enter_context(nc.psum_tensor(f"{nm}p{i}", [P, T], F32)) for i in range(8)]

        @block.sync
        def _(sp):
            st.load_until(sp, p0 + 2 + SLOTS)

        @block.tensor
        def _(pe):
            lat, ctx = slice(TC, TA), slice(0, TC)
            for d in range(2):
                e = slice(64 * d, 64 * (d + 1))
                nc.tensor.matmul(acc[4 + 2 * d][:], par.w2[e, hc], low.wl[e, lat], start=True, stop=True)
                nc.tensor.matmul(acc[5 + 2 * d][:, 0:TC], par.w2[e, hc], low.wl[e, ctx], start=True, stop=True).then_inc(low_done, 1)
            w = st.take_split(pe)

            def project(dst, c, tokens):
                return dense(nc, dst, lambda a, k: w[a][:, k, c], lambda b, k: hT[b][:, k, tokens])
            project(acc[0][:], slice(0, P), lat)
            project(acc[1][:], slice(P, 2 * P), lat)
            project(acc[2][:, 0:TC], slice(P, 2 * P), ctx).then_inc(st.used, 1)
            w = st.take_split(pe)
            project(acc[3][:], slice(0, P), lat)
            pe.wait_ge(step.sem, 8)
            project(acc[2][:, TC:T], slice(0, P), ctx).then_inc(st.used, 1)
            pe.wait_ge(sig_done, 2)
            nc.tensor.matmul(acc[4][:], par.a2[0:64, hc], low.al[0:64, lat], start=True, stop=True)
            nc.tensor.matmul(acc[5][:, 0:TC], par.a2[0:64, hc], low.al[0:64, ctx], start=True, stop=True).then_inc(low_done, 1)
            pe.wait_ge(sq_ready, 1)
            nc.tensor.matmul(acc[6][:], g.headsum[:], sq[:, lat], start=True, stop=True)
            nc.tensor.matmul(acc[7][:, 0:TC], g.headsum[:], sq[:, ctx], start=True, stop=True).then_inc(sums_done, 1)
            pe.wait_ge(bonus_in, 1)
            nc.tensor.matmul(acc[0][:], g.headsum[:], terms, start=True, stop=True).then_inc(sums_done, 1)

        @block.scalar
        def _(act):
            lat, ctx = slice(TC, TA), slice(0, TC)
            for d in range(2):
                act.wait_ge(low_done, d + 1)
                nc.scalar.activation(sg[d][:, lat], acc[4 + 2 * d][:], ACT.Sigmoid, bias=col("w0", 4 * d + hp))
                nc.scalar.activation(sg[d][:, ctx], acc[5 + 2 * d][:, 0:TC], ACT.Sigmoid,
                                     bias=col("w0", 4 * d + hp)).then_inc(sig_done, 1)
            st.round_until(act, p0 + 2)

            def exps(d):
                end, mid = (P - 1, P // 2 - 1) if d == 0 else (0, P // 2)
                b3 = blocks(cs[:])
                act.wait_ge(exps_in, d + 1)
                nc.scalar.activation(ex[1], ex[0], ACT.Exp, scale=DECAY).then_inc(exps_out, 1)
                nc.scalar.activation(ex[2], ex[2], ACT.Exp, scale=-DECAY).then_inc(exps_out, 1)
                act.wait_ge(exps_out, 4 * d + 1)
                nc.scalar.activation(ex[0], ex[0], ACT.Exp, scale=-DECAY).then_inc(exps_out, 1)
                nc.scalar.activation(f.pc[:, d, :].unsqueeze(2), b3[:, :, end:end + 1], ACT.Exp, scale=-DECAY)
                nc.scalar.activation(f.pm[:, d, :].unsqueeze(2), b3[:, :, mid:mid + 1], ACT.Exp, scale=-DECAY)
                nc.scalar.activation(f.pn[:, d, :].unsqueeze(2), b3[:, :, mid:mid + 1], ACT.Exp, scale=DECAY).then_inc(exps_out, 1)

            exps(0)
            act.wait_ge(low_done, 3)
            nc.scalar.activation(ic[:, lat], acc[4][:], ACT.Sigmoid, bias=col("a0"))
            nc.scalar.activation(ic[:, ctx], acc[5][:, 0:TC], ACT.Sigmoid, bias=col("a0")).then_inc(sig_done, 1)
            act.wait_ge(eps_done, 1)
            nc.scalar.activation(sq[:], sq[:], ACT.Sqrt).then_inc(root_done, 1)
            exps(1)

        @block.gpsimd
        def _(pool):
            st.reduce_until(pool, p0 + 2)
            pool.wait_ge(keys_ready, 1)
            for d in range(2):
                pool.wait_ge(exps_out, 4 * d + 1)
                nc.gpsimd.tensor_tensor(f.Kh[:, d], km[:], ex[1], ALU.mult)
                pool.wait_ge(exps_out, 4 * d + 2)
                nc.gpsimd.tensor_tensor(f.A[:, d], kk[:], ex[2], ALU.mult).then_inc(half_scaled, 1)

        @block.vector
        def _(dve):
            lat, ctx = slice(TC, TA), slice(0, TC)
            V = nc.vector

            def accumulate(d):
                o = slice(None, None, 1 if d == 0 else -1)
                mid = P // 2 - 1 if d == 0 else P // 2
                step.link(dve, V.tensor_tensor_scan(cs[:, o], restart[:], sg[d][:, o], 0.0, ALU.mult, ALU.add))
                b3 = blocks(cs[:])
                step.link(dve, V.tensor_tensor(blocks(ex[0]), b3, b3[:, :, mid:mid + 1].to_broadcast([P, NB, P]), ALU.subtract))
                V.tensor_tensor(ex[2], ex[0], sg[d][:], ALU.subtract).then_inc(exps_in, 1)

            dve.wait_ge(sig_done, 1)
            accumulate(0)
            dve.wait_ge(st.used, p0 + 1)
            conv(nc, dve, step, g, 4 + hp, k, [(acc[1][:], TC, T), (acc[2][:, 0:TC], 0, TC)])
            conv(nc, dve, step, g, hp, r, [(acc[0][:], 0, T)])
            step.link(dve, V.tensor_scalar(kk[:], k[:], col("k_k"), None, ALU.mult))
            dve.wait_ge(exps_in, 1)
            V.tensor_tensor(sq[:], kk[:], kk[:], ALU.mult).then_inc(sq_ready, 1)
            dve.wait_ge(sig_done, 3)
            step.link(dve, V.tensor_scalar(less, ic[:], 1.0, col("k_a"), ALU.subtract, ALU.mult))
            step.link(dve, V.scalar_tensor_tensor(km[:], less, 1.0, k[:], ALU.add, ALU.mult))
            V.scalar_tensor_tensor(terms, r[:], col("r_k"), km[:, lat], ALU.mult, ALU.mult).then_inc(bonus_in, 1)
            dve.wait_ge(sums_done, 1)
            V.tensor_copy(sq[:, lat], acc[6][:])
            V.tensor_copy(sq[:, ctx], acc[7][:, 0:TC]).then_inc(eps_done, 1)
            dve.wait_ge(st.used, p0 + 2)
            conv(nc, dve, step, g, 8 + hp, f.v, [(acc[3][:], TC, T), (acc[2][:, TC:T], 0, TC)])
            dve.wait_ge(root_done, 1)
            step.link(dve, V.tensor_scalar(sq[:], sq[:], 1e-12, None, ALU.max))
            step.link(dve, V.reciprocal(sq[:], sq[:]))
            step.link(dve, V.tensor_tensor(kk[:], kk[:], sq[:], ALU.mult))
            V.scalar_tensor_tensor(bn[:], kk[:], -1.0, ic[:], ALU.mult, ALU.mult).then_inc(keys_ready, 1)
            dve.wait_ge(sums_done, 2)
            step.mark(V.tensor_tensor(f.bonus[:], acc[0][:], f.v[:, lat], ALU.mult))
            dve.wait_ge(keys_ready, 1)
            for d in range(2):
                if d:
                    dve.wait_ge(half_scaled, 1)
                    step.settle(dve)
                    accumulate(1)
                dve.wait_ge(exps_out, 4 * d + 1)
                step.mark(V.tensor_tensor(f.Bh[:, d], bn[:], ex[1], ALU.mult))
                dve.wait_ge(exps_out, 4 * d + 3)
                step.mark(V.tensor_tensor(f.R[:, d], r[:], ex[0][:, lat], ALU.mult))
                dve.wait_ge(exps_out, 4 * d + 4)
                step.link(dve, V.tensor_tensor(f.pe[:, d], f.pc[:, d], f.pn[:, d], ALU.mult))


def rwkv_scan(nc, g, hp, f, tri):
    sem = g.sem
    nm = f"rws{hp}_"
    LV = 6
    pe_done = [sem(nm + f"pe_jobs{x}") for x in range(2)]
    dve_done = [sem(nm + f"dve_jobs{x}") for x in range(2)]
    act_done = [sem(nm + f"act_jobs{x}") for x in range(2)]
    pool_done = [sem(nm + f"masks{x}") for x in range(2)]
    step = Tally(sem(nm + "steps"))
    back = [1, 0, 5, 4, 3, 2]
    top = LV - 1
    pe_levels = [j for lv in range(1, top) for j in (f"T{lv}", f"M{lv}", f"N{lv}")] + [f"T{top}", f"N{top}"]
    early = ["TA", "TK"]
    pe_jobs = {lat: early + ["SA"] + ["SR"] * lat + ["M0", "AKV"] + pe_levels + ["XA", "Z", "X", "GR"] + ["Y"] * lat + ["S"]
               for lat in (False, True)}
    dve_jobs = {lat: ["SA", "MT"] + ["SR"] * lat + [j for j in pe_levels if j[0] != "T"] + ["X", "GR", "S"] for lat in (False, True)}
    act_jobs = {lat: early + ["M0", "AKV"] + [f"T{lv}" for lv in range(1, LV)] + ["XA", "Z"] + ["Y"] * lat for lat in (False, True)}

    def upto(jobs, n, name):
        return sum(len(jobs[m >= NTC]) for m in range(n % 2, n, 2)) + jobs[n >= NTC].index(name) + 1

    with ExitStack() as tmp, nc.Block() as block:
        two = lambda n, shape: [tmp.enter_context(nc.sbuf_tensor(f"{nm}{n}{x}", [P] + shape, F32)) for x in range(2)]
        AK, M = (two(n, [4, P]) for n in ("AK", "M"))
        T1 = AK
        spare = g.weight_spare[:].rearrange("p (b x c t) -> p b x c t", b=4, x=2, c=4)
        AT, RB, RK, MT = ([spare[:, b, x] for x in range(2)] for b in range(4))
        ET = [two(f"ET{i}", [4, P]) for i in range(2)]
        W = two("W", [4, P])
        X = AT
        Bt, Kt, Vt = (two(n, [4, HD]) for n in ("Bt", "Kt", "Vt"))
        GT = [m[:, 0].rearrange("p (d k) -> p d k", d=2) for m in M]
        Rp = [m[:, 1:3] for m in M]
        Sc = tmp.enter_context(nc.sbuf_tensor(nm + "Sc", [P, 2, HD], F32))
        bank = [[tmp.enter_context(nc.psum_tensor(f"{nm}q{x}{i}", [P, 512], F32)) for i in range(4)] for x in range(2)]
        four = lambda b: b[:].rearrange("p (c t) -> p c t", c=4)
        as4 = lambda b: b[:].rearrange("p (d h) t -> p d h t", d=2)
        mask = lambda i: tri[:, i].unsqueeze(2).to_broadcast([P, 2, 2, P])
        tok = lambda n, d: slice(P * (n if d == 0 else back[n]), P * (n if d == 0 else back[n]) + P)
        ltok = lambda n, d: slice(tok(n, d).start - TC, tok(n, d).stop - TC)
        head = lambda h: slice(HD * h, HD * (h + 1))
        chains = [(2 * d + h, d, h) for d in range(2) for h in range(2)]

        @block.tensor
        def _(pe):
            mm = nc.tensor.matmul

            def run(name, n):
                x, lat = n % 2, n >= NTC
                q = bank[x]
                need_dve = lambda job, m=n: pe.wait_ge(dve_done[x], upto(dve_jobs, m, job))
                need_act = lambda job, m=n: pe.wait_ge(act_done[x], upto(act_jobs, m, job))
                if name in ("SA", "SR"):
                    if name == "SR":
                        need_dve("SA")
                    elif n >= 2:
                        need_dve("S", n - 2)
                    for c, d, h in chains:
                        rhs = f.A[head(h), d, tok(n, d)] if name == "SA" else f.R[head(h), d, ltok(n, d)]
                        for i, lhs in enumerate((f.Bh, f.Kh)):
                            last = mm(four(q[h])[:, 2 * i + d], lhs[head(h), d, tok(n, d)], rhs, start=True, stop=True)
                elif name == "TA":
                    if n >= 2:
                        need_dve(f"N{top}", n - 2)
                        if n - 2 >= NTC:
                            need_act("Y", n - 2)
                    for i, src in enumerate((f.A, f.Bh)):
                        for d in range(2):
                            last = nc.tensor.transpose(four(q[2])[:, 2 * i + d], src[:, d, tok(n, d)], g.ident[:])
                elif name == "TK":
                    if n >= 2:
                        need_dve("X", n - 2)
                    for d in range(2):
                        nc.tensor.transpose(four(q[3])[:, d], f.Kh[:, d, tok(n, d)], g.ident[:])
                        last = nc.tensor.transpose(four(q[3])[:, 2 + d], f.v[:, tok(n, d)], g.ident[:])
                elif name == "M0":
                    need_dve("MT")
                    need_act("TA")
                    for c, d, h in chains:
                        last = nc.tensor.transpose(four(q[2])[:, c], MT[x][:, c], g.ident[:])
                elif name == "AKV":
                    need_dve("SA")
                    need_act("TK")
                    for c, d, h in chains:
                        last = mm(q[3][:, c * HD:(c + 1) * HD], AK[x][:, c], Vt[x][:, c], start=True, stop=True)
                elif name[0] == "T":
                    lv = int(name[1])
                    pe.wait_ge(pool_done[x], LV * (n // 2) + lv)
                    if lv == 1:
                        need_act("M0")
                        need_dve("SR" if lat else "SA")
                    else:
                        need_dve(f"M{lv - 1}")
                        need_act(f"T{lv - 1}")
                    for c, d, h in chains:
                        last = mm(four(q[0])[:, c], ET[lv % 2][x][:, c], M[x][:, c], start=True, stop=True)
                elif name[0] == "M":
                    lv = int(name[1])
                    need_act(f"T{lv}")
                    if lv == 1:
                        need_dve("SR" if lat else "MT")
                    else:
                        need_dve(f"N{lv - 1}")
                    for c, d, h in chains:
                        last = mm(four(q[1])[:, c], MT[x][:, c], T1[x][:, c], start=True, stop=True)
                elif name[0] == "N":
                    lv = int(name[1])
                    need_act(f"T{lv}")
                    if lv > 1:
                        need_dve(f"N{lv - 1}")
                    for c, d, h in chains:
                        last = mm(four(q[2])[:, c], T1[x][:, c], MT[x][:, c], start=True, stop=True)
                elif name == "XA":
                    need_dve(f"N{top}")
                    need_act("AKV")
                    for c, d, h in chains:
                        last = mm(four(q[3])[:, c], MT[x][:, c], W[x][:, c], start=True, stop=True)
                elif name == "Z":
                    pe.wait_ge(pool_done[x], LV * (n // 2) + LV)
                    need_act("XA")
                    for c, d, h in chains:
                        last = mm(four(q[0])[:, c], ET[LV % 2][x][:, c], X[x][:, c], start=True, stop=True)
                elif name == "X":
                    need_act("Z")
                    for c, d, h in chains:
                        last = mm(four(q[3])[:, c], MT[x][:, c], T1[x][:, c], start=True, stop=True)
                elif name == "GR":
                    need_dve("X")
                    need_act("Z")
                    for c, d, h in chains:
                        last = mm(q[0][head(h), d * HD:(d + 1) * HD], X[x][:, c, 0:HD], Bt[x][:, c], start=True, stop=True)
                        if lat:
                            last = mm(q[0][head(h), P + d * P:P + (d + 1) * P], X[x][:, c, 0:HD], RB[x][:, c], start=True, stop=True)
                elif name == "Y":
                    need_dve("GR")
                    pe.wait_ge(dve_done[1 - x], upto(dve_jobs, n - 1, "S"))
                    for c, d, h in chains:
                        dst = q[2][head(h), d * P:(d + 1) * P]
                        mm(dst, Sc[head(h), d], Rp[x][head(h), d], start=True, stop=False)
                        mm(dst, X[x][:, c, HD:P], RB[x][:, c], start=False, stop=False)
                        last = mm(dst, Vt[x][:, c], RK[x][:, c], start=False, stop=True)
                elif name == "S":
                    need_dve("GR")
                    if n:
                        pe.wait_ge(dve_done[1 - x], upto(dve_jobs, n - 1, "S"))
                    else:
                        pe.wait_ge(step.sem, 1)
                    for c, d, h in chains:
                        dst = q[1][head(h), d * HD:(d + 1) * HD]
                        mm(dst, Bt[x][:, c], X[x][:, c, HD:P], start=True, stop=False)
                        mm(dst, Kt[x][:, c], Vt[x][:, c], start=False, stop=False)
                        last = mm(dst, GT[x][head(h), d], Sc[head(h), d], start=False, stop=True)
                last.then_inc(pe_done[x], 1)

            for n in range(2):
                for job in early:
                    run(job, n)
            for n in range(0, TA // P, 2):
                jobs = pe_jobs[n >= NTC]
                tail = jobs.index("GR") + 1
                for job in jobs[len(early):tail]:
                    run(job, n)
                    run(job, n + 1)
                for m in (n, n + 1):
                    for job in jobs[tail:]:
                        run(job, m)
                    if m + 2 < TA // P:
                        for job in early:
                            run(job, m + 2)

        @block.vector
        def _(dve):
            V = nc.vector
            step.mark(V.memset(Sc[:], 0.0))

            def run(name, n):
                x, lat = n % 2, n >= NTC
                q = bank[x]
                own = lambda job: dve.wait_ge(dve_done[x], upto(dve_jobs, n, job))
                if name == "MT":
                    own("SA")
                    step.link(dve, V.tensor_tensor(as4(MT[x]), as4(AT[x]), mask(2), ALU.mult))
                    last = V.tensor_tensor(MT[x][:], MT[x][:], g.ident[:].unsqueeze(1).to_broadcast([P, 4, P]), ALU.add)
                    last.then_inc(dve_done[x], 1)
                    return
                dve.wait_ge(pe_done[x], upto(pe_jobs, n, name))
                if name in ("SA", "SR"):
                    for i, dst in enumerate((AT, AK) if name == "SA" else (RB, RK)):
                        for h in range(2):
                            last = V.tensor_tensor(as4(dst[x])[:, :, h], four(q[h])[:, 2 * i:2 * i + 2], tri[:, 0 if name == "SA" else 1], ALU.mult)
                elif name[0] in "MN":
                    lv = int(name[1])
                    buf = M if name[0] == "M" else MT
                    if lv > 1:
                        own(f"{name[0]}{lv - 1}")
                    else:
                        own("MT")
                    last = V.tensor_tensor(buf[x][:], buf[x][:], four(q[1 if name[0] == "M" else 2]), ALU.add)
                elif name == "X":
                    last = V.tensor_tensor(X[x][:], X[x][:], four(q[3]), ALU.add)
                elif name == "GR":
                    last = V.tensor_copy(GT[x], q[0][:, 0:2 * HD].rearrange("p (d k) -> p d k", d=2))
                    if lat:
                        for d in range(2):
                            last = V.tensor_tensor(Rp[x][:, d], q[0][:, P + d * P:P + (d + 1) * P], f.R[:, d, ltok(n, d)], ALU.add)
                elif name == "S":
                    if n:
                        dve.wait_ge(dve_done[1 - x], upto(dve_jobs, n - 1, "S"))
                    else:
                        step.settle(dve)
                    step.link(dve, V.tensor_tensor(Sc[:], Sc[:], q[1][:, 0:2 * HD].rearrange("p (d k) -> p d k", d=2), ALU.add))
                    for d in range(2):
                        m = min(n + 1, TA // P - 1)
                        b, b1 = tok(n, d).start // P, tok(m, d).start // P
                        last = V.tensor_scalar(Sc[:, d], Sc[:, d], f.pe[:, d, b:b + 1], f.pm[:, d, b1:b1 + 1], ALU.mult, ALU.mult)
                last.then_inc(dve_done[x], 1)

            for n in range(0, TA // P, 2):
                for job in dve_jobs[n >= NTC]:
                    run(job, n)
                    run(job, n + 1)

        @block.scalar
        def _(act):
            def run(name, n):
                x = n % 2
                q = bank[x]
                quarters = lambda b: b.rearrange("p (c k) -> p c k", k=HD)
                act.wait_ge(pe_done[x], upto(pe_jobs, n, name))
                if name == "TA":
                    nc.scalar.copy(W[x][:, :, 0:HD], quarters(q[2][:, 0:2 * P]))
                    last = nc.scalar.copy(Bt[x][:], quarters(q[2][:, 2 * P:]))
                elif name == "TK":
                    nc.scalar.copy(Kt[x][:], quarters(q[3][:, 0:2 * P]))
                    last = nc.scalar.copy(Vt[x][:], quarters(q[3][:, 2 * P:]))
                elif name == "M0":
                    last = nc.scalar.copy(M[x][:], four(q[2]))
                elif name == "AKV":
                    last = nc.scalar.copy(W[x][:, :, HD:P], quarters(q[3][:, 0:2 * P]))
                elif name == "XA":
                    act.wait_ge(pool_done[x], LV * (n // 2) + LV)
                    last = nc.scalar.copy(X[x][:], four(q[3]))
                elif name == "Y":
                    for d in range(2):
                        last = nc.scalar.copy(f.Y[:, d, ltok(n, d)], q[2][:, d * P:(d + 1) * P])
                else:
                    last = nc.scalar.copy(T1[x][:], four(q[0]))
                last.then_inc(act_done[x], 1)

            for n in range(2):
                for job in early:
                    run(job, n)
            for n in range(0, TA // P, 2):
                jobs = act_jobs[n >= NTC]
                tail = jobs.index("Z") + 1
                for job in jobs[len(early):tail]:
                    run(job, n)
                    run(job, n + 1)
                for m in (n, n + 1):
                    for job in jobs[tail:]:
                        run(job, m)
                    if m + 2 < TA // P:
                        for job in early:
                            run(job, m + 2)

        @block.gpsimd
        def _(pool):
            for n in range(0, TA // P, 2):
                for lv in range(1, LV + 1):
                    for m in (n, n + 1):
                        x = m % 2
                        if lv == 1:
                            pool.wait_ge(dve_done[x], upto(dve_jobs, m, "SA"))
                        if lv >= 3:
                            pool.wait_ge(pe_done[x], upto(pe_jobs, m, f"T{lv - 2}"))
                        nc.gpsimd.tensor_tensor(as4(ET[lv % 2][x]), as4(AT[x]), mask(2 + lv), ALU.mult).then_inc(pool_done[x], 1)


def rwkv_out(nc, g, hp, f, low, par, latT):
    sem = g.sem
    nm = f"rwo{hp}_"
    sums = sem(nm + "sums")
    centred = sem(nm + "centred")
    squared = sem(nm + "squared")
    vared = sem(nm + "var_ready")
    rooted = sem(nm + "rooted")
    step = Tally(sem(nm + "steps"))
    col = lambda name: g.cols[:, g.col[name] + hp:g.col[name] + hp + 1]
    with ExitStack() as tmp, nc.Block() as block:
        yc = tmp.enter_context(nc.sbuf_tensor(nm + "yc", [P, 2, T], F32))
        sq = tmp.enter_context(nc.sbuf_tensor(nm + "sq", [P, 2, T], F32))
        rt = tmp.enter_context(nc.sbuf_tensor(nm + "rt", [P, 2, T], F32))
        g2 = tmp.enter_context(nc.sbuf_tensor(nm + "g2", [P, 2, P], F32))
        g2_loaded = sem(nm + "g2_loaded")
        acc = [tmp.enter_context(nc.psum_tensor(f"{nm}p{i}", [P, T], F32)) for i in range(6)]

        @block.sync
        def _(sp):
            sp.dma_start(g2[:], par.g2_rows[:, :, hp * P:(hp + 1) * P]).then_inc(g2_loaded, 16)

        @block.gpsimd
        def _(pool):
            g.stream.reduce_until(pool, g.stream.taken + 2)

        @block.tensor
        def _(pe):
            for d in range(2):
                nc.tensor.matmul(acc[d][:], g.headsum[:], f.Y[:, d], start=True, stop=True).then_inc(sums, 1)
            pe.wait_ge(g2_loaded, 16)
            for d in range(2):
                last = nc.tensor.matmul(acc[4 + d][:], g2[:, d], low.gl[:, d], start=True, stop=True)
                last.then_inc(sums, 1)
            for d in range(2):
                pe.wait_ge(squared, d + 1)
                nc.tensor.matmul(acc[2 + d][:], g.headsum[:], sq[:, d], start=True, stop=True).then_inc(sums, 1)

        @block.scalar
        def _(act):
            g.stream.round_until(act, g.stream.taken + 2)
            for d in range(2):
                act.wait_ge(centred, d + 1)
                nc.scalar.activation(sq[:, d], yc[:, d], ACT.Square).then_inc(squared, 1)
            for d in range(2):
                act.wait_ge(vared, d + 1)
                nc.scalar.activation(rt[:, d], rt[:, d], ACT.Sqrt).then_inc(rooted, 1)

        @block.vector
        def _(dve):
            V = nc.vector
            for d in range(2):
                dve.wait_ge(sums, d + 1)
                V.scalar_tensor_tensor(yc[:, d], acc[d][:], -1.0 / HD, f.Y[:, d], ALU.mult, ALU.add).then_inc(centred, 1)
            for d in range(2):
                dve.wait_ge(sums, 5 + d)
                V.tensor_scalar(rt[:, d], acc[2 + d][:], 1.0 / HD, GN_EPS, ALU.mult, ALU.add).then_inc(vared, 1)
            for d in range(2):
                dve.wait_ge(rooted, d + 1)
                step.link(dve, V.reciprocal(rt[:, d], rt[:, d]))
                step.link(dve, V.tensor_tensor(yc[:, d], yc[:, d], rt[:, d], ALU.mult))
                step.link(dve, V.tensor_scalar(yc[:, d], yc[:, d], col("lnx_w"), col("lnx_b"), ALU.mult, ALU.add))
                step.link(dve, V.tensor_tensor(yc[:, d], yc[:, d], f.bonus[:], ALU.add))
                step.link(dve, V.tensor_tensor(yc[:, d], yc[:, d], acc[4 + d][:], ALU.mult))
            dst = latT[:, 4 + hp, :].rearrange("c (j p) -> c p j", j=NT)
            a, b = (yc[:, d].rearrange("c (p j) -> c p j", j=NT) for d in range(2))
            step.link(dve, V.tensor_tensor(dst, a, b, ALU.add))


def row_vector(nc, g, name, out, col):
    diag_ready = g.sem(name + "_diag_ready")
    spread = g.sem(name + "_spread")
    with ExitStack() as tmp, nc.Block() as block:
        diag = tmp.enter_context(nc.sbuf_tensor(name + "_diag", [P, KD, P], F32))
        acc = tmp.enter_context(nc.psum_tensor(name + "_rows", [P, 2, 512], F32))

        @block.vector
        def _(dve):
            nc.vector.tensor_tensor(diag[:], g.ident[:].unsqueeze(1).to_broadcast([P, KD, P]),
                                    col.unsqueeze(2).to_broadcast([P, KD, P]), ALU.mult).then_inc(diag_ready, 1)
            dve.wait_ge(spread, 1)
            nc.vector.tensor_copy(out[:], acc[:].rearrange("p a b -> p (a b)"))

        @block.tensor
        def _(pe):
            pe.wait_ge(diag_ready, 1)
            for h in range(2):
                last = nc.tensor.matmul(acc[:, h], g.ones[:], diag[:, 4 * h:4 * h + 4].rearrange("p k c -> p (k c)"),
                                        start=True, stop=True)
            last.then_inc(spread, 1)


def project_rows(nc, g, name, xT, hi, lo, write):
    st = g.stream
    p0 = st.taken
    n_panel = D // PW
    emptied = g.sem(name + "_emptied")
    rounded = g.sem(name + "_rounded")
    reduced = g.sem(name + "_reduced")
    parts = (hi, lo)
    with ExitStack() as tmp, nc.Block() as block:
        acc = [[tmp.enter_context(nc.psum_tensor(f"{name}_o{s}{i}", [P, 2, PW], F32)) for i in range(2)] for s in range(2)]

        @block.sync
        def _(sp):
            st.load_until(sp, p0 + n_panel + SLOTS)

        @block.tensor
        def _(pe):
            pe.wait_ge(reduced, KD)
            for n in range(n_panel):
                w = st.take_split(pe)
                if n >= 2:
                    pe.wait_ge(emptied, n - 1)
                for j in range(NT):
                    last = dense(nc, acc[n % 2][j // 2][:, j % 2], lambda a, k: parts[a][:, k, j * P:(j + 1) * P],
                                 lambda b, k: w[b][:, k, :])
                last.then_inc(st.used, 1)

        @block.scalar
        def _(act):
            st.round_until(act, p0 + 1)
            for k in range(KD):
                nc.scalar.copy(hi[:, k], xT[:, k]).then_inc(rounded, 1)
            st.round_until(act, p0 + n_panel)

        @block.gpsimd
        def _(pool):
            st.reduce_until(pool, p0 + n_panel)

        @block.vector
        def _(dve):
            for k in range(KD):
                dve.wait_ge(rounded, k + 1)
                nc.vector.tensor_tensor(parts[1][:, k], xT[:, k], hi[:, k].bitcast(F32), ALU.subtract).then_inc(reduced, 1)
            for n in range(n_panel):
                dve.wait_ge(st.used, p0 + n + 1)
                for i in range(2):
                    last = write(slice(2 * i, 2 * i + 2), slice(n * PW, (n + 1) * PW), acc[n % 2][i][:])
                last.then_inc(emptied, 1)


def post_norm(nc, g, name, y, row, x):
    squares = g.sem(name + "_squares")
    meaned = g.sem(name + "_mean_ready")
    rooted = g.sem(name + "_root_ready")
    step = Tally(g.sem(name + "_steps"))
    with ExitStack() as tmp, nc.Block() as block:
        junk = tmp.enter_context(nc.sbuf_tensor(name + "_sq", [P, NT, D], F32))
        ms = tmp.enter_context(nc.sbuf_tensor(name + "_ms", [P, NT], F32))
        rt = tmp.enter_context(nc.sbuf_tensor(name + "_rt", [P, NT], F32))
        rs = tmp.enter_context(nc.sbuf_tensor(name + "_rs", [P, NT], F32))

        @block.scalar
        def _(act):
            for j in range(NT):
                nc.scalar.activation(junk[:, j], y[:, j], ACT.Square, accum_out=ms[:, j:j + 1]).then_inc(squares, 1)
            act.wait_ge(meaned, 1)
            nc.scalar.activation(rt[:], ms[:], ACT.Sqrt).then_inc(rooted, 1)

        @block.vector
        def _(dve):
            dve.wait_ge(squares, NT)
            nc.vector.tensor_scalar(ms[:], ms[:], 1.0 / D, EPS, ALU.mult, ALU.add).then_inc(meaned, 1)
            dve.wait_ge(rooted, 1)
            step.link(dve, nc.vector.reciprocal(rs[:], rt[:]))
            for j in range(NT):
                step.mark(nc.vector.scalar_tensor_tensor(y[:, j], y[:, j], rs[:, j:j + 1], row[:], ALU.mult, ALU.mult))
            step.settle(dve)
            for j in range(NT):
                nc.vector.tensor_tensor(x[:, j], x[:, j], y[:, j], ALU.add)


def router(nc, g, h2T, w_r, pick, tokrow, tokcol, xsT, selT, spare):
    sem = g.sem
    logits_ready = sem("router_logits_ready")
    maxed = sem("router_max_ready")
    exps_ready = sem("router_exps_ready")
    aff_ready = sem("router_affinities_ready")
    aff_turned = sem("router_affinities_turned")
    picked = sem("router_picked")
    spread = sem("router_spread")
    cols_turned = sem("router_columns_turned")
    sel_ready = sem("router_sel_ready")
    tok_turned = sem("router_tokens_turned")
    tok_ready = sem("router_tokens_ready")
    tok_rounded = sem("router_tokens_rounded")
    gathered = sem("router_gathered")
    stored = sem("router_gather_stored")
    step = Tally(sem("router_steps"))
    rounds = CAP // 8
    with ExitStack() as tmp, nc.Block() as block:
        sb = lambda n, s, dt=F32: tmp.enter_context(nc.sbuf_tensor("router_" + n, s, dt))
        h2 = [spare.rearrange("p (j c) t -> p j (c t)", j=NT), sb("h2_lo", [P, NT, D], F32R)]
        sel = sb("sel", [P, NT, E_N * CAP], F32R)
        aff = sb("aff", [P, NT, E_N])
        red = sb("red", [P, 2, NT])
        affT = sb("affT", [E_N, 2, T])
        val = sb("val", [E_N, 2, CAP])
        idx = sb("idx", [E_N, CAP], U32)
        idxf = sb("idxf", [E_N, 2, CAP])
        cols = sb("cols", [P, 2, E_N // 2])
        bank = [tmp.enter_context(nc.psum_tensor(f"router_b{i}", [P, 512], F32)) for i in range(8)]
        logit, turn, both = bank[0], bank[1], bank[2:4]
        half = lambda b: b[:, 0:NT * E_N].rearrange("p (j e) -> p j e", j=NT)

        @block.tensor
        def _(pe):
            for j in range(NT):
                for k in range(KD):
                    last = nc.tensor.matmul(half(logit)[:, j], h2T[:, k, j * P:(j + 1) * P], w_r[:, k, :],
                                            start=(k == 0), stop=(k == KD - 1))
            last.then_inc(logits_ready, 1)
            for i in range(2 * NT):
                j, c = i // 2, i % 2
                if i >= 4:
                    pe.wait_ge(tok_ready, i - 3)
                for k in range(4):
                    src = h2T[:, 4 * c + k, :].rearrange("c (p j) -> c j p", j=NT)[:, j]
                    last = nc.tensor.transpose(bank[4 + i % 4][:, k * P:(k + 1) * P], src, g.ident[:])
                last.then_inc(tok_turned, 1)
            pe.wait_ge(aff_ready, 1)
            for j in range(NT):
                last = nc.tensor.transpose(turn[0:E_N, j * P:(j + 1) * P], aff[:, j, :], g.ident[:])
            last.then_inc(aff_turned, 1)
            pe.wait_ge(picked, 1)
            for e in range(E_N):
                last = nc.tensor.matmul(both[e // 8][:, (e % 8) * CAP:(e % 8 + 1) * CAP], pick[:, e, :], idxf[:, 0, :],
                                        start=True, stop=True)
            last.then_inc(spread, 1)
            nc.tensor.transpose(logit[:, 0:E_N], idxf[:].rearrange("e a c -> e (a c)"), g.ident[0:E_N, 0:E_N])
            nc.tensor.transpose(logit[:, E_N:2 * E_N], val[:].rearrange("e a c -> e (a c)"), g.ident[0:E_N, 0:E_N]).then_inc(cols_turned, 1)
            pe.wait_ge(sel_ready, NT)
            pe.wait_ge(tok_ready, 2 * NT)
            for k in range(KD):
                for h in range(2):
                    n = 2 * k + h
                    if n >= 4:
                        pe.wait_ge(stored, n - 3)
                    for part in range(2):
                        for j in range(NT):
                            last = nc.tensor.matmul(bank[4 + n % 4][:], h2[part][:, j, k * P:(k + 1) * P], sel[:, j, h * 512:(h + 1) * 512],
                                                    start=(part + j == 0), stop=(part == 1 and j == NT - 1))
                    last.then_inc(gathered, 1)

        @block.scalar
        def _(act):
            for i in range(2 * NT):
                act.wait_ge(tok_turned, i + 1)
                nc.scalar.copy(h2[0][:, i // 2, (i % 2) * 512:(i % 2 + 1) * 512], bank[4 + i % 4][:]).then_inc(tok_rounded, 1)
            act.wait_ge(maxed, 1)
            nc.scalar.activation(aff[:], aff[:], ACT.Exp).then_inc(exps_ready, 1)
            for n in range(2 * KD):
                act.wait_ge(gathered, n + 1)
                nc.scalar.copy(xsT[:, n // 2, (n % 2) * 512:(n % 2 + 1) * 512], bank[4 + n % 4][:]).then_inc(stored, 1)

        @block.vector
        def _(dve):
            V = nc.vector
            spread_out = lambda x: x.unsqueeze(2).to_broadcast([P, NT, E_N])
            dve.wait_ge(logits_ready, 1)
            for i in range(2 * NT):
                c = slice((i % 2) * 512, (i % 2 + 1) * 512)
                dve.wait_ge(tok_rounded, i + 1)
                V.tensor_tensor(h2[1][:, i // 2, c], bank[4 + i % 4][:], h2[0][:, i // 2, c].bitcast(F32), ALU.subtract).then_inc(tok_ready, 1)
            step.link(dve, V.tensor_reduce(red[:, 0], half(logit), AX, ALU.max))
            V.tensor_tensor(aff[:], half(logit), spread_out(red[:, 0]), ALU.subtract).then_inc(maxed, 1)
            dve.wait_ge(exps_ready, 1)
            step.link(dve, V.tensor_reduce(red[:, 1], aff[:], AX, ALU.add))
            step.link(dve, V.reciprocal(red[:, 1], red[:, 1]))
            V.tensor_tensor(aff[:], aff[:], spread_out(red[:, 1]), ALU.mult).then_inc(aff_ready, 1)
            dve.wait_ge(aff_turned, 1)
            step.link(dve, V.tensor_copy(affT[:, 0], turn[0:E_N, :]))
            for r in range(rounds):
                now, then = affT[:, r % 2], affT[:, (r + 1) % 2]
                c = slice(8 * r, 8 * r + 8)
                step.link(dve, V.max(val[:, 0, c], now))
                step.mark(V.max_index(idx[:, c], val[:, 0, c], now))
                if r + 1 < rounds:
                    step.mark(V.match_replace(then, val[:, 0, c], now, -1.0))
                step.settle(dve)
            step.mark(V.tensor_copy(idxf[:, 0], idx[:]))
            step.mark(V.tensor_copy(idxf[:, 1], idx[:]))
            step.settle(dve)
            V.tensor_copy(val[:, 1], val[:, 0]).then_inc(picked, 1)
            dve.wait_ge(spread, 1)
            for j in range(NT):
                for h in range(2):
                    last = V.tensor_scalar(sel[:, j, h * 512:(h + 1) * 512], both[h][:], tokcol[:, j:j + 1], None, ALU.is_equal)
                last.then_inc(sel_ready, 1)
            dve.wait_ge(cols_turned, 1)
            for i in range(2):
                src = logit[:, i * E_N:(i + 1) * E_N].rearrange("p (a b) -> p a b", b=2)
                for h in range(2):
                    step.mark(V.tensor_copy(cols[h * CAP:(h + 1) * CAP, i], src[h * CAP:(h + 1) * CAP, :, h]))
            step.settle(dve)
            for m in range(E_N // 2):
                V.tensor_scalar(selT[:, m], tokrow[:], cols[:, 0, m:m + 1], cols[:, 1, m:m + 1], ALU.is_equal, ALU.mult)


def experts(nc, g, xsT, ye):
    sem, st = g.sem, g.stream
    p0 = st.taken
    NP = D // PW
    per = 3 * NP
    copied = sem("moe_gate_up_copied")
    turned = sem("moe_gate_up_turned")
    silued = sem("moe_silu_ready")
    hidden = sem("moe_hidden_ready")
    stored = sem("moe_down_stored")
    with ExitStack() as tmp, nc.Block() as block:
        gu = tmp.enter_context(nc.sbuf_tensor("moe_gu", [P, 2, PW], F32))
        silu = tmp.enter_context(nc.sbuf_tensor("moe_silu", [P, 2, 2, CAP], F32))
        hid = tmp.enter_context(nc.sbuf_tensor("moe_hid", [P, 2, KD, CAP], F32))
        acc = [tmp.enter_context(nc.psum_tensor(f"moe_gu{i}", [P, 512], F32)) for i in range(2)]
        turn = [tmp.enter_context(nc.psum_tensor(f"moe_t{i}", [P, 512], F32)) for i in range(2)]
        down = [tmp.enter_context(nc.psum_tensor(f"moe_d{i}", [P, 512], F32)) for i in range(2)]
        chunk = lambda b: b[:, 0:2 * P].rearrange("p (f t) -> p f t", f=2)
        done = lambda e, n: p0 + per * e + n

        @block.sync
        def _(sp):
            st.load_until(sp, p0 + E_N * per + SLOTS)

        @block.tensor
        def _(pe):
            def turn_chunk(e, n):
                i = NP * e + n
                pe.wait_ge(copied, i + 1)
                if i >= 2:
                    pe.wait_ge(hidden, i - 1)
                for f in range(2):
                    last = nc.tensor.transpose(chunk(turn[i % 2])[:, f], gu[:, i % 2, f * P:(f + 1) * P], g.ident[:])
                last.then_inc(turned, 1)

            for e in range(E_N):
                tokens = slice(e * CAP, (e + 1) * CAP)
                for n in range(NP):
                    i = NP * e + n
                    wg = st.take(pe)
                    wu = st.take(pe)
                    if i >= 2:
                        pe.wait_ge(copied, i - 1)
                    for k in range(KD):
                        a = nc.tensor.matmul(acc[i % 2][0:CAP, 0:PW], xsT[:, k, tokens], wg[:, k, :], start=(k == 0), stop=(k == KD - 1))
                        b = nc.tensor.matmul(acc[i % 2][CAP:P, 0:PW], xsT[:, k, tokens], wu[:, k, :], start=(k == 0), stop=(k == KD - 1))
                    a.then_inc(st.used, 1)
                    b.then_inc(st.used, 1)
                    if n >= 1:
                        turn_chunk(e, n - 1)
                turn_chunk(e, NP - 1)
                pe.wait_ge(hidden, NP * (e + 1))
                rows = slice((e % 2) * CAP, (e % 2 + 1) * CAP)
                for n in range(NP):
                    i = NP * e + n
                    w = st.take(pe)
                    if i >= 2:
                        pe.wait_ge(stored, i - 1)
                    for k in range(KD):
                        last = nc.tensor.matmul(down[i % 2][rows, 0:PW], hid[:, e % 2, k, :], w[:, k, :], start=(k == 0), stop=(k == KD - 1))
                    last.then_inc(st.used, 1)

        @block.scalar
        def _(act):
            def silu_chunk(i):
                act.wait_ge(turned, i + 1)
                if i >= 2:
                    act.wait_ge(hidden, i - 1)
                nc.scalar.activation(silu[:, i % 2], chunk(turn[i % 2])[:, :, 0:CAP], ACT.Silu).then_inc(silued, 1)

            for e in range(E_N):
                for n in range(NP):
                    i = NP * e + n
                    act.wait_ge(st.used, done(e, 2 * n + 2))
                    if i >= 2:
                        act.wait_ge(turned, i - 1)
                    nc.scalar.copy(gu[:, i % 2, :], acc[i % 2][:, 0:PW]).then_inc(copied, 1)
                    if n >= 1:
                        silu_chunk(i - 1)
                silu_chunk(NP * (e + 1) - 1)

        @block.vector
        def _(dve):
            for e in range(E_N):
                for n in range(NP):
                    i = NP * e + n
                    dve.wait_ge(silued, i + 1)
                    if e >= 2 and n == 0:
                        dve.wait_ge(st.used, done(e - 2, per))
                    nc.vector.tensor_tensor(hid[:, e % 2, 2 * n:2 * n + 2, :], silu[:, i % 2], chunk(turn[i % 2])[:, :, CAP:P], ALU.mult).then_inc(hidden, 1)
                rows = slice((e % 2) * CAP, (e % 2 + 1) * CAP)
                for n in range(NP):
                    dve.wait_ge(st.used, done(e, 2 * NP + n + 1))
                    nc.vector.tensor_copy(ye[rows, e // 2, n * PW:(n + 1) * PW], down[(NP * e + n) % 2][rows, 0:PW]).then_inc(stored, 1)


def scatter(nc, g, ye, selT, moe):
    summed = g.sem("moe_summed")
    stored = g.sem("moe_sum_stored")
    with ExitStack() as tmp, nc.Block() as block:
        acc = [tmp.enter_context(nc.psum_tensor(f"moe_s{i}", [P, 512], F32)) for i in range(4)]

        @block.tensor
        def _(pe):
            for n in range(2 * NT):
                j, h = n // 2, n % 2
                if n >= 4:
                    pe.wait_ge(stored, n - 3)
                for m in range(E_N // 2):
                    last = nc.tensor.matmul(acc[n % 4][:], selT[:, m, j * P:(j + 1) * P], ye[:, m, h * 512:(h + 1) * 512],
                                            start=(m == 0), stop=(m == E_N // 2 - 1))
                last.then_inc(summed, 1)

        @block.vector
        def _(dve):
            for n in range(2 * NT):
                dve.wait_ge(summed, n + 1)
                nc.vector.tensor_copy(moe[:, n // 2, (n % 2) * 512:(n % 2 + 1) * 512], acc[n % 4][:]).then_inc(stored, 1)


GH = 8
HALF = GH * HD


def gain_rows(nc, g, a, out):
    loaded = g.sem("a_gains_loaded")
    cleared = g.sem("a_gains_cleared")
    spread = g.sem("a_gains_spread")
    with ExitStack() as tmp, nc.Block() as block:
        row = tmp.enter_context(nc.sbuf_tensor("a_gain_row", [P, 6 * HD], F32))
        acc = tmp.enter_context(nc.psum_tensor("a_gain_acc", [P, 6 * HD], F32))

        @block.gpsimd
        def _(pool):
            nc.gpsimd.memset(row[:], 0.0).then_inc(cleared, 1)

        @block.sync
        def _(sp):
            sp.wait_ge(cleared, 1)
            for i, name in enumerate(("a_q_gain_2", "a_k_gain_2")):
                sp.dma_start(row[0:1, i * 3 * HD:(i + 1) * 3 * HD], a[name].rearrange("(o n) -> o n", o=1)).then_inc(loaded, 16)

        @block.tensor
        def _(pe):
            pe.wait_ge(loaded, 32)
            nc.tensor.matmul(acc[:], g.ones[:], row[:], start=True, stop=True).then_inc(spread, 1)

        @block.vector
        def _(dve):
            dve.wait_ge(spread, 1)
            nc.vector.tensor_scalar(out[:, 0:3].rearrange("p g d -> p (g d)"), acc[:, 0:3 * HD], HD ** -0.5, None, ALU.mult)
            nc.vector.tensor_copy(out[:, 3:6].rearrange("p g d -> p (g d)"), acc[:, 3 * HD:])


def dilated_inputs(nc, g, nm, grp, yT, v, qT, kT, gains, rope, num):
    sem, st = g.sem, g.stream
    p0 = st.taken
    emptied = sem(nm + "_emptied")
    meaned = sem(nm + "_mean_ready")
    rooted = sem(nm + "_root_ready")
    normed = sem(nm + "_normed")
    turned = sem(nm + "_turned")
    written = sem(nm + "_written")
    step = Tally(sem(nm + "_steps"))
    with ExitStack() as tmp, nc.Block() as block:
        q = tmp.enter_context(nc.sbuf_tensor(nm + "_q", [P, NT, HALF], F32))
        k = tmp.enter_context(nc.sbuf_tensor(nm + "_k", [P, NT, HALF], F32))
        sq = num[:, grp].rearrange("p j h d -> p j (h d)")
        ms = tmp.enter_context(nc.sbuf_tensor(nm + "_ms", [P, 2, NT, GH], F32))
        rt = tmp.enter_context(nc.sbuf_tensor(nm + "_rt", [P, 2, NT, GH], F32))
        prod = [tmp.enter_context(nc.sbuf_tensor(f"{nm}_rope{i}", [P, NT, GH, 8], F32)) for i in range(4)]
        acc = [[tmp.enter_context(nc.psum_tensor(f"{nm}_o{s}{i}", [P, 2, PW], F32)) for i in range(2)] for s in range(3)]
        turn = [tmp.enter_context(nc.psum_tensor(f"{nm}_t{i}", [P, NT, P], F32)) for i in range(2)]

        @block.sync
        def _(sp):
            st.load_until(sp, p0 + 6 + SLOTS)

        @block.tensor
        def _(pe):
            for n in range(6):
                w = st.take_split(pe)
                if n >= 3:
                    pe.wait_ge(emptied, n - 2)
                for j in range(NT):
                    last = dense(nc, acc[n % 3][j // 2][:, j % 2], lambda a, i: yT[a][:, i, j * P:(j + 1) * P],
                                 lambda b, i: w[b][:, i, :])
                last.then_inc(st.used, 1)
            for n in range(8):
                if n % 4 == 0:
                    pe.wait_ge(normed, n // 4 + 1)
                if n >= 2:
                    pe.wait_ge(written, n - 1)
                for j in range(NT):
                    last = nc.tensor.transpose(turn[n % 2][:, j], (q if n < 4 else k)[:, j, (n % 4) * P:(n % 4 + 1) * P], g.ident[:])
                last.then_inc(turned, 1)

        @block.scalar
        def _(act):
            def root(i):
                act.wait_ge(meaned, i + 1)
                nc.scalar.activation(rt[:, i], ms[:, i], ACT.Sqrt).then_inc(rooted, 1)

            st.round_until(act, p0 + 2)
            for n in range(6):
                act.wait_ge(st.used, p0 + n + 1)
                st.round_until(act, p0 + n + 3)
                for i in range(2):
                    last = nc.scalar.copy((q, k, v)[n // 2][:, 2 * i:2 * i + 2, (n % 2) * PW:(n % 2 + 1) * PW], acc[n % 3][i][:])
                last.then_inc(emptied, 1)
                if n in (2, 4):
                    root(n // 2 - 1)
            for n in range(8):
                act.wait_ge(turned, n + 1)
                nc.scalar.copy((qT if n < 4 else kT)[:, n % 4, :], turn[n % 2][:].rearrange("p j t -> p (j t)")).then_inc(written, 1)

        @block.gpsimd
        def _(pool):
            st.reduce_until(pool, p0 + 8)

        @block.vector
        def _(dve):
            V = nc.vector
            for i, x in enumerate((q, k)):
                heads = x[:].rearrange("p j (h d) -> p j h d", d=HD)
                dve.wait_ge(emptied, 2 * i + 2)
                step.link(dve, V.tensor_tensor(sq, x[:], x[:], ALU.mult))
                step.link(dve, V.tensor_reduce(ms[:, i], sq.rearrange("p j (h d) -> p j h d", d=HD), AX, ALU.add))
                V.tensor_scalar(ms[:, i], ms[:, i], 1.0 / HD, EPS, ALU.mult, ALU.add).then_inc(meaned, 1)
                dve.wait_ge(rooted, i + 1)
                step.link(dve, V.reciprocal(rt[:, i], rt[:, i]))
                step.link(dve, V.tensor_tensor(heads, heads, rt[:, i].unsqueeze(3).to_broadcast([P, NT, GH, HD]), ALU.mult))
                gain = gains[:, 3 * i + grp].unsqueeze(1).to_broadcast([P, NT * GH, HD])
                flat = x[:].rearrange("p j (h d) -> p (j h) d", d=HD)
                step.link(dve, V.tensor_tensor(flat, flat, gain, ALU.mult))
                x1, x2 = heads[:, :, :, 0:8], heads[:, :, :, 8:16]
                cos, sin = (rope[:, c].unsqueeze(2).to_broadcast([P, NT, GH, 8]) for c in range(2))
                for dst, part, tab in ((prod[0], x1, cos), (prod[1], x2, sin), (prod[2], x2, cos), (prod[3], x1, sin)):
                    step.mark(V.tensor_tensor(dst[:], part, tab, ALU.mult))
                step.settle(dve)
                step.mark(V.tensor_tensor(x1, prod[0][:], prod[1][:], ALU.subtract))
                step.mark(V.tensor_tensor(x2, prod[2][:], prod[3][:], ALU.add))
                step.settle(dve)
                V.tensor_copy(ms[:, i], rt[:, i]).then_inc(normed, 1)


def dilated_attention(nc, g, nm, grp, qT, kT, v, mask, num, mx, den):
    sem = g.sem
    scored = sem(nm + "_scored")
    masked = sem(nm + "_masked")
    maxed = sem(nm + "_max_ready")
    exped = sem(nm + "_exps_ready")
    turned = sem(nm + "_turned")
    copied = sem(nm + "_turned_copied")
    applied = sem(nm + "_applied")
    kept = sem(nm + "_kept")
    step = Tally(sem(nm + "_steps"))
    if grp == 0:
        steps = [(2 * hp + e, (j,)) for hp in range(GH // 2) for j in range(NT) for e in range(2)]
    else:
        steps = [(h, tuple(range(NT))) for h in range(GH)]
    final = [max(u for u, step_ in enumerate(steps) if step_[0] == h) for h in range(GH)]
    with ExitStack() as tmp, nc.Block() as block:
        s = [tmp.enter_context(nc.sbuf_tensor(f"{nm}_s{i}", [P, NT, P], F32)) for i in range(3)]
        neg = tmp.enter_context(nc.sbuf_tensor(nm + "_neg", [P, 3, NT], F32))
        pT = [tmp.enter_context(nc.sbuf_tensor(f"{nm}_pT{i}", [P, NT, P], F32)) for i in range(2)]
        sc = [tmp.enter_context(nc.psum_tensor(f"{nm}_sc{i}", [P, NT, P], F32)) for i in range(4)]
        tp = [tmp.enter_context(nc.psum_tensor(f"{nm}_tp{i}", [P, NT, P], F32)) for i in range(2)]
        pv = [tmp.enter_context(nc.psum_tensor(f"{nm}_pv{i}", [P, NT, HD], F32)) for i in range(2)]

        @block.tensor
        def _(pe):
            def score(u):
                h, js = steps[u]
                e = slice(HD * (h % 2), HD * (h % 2 + 1))
                if u >= 4:
                    pe.wait_ge(masked, u - 3)
                for j in js:
                    tile = slice(j * P, (j + 1) * P)
                    if grp == 0:
                        last = nc.tensor.matmul(sc[u % 4][:].rearrange("p j t -> p (j t)"), qT[e, h // 2, tile], kT[e, h // 2, :], start=True, stop=True)
                    else:
                        last = nc.tensor.matmul(sc[u % 4][:, j], qT[e, h // 2, tile], kT[e, h // 2, tile], start=True, stop=True)
                last.then_inc(scored, 1)

            def turn(u):
                if u >= 2:
                    pe.wait_ge(copied, u - 1)
                pe.wait_ge(exped, u + 1)
                for j in range(NT):
                    last = nc.tensor.transpose(tp[u % 2][:, j], s[u % 3][:, j], g.ident[:])
                last.then_inc(turned, 1)

            def apply(u):
                h, js = steps[u]
                pe.wait_ge(copied, u + 1)
                if js[0] == 0 and h >= 2:
                    pe.wait_ge(kept, h - 1)
                for i in range(NT):
                    first, last_key = (i == 0, i == NT - 1) if grp == 0 else (True, True)
                    last = nc.tensor.matmul(pv[h % 2][:, js[0] if grp == 0 else i], pT[u % 2][:, i], v[:, i, h * HD:(h + 1) * HD],
                                            start=first, stop=last_key)
                last.then_inc(applied, 1)

            score(0)
            score(1)
            for u in range(len(steps)):
                if u % 2 == 0 and u + 2 < len(steps):
                    score(u + 2)
                    score(u + 3)
                turn(u)
                if u:
                    apply(u - 1)
            apply(len(steps) - 1)

        @block.vector
        def _(dve):
            V = nc.vector

            def keep(h):
                dve.wait_ge(applied, final[h] + 1)
                V.tensor_copy(num[:, grp, :, h, :], pv[h % 2][:]).then_inc(kept, 1)

            for u, (h, js) in enumerate(steps):
                dve.wait_ge(scored, u + 1)
                if u >= 3:
                    dve.wait_ge(turned, u - 2)
                m = mask[:, js[0]] if grp == 0 else mask.unsqueeze(1).to_broadcast([P, NT, P])
                V.tensor_tensor(s[u % 3][:], sc[u % 4][:], m, ALU.add).then_inc(masked, 1)
                dve.wait_ge(masked, u + 1)
                dst = mx[:, grp, js[0]:js[-1] + 1, h]
                src = s[u % 3][:].rearrange("p j t -> p (j t)").unsqueeze(1) if grp == 0 else s[u % 3][:]
                step.link(dve, V.tensor_reduce(dst, src, AX, ALU.max))
                V.tensor_scalar(neg[:, u % 3, 0:len(js)], dst, -1.0, None, ALU.mult).then_inc(maxed, 1)
                for head in range(GH):
                    if u == final[head | 1] + 2:
                        keep(head)
            for head in range(GH - 2, GH):
                keep(head)

        @block.scalar
        def _(act):
            def copy(u):
                act.wait_ge(turned, u + 1)
                if u >= 2:
                    act.wait_ge(applied, u - 1)
                nc.scalar.copy(pT[u % 2][:], tp[u % 2][:]).then_inc(copied, 1)

            for u, (h, js) in enumerate(steps):
                act.wait_ge(maxed, u + 1)
                if grp == 0:
                    flat = s[u % 3][:].rearrange("p j t -> p (j t)")
                    last = nc.scalar.activation(flat, flat, ACT.Exp, bias=neg[:, u % 3, 0:1], accum_out=den[:, grp, js[0], h:h + 1])
                else:
                    for j in js:
                        last = nc.scalar.activation(s[u % 3][:, j], s[u % 3][:, j], ACT.Exp, bias=neg[:, u % 3, j:j + 1],
                                                    accum_out=den[:, grp, j, h:h + 1])
                last.then_inc(exped, 1)
                if u:
                    copy(u - 1)
            copy(len(steps) - 1)


def dilated_combine(nc, g, nm, half, num, mx, den, oT):
    sem = g.sem
    shifted = sem(nm + "_shifted")
    weighed = sem(nm + "_weights_ready")
    ready = sem(nm + "_out_ready")
    turned = sem(nm + "_turned")
    step = Tally(sem(nm + "_steps"))
    with ExitStack() as tmp, nc.Block() as block:
        top = tmp.enter_context(nc.sbuf_tensor(nm + "_top", [P, NT, GH], F32))
        wt = tmp.enter_context(nc.sbuf_tensor(nm + "_wt", [P, 3, NT, GH], F32))
        wd = tmp.enter_context(nc.sbuf_tensor(nm + "_wd", [P, 3, NT, GH], F32))
        acc = [tmp.enter_context(nc.psum_tensor(f"{nm}_t{i}", [P, NT, P], F32)) for i in range(4)]
        every = lambda x: x.unsqueeze(1).to_broadcast([P, 3, NT, GH])

        @block.vector
        def _(dve):
            V = nc.vector
            step.link(dve, V.tensor_tensor(top[:], mx[:, 0], mx[:, 1], ALU.max))
            step.link(dve, V.tensor_tensor(top[:], top[:], mx[:, 2], ALU.max))
            V.tensor_tensor(wt[:], mx[:], every(top[:]), ALU.subtract).then_inc(shifted, 1)
            dve.wait_ge(weighed, 1)
            step.link(dve, V.tensor_tensor(wd[:], wt[:], den[:], ALU.mult))
            step.link(dve, V.tensor_tensor(top[:], wd[:, 0], wd[:, 1], ALU.add))
            step.link(dve, V.tensor_tensor(top[:], top[:], wd[:, 2], ALU.add))
            step.link(dve, V.reciprocal(top[:], top[:]))
            step.link(dve, V.tensor_tensor(wt[:], wt[:], every(top[:]), ALU.mult))
            for i in range(3):
                step.mark(V.tensor_tensor(num[:, i], num[:, i], wt[:, i].unsqueeze(3).to_broadcast([P, NT, GH, HD]), ALU.mult))
            step.settle(dve)
            step.link(dve, V.tensor_tensor(num[:, 0], num[:, 0], num[:, 1], ALU.add))
            V.tensor_tensor(num[:, 0], num[:, 0], num[:, 2], ALU.add).then_inc(ready, 1)
            for c in range(4):
                dve.wait_ge(turned, c + 1)
                V.tensor_copy(oT[:, 4 * half + c, :], acc[c][:].rearrange("p j t -> p (j t)"))

        @block.scalar
        def _(act):
            act.wait_ge(shifted, 1)
            nc.scalar.activation(wt[:], wt[:], ACT.Exp).then_inc(weighed, 1)

        @block.tensor
        def _(pe):
            pe.wait_ge(ready, 1)
            o = num[:, 0].rearrange("p j h d -> p j (h d)")
            for c in range(4):
                for j in range(NT):
                    last = nc.tensor.transpose(acc[c][:, j], o[:, j, c * P:(c + 1) * P], g.ident[:])
                last.then_inc(turned, 1)


def mlp_order():
    NP, quarters = D // PW, FF // D
    order = [(1, 0, n) for n in range(NP)]
    for q in range(quarters):
        if q + 1 < quarters:
            order.append((1, q + 1, 0))
        order += [(2, q, n) for n in range(NP)]
        if q + 1 < quarters:
            order += [(1, q + 1, n) for n in range(1, NP)]
    return order


def mlp(nc, g, nm, yT, x):
    sem, st = g.sem, g.stream
    p0 = st.taken
    NP = D // PW
    order = mlp_order()
    positive = sem(nm + "_relu_ready")
    squared = sem(nm + "_squared")
    rounded = sem(nm + "_rounded")
    hidden = sem(nm + "_hidden_ready")
    emptied = sem(nm + "_emptied")
    with ExitStack() as tmp, nc.Block() as block:
        hid = tmp.enter_context(nc.sbuf_tensor(nm + "_hid", [P, 2, KD, T], F32))
        hid_lo = g.twin(nm + "_hid_lo", [P, 2, KD, T], F32R)
        hid_hi = tmp.enter_context(nc.sbuf_tensor(nm + "_hid_hi", [P, 2, KD, T], F32R))
        hid_parts = (hid_hi[:], hid_lo[:])
        up = [[tmp.enter_context(nc.psum_tensor(f"{nm}_h{s}{i}", [P, T], F32)) for i in range(2)] for s in range(2)]
        acc = [[tmp.enter_context(nc.psum_tensor(f"{nm}_o{s}{i}", [P, 2, PW], F32)) for i in range(2)] for s in range(2)]

        @block.sync
        def _(sp):
            st.load_until(sp, p0 + len(order) + SLOTS)

        @block.tensor
        def _(pe):
            for kind, q, n in order:
                i = NP * q + n
                w = st.take_split(pe)
                if kind == 1:
                    if i >= 2:
                        pe.wait_ge(squared, i - 1)
                    for h in range(2):
                        last = dense(nc, up[i % 2][h][:], lambda a, k: w[a][:, k, h * P:(h + 1) * P], lambda b, k: yT[b][:, k, :])
                else:
                    if n == 0:
                        pe.wait_ge(hidden, NP * (q + 1))
                    if i >= 2:
                        pe.wait_ge(emptied, i - 1)
                    for j in range(NT):
                        last = dense(nc, acc[i % 2][j // 2][:, j % 2], lambda a, k: hid_parts[a][:, q % 2, k, j * P:(j + 1) * P],
                                     lambda b, k: w[b][:, k, :])
                last.then_inc(st.used, 1)

        @block.gpsimd
        def _(pool):
            st.reduce_until(pool, p0 + len(order) + 2)

        @block.scalar
        def _(act):
            st.round_until(act, p0 + 2)
            for t, (kind, q, n) in enumerate(order):
                act.wait_ge(st.used, p0 + t + 1)
                if kind == 1:
                    i = NP * q + n
                    for h in range(2):
                        last = nc.scalar.activation(hid[:, q % 2, 2 * n + h, :], up[i % 2][h][:], ACT.Relu)
                    last.then_inc(positive, 1)
                    c = slice(2 * n, 2 * n + 2)
                    act.wait_ge(squared, i + 1)
                    nc.scalar.copy(hid_hi[:, q % 2, c], hid[:, q % 2, c]).then_inc(rounded, 1)
                st.round_until(act, p0 + t + 3)

        @block.vector
        def _(dve):
            V = nc.vector
            for t, (kind, q, n) in enumerate(order):
                i = NP * q + n
                if kind == 1:
                    c = slice(2 * n, 2 * n + 2)
                    dve.wait_ge(positive, i + 1)
                    for h in range(2):
                        d = hid[:, q % 2, 2 * n + h, :]
                        last = V.tensor_tensor(d, d, up[i % 2][h][:], ALU.mult)
                    last.then_inc(squared, 1)
                    dve.wait_ge(rounded, i + 1)
                    V.tensor_tensor(hid_parts[1][:, q % 2, c], hid[:, q % 2, c], hid_hi[:, q % 2, c].bitcast(F32), ALU.subtract).then_inc(hidden, 1)
                else:
                    dve.wait_ge(st.used, p0 + t + 1)
                    if q:
                        dve.wait_ge(emptied, i - NP + 1)
                    for h in range(2):
                        d = x[:, 2 * h:2 * h + 2, n * PW:(n + 1) * PW]
                        last = V.tensor_tensor(d, d, acc[i % 2][h][:], ALU.add)
                    last.then_inc(emptied, 1)


def gated_conv(nc, g, yT, zT):
    sem, st = g.sem, g.stream
    p0 = st.taken
    emptied = sem("gc_emptied")
    copied = sem("gc_b_c_copied")
    step = Tally(sem("gc_steps"))
    n_chunk = D // PW
    with ExitStack() as tmp, nc.Block() as block:
        bc = tmp.enter_context(nc.sbuf_tensor("gc_bc", [P, 2, 2, 2, T], F32))
        u = tmp.enter_context(nc.sbuf_tensor("gc_u", [P, 2, T], F32))
        y = tmp.enter_context(nc.sbuf_tensor("gc_y", [P, 2, T], F32))
        acc = [[tmp.enter_context(nc.psum_tensor(f"gc_o{s}{i}", [P, T], F32)) for i in range(2)] for s in range(3)]

        @block.sync
        def _(sp):
            st.load_until(sp, p0 + 3 * n_chunk + SLOTS)

        @block.tensor
        def _(pe):
            for n in range(3 * n_chunk):
                c, part = n // 3, n % 3
                w = st.take_split(pe)
                if c:
                    if part < 2:
                        pe.wait_ge(copied, 2 * (c - 1) + part + 1)
                    else:
                        pe.wait_ge(emptied, c)
                for h in range(2):
                    last = dense(nc, acc[part][h][:], lambda a, k: w[a][:, k, h * P:(h + 1) * P], lambda b, k: yT[b][:, k, :])
                last.then_inc(st.used, 1)

        @block.gpsimd
        def _(pool):
            st.reduce_until(pool, p0 + 3 * n_chunk + 2)

        @block.scalar
        def _(act):
            st.round_until(act, p0 + 2)
            for c in range(n_chunk):
                for part in range(2):
                    act.wait_ge(st.used, p0 + 3 * c + part + 1)
                    st.round_until(act, p0 + 3 * c + part + 3)
                    if c >= 2 and part == 0:
                        act.wait_ge(emptied, c)
                    for h in range(2):
                        last = nc.scalar.copy(bc[:, c % 2, part, h], acc[part][h][:])
                    last.then_inc(copied, 1)
                st.round_until(act, p0 + 3 * c + 5)

        @block.vector
        def _(dve):
            V = nc.vector
            tap = lambda t, k: g.cols[:, g.col["b_conv"] + KD * t + k:g.col["b_conv"] + KD * t + k + 1]
            for c in range(n_chunk):
                dve.wait_ge(st.used, p0 + 3 * c + 3)
                dve.wait_ge(copied, 2 * c + 2)
                for h in range(2):
                    last = V.tensor_tensor(u[:, h], bc[:, c % 2, 1, h], acc[2][h][:], ALU.mult)
                    step.mark(last)
                step.settle(dve)
                for h in range(2):
                    step.mark(V.tensor_scalar(y[:, h], u[:, h], tap(1, 2 * c + h), None, ALU.mult))
                step.settle(dve)
                for h in range(2):
                    step.mark(V.scalar_tensor_tensor(y[:, h, 1:], u[:, h, 0:T - 1], tap(0, 2 * c + h), y[:, h, 1:], ALU.mult, ALU.add))
                step.settle(dve)
                for h in range(2):
                    step.mark(V.scalar_tensor_tensor(y[:, h, 0:T - 1], u[:, h, 1:], tap(2, 2 * c + h), y[:, h, 0:T - 1], ALU.mult, ALU.add))
                step.settle(dve)
                for h in range(2):
                    dst = zT[:, 2 * c + h, :].rearrange("c (j p) -> c p j", j=NT)
                    last = V.tensor_tensor(dst, y[:, h].rearrange("c (p j) -> c p j", j=NT), bc[:, c % 2, 0, h].rearrange("c (p j) -> c p j", j=NT), ALU.mult)
                last.then_inc(emptied, 1)
                dve.wait_ge(emptied, c + 1)


def store(nc, x, out, stored):
    with nc.Block() as block:
        @block.sync
        def _(sp):
            sp.dma_start(out.rearrange("(p j) d -> p j d", j=NT), x[:]).then_inc(stored, 16)
            sp.wait_ge(stored, 16)


def program(nc, a, out):
    with ExitStack() as ctx:
        g = Buffers()
        g.sb = lambda n, s, dt=F32: ctx.enter_context(nc.sbuf_tensor(n, s, dt))
        g.sb_in = lambda stack, n, s, dt=F32: stack.enter_context(nc.sbuf_tensor(n, s, dt))
        g.passing = []

        def sem(name):
            g.passing.append(nc.alloc_semaphore(name=name))
            return g.passing[-1]

        def retire():
            nc.clear_and_free_semaphores(g.passing)
            nc.all_engine_barrier()
            g.passing = []

        def twin(name, shape, dtype, side="left"):
            size = 4 * int(np.prod(shape[1:]))
            return nc.alloc_sbuf_tensor_at(name, shape, dtype, offset=nc.sbuf_base - size if side == "left" else nc.sbuf_top)

        g.twin = twin
        g.sem = sem
        lasting = lambda n: ctx.enter_context(nc.semaphore(n))
        g.ident = g.sb("ident", [P, P])
        g.headsum = g.sb("headsum", [P, P])
        g.ones = g.sb("ones", [P, P])
        g.cols = g.sb("cols", [P, 3 * P])
        g.mod = g.sb("mod", [P, 6 * KD, 2])
        g.mix_scale = g.sb("mix_scale", [P, KD, 2])
        g.ffn_scale = g.sb("ffn_scale", [P, KD, 2])
        g.post = g.sb("post_gains", [P, 2, KD])
        output_stored = lasting("output_stored")
        g.ring = g.sb("weight_ring", [P, SLOTS, KD, PW])
        ring_lo = g.twin("weight_ring_lo", [P, SLOTS, KD, PW], F32R)
        g.weight_hi = g.sb("weight_hi", [P, 2, KD, PW], F32R)
        g.weight_spare = g.twin("weight_hi_spare", [P, 2 * KD * PW], F32)
        g.stream = st = Stream(nc, g.ring, ring_lo, g.weight_hi, [lasting(f"slot{s}_full") for s in range(SLOTS)],
                               lasting("panels_used"), lasting("panels_hi_ready"), lasting("panels_lo_ready"))
        st.add_matrix(a["w_mod"], 0, 0, 6 * D, split=False)
        w = a["w_in"]
        st.add_matrix(w, 0, 0, RET_COLS)
        r0 = RET_COLS
        st.add((w[:, r0 + 1536:r0 + 1728], 0))
        st.add((w[:, r0 + 1728:r0 + 1984], 0))
        for hp in range(4):
            st.add((w[:, r0 + hp * P:r0 + (hp + 1) * P], 0), (w[:, r0 + 512 + hp * P:r0 + 512 + (hp + 1) * P], P))
            st.add((w[:, r0 + 1024 + hp * P:r0 + 1024 + (hp + 1) * P], 0))
        st.add_matrix(a["w_out"], 0, 0, D)
        for e in range(E_N):
            for c in range(0, D, PW):
                st.add((a["w_gate"][e, :, c:c + PW], 0), split=False)
                st.add((a["w_up"][e, :, c:c + PW], 0), split=False)
            for c in range(0, D, PW):
                st.add((a["w_down"][e, :, c:c + PW], 0), split=False)
        for half in range(2):
            for grp in range(3):
                for part in range(3):
                    c0 = (grp * 3 + part) * D + half * 512
                    st.add_matrix(a["a_wqkv"], 0, c0, c0 + 512)
        st.add_matrix(a["a_wo"], 0, 0, D)

        def add_mlp(layer):
            for kind, q, n in mlp_order():
                c = q * D + n * PW
                st.add((a["mlp_w1"][layer][:, c:c + PW] if kind == 1 else a["mlp_w2"][layer][q * D:(q + 1) * D, n * PW:(n + 1) * PW], 0))
        add_mlp(0)
        for c in range(0, D, PW):
            for part in range(3):
                st.add((a["b_win"][:, part * D + c:part * D + c + PW], 0))
        st.add_matrix(a["b_wout"], 0, 0, D)
        add_mlp(1)

        def fetch(name, *pairs):
            there = g.sem(name + "_loaded")
            with nc.Block() as block:
                @block.sync
                def _(sp):
                    for dst, src in pairs:
                        sp.dma_start(dst, src).then_inc(there, 16)
                    sp.wait_ge(there, 16 * len(pairs))

        setup(nc, g, a)
        modulation(nc, g)
        with ExitStack() as first:
            latT = g.sb_in(first, "latT", [P, KD, T])
            lat_lo = g.twin("latT_lo", [P, KD, T], F32R)
            with ExitStack() as mix:
                h_all = mix.enter_context(nc.sbuf_tensor("hT", [P, KD, TA], F32, side="right"))
                h_lo = g.twin("hT_lo", [P, KD, TA], F32R, "right")
                h_hi = mix.enter_context(nc.sbuf_tensor("hT_hi", [P, KD, TA], F32R, side="right"))
                hT = (h_hi[:], h_lo[:])
                with ExitStack() as tmp:
                    x_tiles = g.sb_in(tmp, "x_tiles", [P, NT, D])
                    ctx_tiles = g.sb_in(tmp, "ctx_tiles", [P, NTC, D])
                    fetch("tokens", (x_tiles[:], a["x"].rearrange("(p j) d -> p j d", j=NT)),
                          (ctx_tiles[:], a["ctx"].rearrange("(p j) d -> p j d", j=NTC)))
                    norm_turn(nc, g, "pre_mix", [
                        (x_tiles, NT, h_all, TC, lambda k: g.mix_scale[:, k, 0:1], lambda k: g.mod[:, k, 0:1]),
                        (ctx_tiles, NTC, h_all, 0, lambda k: g.mix_scale[:, k, 1:2], lambda k: g.mod[:, k, 1:2])], hi=h_hi, lo=h_lo)
                with ExitStack() as ret:
                    gates = g.sb_in(ret, "ret_gates", [P, KD, T])
                    v_tok = g.sb_in(ret, "ret_v", [P, NTC + NT, RET_W])
                    qT = g.sb_in(ret, "ret_qT", [P, 4, T])
                    kT = g.sb_in(ret, "ret_kT", [P, 4, TA])
                    with ExitStack() as tmp:
                        q_tok = g.sb_in(tmp, "ret_q", [P, NT, RET_W])
                        k_tok = g.sb_in(tmp, "ret_k", [P, NTC + NT, RET_W])
                        rope = g.sb_in(tmp, "ret_rope_tab", [P, 2, NT, 32])
                        fetch("rope", (rope[:], a["c_rope"]))
                        retention_inputs(nc, g, hT, q_tok, k_tok, v_tok, gates, rope)
                        retention_turn(nc, g, q_tok, k_tok, qT, kT)
                    dist = g.sb_in(ret, "ret_dist", [P, 2, TA])
                    fetch("dist", (dist[:], a["c_dist"]))
                    retention(nc, g, qT, kT, v_tok, gates, dist, latT)
                retire()
                with ExitStack() as rw:
                    buf = lambda stack, n, shape: g.sb_in(stack, "rw_" + n, [P] + shape)
                    low, par, f = Buffers(), Buffers(), Buffers()
                    low.wl, low.al, low.gl = buf(rw, "wl", [TA]), buf(rw, "al", [TA]), buf(rw, "gl", [2, T])
                    par.w2, par.a2 = buf(rw, "w2", [RW_W]), buf(rw, "a2", [RW_W])
                    tri = buf(rw, "tri", [9, 2, P])
                    restart = buf(rw, "restart", [TA])
                    fetch("rwkv_tables", (tri[:], a["c_tri"]), (par.w2[:], a["rwkv_w2"]), (par.a2[0:64, :], a["rwkv_a2"]),
                          (restart[:], a["c_restart"]))
                    par.g2_rows = a["rwkv_g2"].rearrange("d p n -> p d n")
                    rwkv_low(nc, g, hT, low.wl, low.al, low.gl)
                    f.A, f.Bh, f.Kh = (buf(rw, n, [2, TA]) for n in ("A", "Bh", "Kh"))
                    f.R, f.Y = buf(rw, "R", [2, T]), buf(rw, "Y", [2, T])
                    f.v, f.bonus = buf(rw, "v", [TA]), buf(rw, "bonus", [T])
                    f.pc, f.pm, f.pn, f.pe = (buf(rw, n, [2, TA // P]) for n in ("pc", "pm", "pn", "pe"))
                    for hp in range(4):
                        rwkv_prepare(nc, g, hp, hT, f, low, par, restart)
                        rwkv_scan(nc, g, hp, f, tri)
                        rwkv_out(nc, g, hp, f, low, par, latT)
                        retire()
            x = g.sb_in(first, "x", [P, NT, D])
            lat_hi = g.sb_in(first, "latT_hi", [P, KD, T], F32R)
            with ExitStack() as tmp:
                mix = g.sb_in(tmp, "mix", [P, NT, D])
                row = g.sb_in(tmp, "post_mix_row", [P, D])
                fetch("x", (x[:], a["x"].rearrange("(p j) d -> p j d", j=NT)))
                row_vector(nc, g, "post_mix", row, g.post[:, 0])
                project_rows(nc, g, "w_out", latT[:], lat_hi[:], lat_lo[:], lambda js, c, acc: nc.vector.tensor_copy(mix[:, js, c], acc))
                post_norm(nc, g, "post_mix_norm", mix, row, x)
            retire()
            with ExitStack() as moe:
                xsT = g.sb_in(moe, "moe_xsT", [P, KD, E_N * CAP])
                selT = g.sb_in(moe, "moe_selT", [P, E_N // 2, T])
                with ExitStack() as tmp:
                    h2T = latT
                    norm_turn(nc, g, "pre_ffn", [(x, NT, h2T, 0, lambda k: g.ffn_scale[:, k, 0:1], lambda k: g.mod[:, 3 * KD + k, 0:1])])
                    w_r = g.sb_in(tmp, "w_router", [P, KD, E_N])
                    pick = g.sb_in(tmp, "pick", [E_N, E_N, P])
                    tokrow = g.sb_in(tmp, "tokrow", [P, T])
                    tokcol = g.sb_in(tmp, "tokcol", [P, NT])
                    fetch("router", (w_r[:], a["w_router"].rearrange("(k p) e -> p k e", p=P)), (pick[:], a["c_pick"]),
                          (tokrow[:], a["c_tokrow"]), (tokcol[:], a["c_tokcol"]))
                    router(nc, g, h2T, w_r, pick, tokrow, tokcol, xsT, selT, lat_hi[:])
                ye = g.sb_in(moe, "moe_ye", [P, E_N // 2, D])
                experts(nc, g, xsT, ye)
                out_sum = xsT[:, 0:NT]
                row = g.sb_in(moe, "post_ffn_row", [P, D])
                row_vector(nc, g, "post_ffn", row, g.post[:, 1])
                scatter(nc, g, ye, selT, out_sum)
                post_norm(nc, g, "post_ffn_norm", out_sum, row, x)
            retire()

            def add_to_x(js, c, acc):
                return nc.vector.tensor_tensor(x[:, js, c], x[:, js, c], acc, ALU.add)

            def normalised(name, gain, layer, permuted):
                c0 = g.col[gain] + KD * layer
                norm_turn(nc, g, name, [(x, NT, latT, 0, lambda k: g.cols[:, c0 + k:c0 + k + 1], None)], permuted=permuted, hi=lat_hi, lo=lat_lo)

            yT = (lat_hi[:], lat_lo[:])
            normalised("norm1_0", "norm1", 0, True)
            with ExitStack() as att:
                oT = g.sb_in(att, "a_oT", [P, KD, T])
                oT_lo = g.twin("a_oT_lo", [P, KD, T], F32R)
                num = g.sb_in(att, "a_num", [P, 3, NT, GH, HD])
                mx = g.sb_in(att, "a_max", [P, 3, NT, GH])
                den = g.sb_in(att, "a_den", [P, 3, NT, GH])
                qT = g.sb_in(att, "a_qT", [P, 4, T])
                kT = g.sb_in(att, "a_kT", [P, 4, T])
                v = g.sb_in(att, "a_v", [P, NT, HALF])
                gains = g.sb_in(att, "a_gains", [P, 6, HD])
                rope = g.sb_in(att, "a_rope", [P, 2, NT, 8])
                band = g.sb_in(att, "a_band", [P, NT, NT, P])
                stride = g.sb_in(att, "a_stride", [P, 2, P])
                gain_rows(nc, g, a, gains)
                fetch("a_tables", (rope[:], a["c_rope2"]), (band[:], a["c_band"]), (stride[:], a["c_stride"]))
                for half in range(2):
                    for grp in range(3):
                        nm = f"a{half}{grp}"
                        dilated_inputs(nc, g, nm + "i", grp, yT, v, qT, kT, gains, rope, num)
                        dilated_attention(nc, g, nm + "s", grp, qT, kT, v, band[:] if grp == 0 else stride[:, grp - 1], num, mx, den)
                        retire()
                    dilated_combine(nc, g, f"a{half}c", half, num, mx, den, oT)
                project_rows(nc, g, "a_wo", oT[:], lat_hi[:], oT_lo[:], add_to_x)
            retire()
            normalised("norm2_0", "norm2", 0, True)
            mlp(nc, g, "mlp0", yT, x)
            retire()
            normalised("norm1_1", "norm1", 1, False)
            with ExitStack() as tmp:
                zT = g.sb_in(tmp, "gc_zT", [P, KD, T])
                zT_lo = g.twin("gc_zT_lo", [P, KD, T], F32R)
                gated_conv(nc, g, yT, zT)
                project_rows(nc, g, "b_wout", zT[:], lat_hi[:], zT_lo[:], add_to_x)
            retire()
            normalised("norm2_1", "norm2", 1, True)
            mlp(nc, g, "mlp1", yT, x)
            store(nc, x, out, output_stored)


_FLAT = {"x": (T, D), "c": (D,), "ctx": (TC, D), "w_mod": (D, 6 * D), "b_mod": (6 * D,), "norm_gains": (4 * D,),
         "w_in": (D, RET_COLS + RW_COLS), "rwkv_conv": (3, RW_COLS), "rwkv_w0": (2 * RW_W,), "rwkv_w2": (P, RW_W),
         "rwkv_a0": (RW_W,), "rwkv_a2": (64, RW_W), "rwkv_g2": (2, P, RW_W), "rwkv_k_k": (RW_W,),
         "rwkv_k_a": (RW_W,), "rwkv_r_k": (RW_W,), "rwkv_lnx_w": (RW_W,), "rwkv_lnx_b": (RW_W,),
         "w_out": (D, D), "w_router": (D, E_N), "w_gate": (E_N, D, D), "w_up": (E_N, D, D), "w_down": (E_N, D, D),
         "norm1_2": (2 * D,), "norm2_2": (2 * D,), "a_wqkv_2": (D, 9 * D), "a_q_gain_2": (3 * HD,),
         "a_k_gain_2": (3 * HD,), "a_wo_2": (D, D), "b_win_2": (D, 3 * D), "b_conv_2": (3 * D,),
         "b_wout_2": (D, D), "mlp_w1_2": (2, D, FF), "mlp_w2_2": (2, FF, D), "c_ctx": (D,)}


def kernel(**inputs):
    import concourse.bacc as _bacc
    from concourse.bass_utils import run_bass_kernel_spmd as _run

    nc = _bacc.Bacc("TRN2", target_bir_lowering=False, num_devices=1)
    arrays, a = {}, {}
    for name, shape in _FLAT.items():
        arrays["in_" + name] = np.ascontiguousarray(inputs[name]).reshape(shape)
    for name, table in consts().items():
        arrays["in_" + name] = table
    for name, x in arrays.items():
        a[name[3:]] = nc.dram_tensor(name, x.shape, F32, kind="ExternalInput").ap()
    aliases(a)
    out = nc.dram_tensor("out_0", (T, D), F32, kind="ExternalOutput").ap()
    program(nc, a, out)
    r = _run(nc, [arrays], core_ids=[0])
    return np.asarray(r.results[0]["out_0"]).reshape(1, T, D)


def aliases(a):
    for name in ("a_wqkv", "a_wo", "b_win", "b_wout", "mlp_w1", "mlp_w2"):
        a[name] = a[name + "_2"]
```
